# Optimizing a Trainium2 kernel written in Bass

```python
import math
import jax, jax.numpy as jnp
from jax import lax
import numpy as np

D_MODEL = 1024
BATCH = 1
SEQ = 256
DEPTH = 2

CONF_WIDTH = 512
CONF_KERNEL = 31
SSM_D_INNER = 1024
SSM_HEADDIM = 64
SSM_HEADS = SSM_D_INNER // SSM_HEADDIM
SSM_GROUPS = 2
SSM_STATE = 128
SSM_CONV = 4
SSM_CHUNK = 128
SSM_XBC = SSM_D_INNER + 2 * SSM_GROUPS * SSM_STATE
ATTN_HEADS = 8
ATTN_HEAD_DIM = 64
ATTN_WIDTH = ATTN_HEADS * ATTN_HEAD_DIM
MOBA_BLOCK = 256
MOBA_TOPK = 3
MOBA_Q_CHUNK = 64
FFN_DENSE = 2816
N_EXPERTS = 8
MOE_TOPK = 2
FFN_EXPERT = 3584
N_BRANCHES = 3
EPS = 1e-6
IN_SPLITS = (2 * CONF_WIDTH, SSM_D_INNER, SSM_XBC, SSM_HEADS, 3 * ATTN_WIDTH, N_BRANCHES * D_MODEL)
IN_WIDTH = 2 * CONF_WIDTH + SSM_D_INNER + SSM_XBC + SSM_HEADS + 3 * ATTN_WIDTH + N_BRANCHES * D_MODEL

kernel_name = 'hybrid_conformer_ssd_moba_moe_block'

def _split(a, sizes):
    idx = np.cumsum(np.array(sizes))[:-1].tolist()
    return jnp.split(a, idx, axis=-1)

def _rmsnorm(x, w):
    xf = x.astype(jnp.float32)
    y = xf * lax.rsqrt(jnp.mean(xf * xf, axis=-1, keepdims=True) + EPS)
    return (y * w.astype(jnp.float32)).astype(x.dtype)

def _layernorm(x, w, b):
    xf = x.astype(jnp.float32)
    mu = jnp.mean(xf, axis=-1, keepdims=True)
    xc = xf - mu
    y = xc * lax.rsqrt(jnp.mean(xc * xc, axis=-1, keepdims=True) + EPS)
    return (y * w.astype(jnp.float32) + b.astype(jnp.float32)).astype(x.dtype)

def _causal_dwconv(x, w, b):
    k = w.shape[0]
    y = lax.conv_general_dilated(
        x, w[:, None, :].astype(x.dtype), window_strides=(1,), padding=((k - 1, 0),),
        dimension_numbers=('NWC', 'WIO', 'NWC'), feature_group_count=x.shape[-1])
    return y + b

def _swiglu(h, wg, wu, wd):
    return (jax.nn.silu(h @ wg) * (h @ wu)) @ wd

def _ssd(x, dt, a, bm, cm, d_skip):
    bsz, s, h, p = x.shape
    g, n = bm.shape[2], bm.shape[3]
    r = h // g
    lc = SSM_CHUNK
    nc = s // lc
    xr = x.reshape(bsz, nc, lc, g, r, p)
    dtr = dt.reshape(bsz, nc, lc, g, r)
    br = bm.reshape(bsz, nc, lc, g, n)
    cr = cm.reshape(bsz, nc, lc, g, n)
    ad = (dtr * a.reshape(g, r)).astype(jnp.float32).transpose(0, 3, 4, 1, 2)
    a_cum = jnp.cumsum(ad, axis=-1)
    xdt = xr * dtr[..., None]
    causal = jnp.tril(jnp.ones((lc, lc), dtype=bool))
    seg = a_cum[..., :, None] - a_cum[..., None, :]
    lmat = jnp.where(causal, jnp.exp(jnp.where(causal, seg, 0.0)), 0.0)
    cb = jnp.einsum('bclgn,bcsgn->bgcls', cr, br)
    y_diag = jnp.einsum('bgrcls,bcsgrp->bclgrp', cb[:, :, None] * lmat, xdt)
    decay_states = jnp.exp(a_cum[..., -1:] - a_cum)
    states = jnp.einsum('bcsgn,bgrcs,bcsgrp->bcgrpn', br, decay_states, xdt)
    chunk_decay = jnp.exp(a_cum[..., -1])

    def step(hstate, inp):
        s_c, d_c = inp
        return hstate * d_c[..., None, None] + s_c, hstate

    h0 = jnp.zeros((bsz, g, r, p, n), dtype=states.dtype)
    _, prev = lax.scan(step, h0, (jnp.moveaxis(states, 1, 0), jnp.moveaxis(chunk_decay, -1, 0)))
    y_off = jnp.einsum('bclgn,cbgrpn,bgrcl->bclgrp', cr, prev, jnp.exp(a_cum))
    y = y_diag + y_off + xr * d_skip.reshape(g, r)[:, :, None]
    return y.reshape(bsz, s, h * p)

def _gated_group_rmsnorm(y, z, w):
    gz = (y * jax.nn.silu(z)).astype(jnp.float32)
    shp = gz.shape
    gg = gz.reshape(shp[:-1] + (SSM_GROUPS, shp[-1] // SSM_GROUPS))
    gg = gg * lax.rsqrt(jnp.mean(gg * gg, axis=-1, keepdims=True) + EPS)
    return (gg.reshape(shp) * w.astype(jnp.float32)).astype(y.dtype)

def _moba(q, k, v):
    bsz, s, h, dh = q.shape
    nb = -(-s // MOBA_BLOCK)
    pad = nb * MOBA_BLOCK - s
    k_eff = min(MOBA_TOPK, nb)
    scale = ATTN_HEAD_DIM ** -0.5
    qt = q.transpose(0, 2, 1, 3)
    kt = jnp.pad(k.transpose(0, 2, 1, 3), ((0, 0), (0, 0), (0, pad), (0, 0)))
    vt = jnp.pad(v.transpose(0, 2, 1, 3), ((0, 0), (0, 0), (0, pad), (0, 0)))
    kb = kt.reshape(bsz, h, nb, MOBA_BLOCK, dh)
    vb = vt.reshape(bsz, h, nb, MOBA_BLOCK, dh)
    kmean = jnp.mean(kb.astype(jnp.float32), axis=3)
    bi = jnp.arange(bsz)[:, None, None, None]
    hi = jnp.arange(h)[None, :, None, None]

    def chunk(i):
        q0 = i * MOBA_Q_CHUNK
        blk = q0 // MOBA_BLOCK
        qc = lax.dynamic_slice_in_dim(qt, q0, MOBA_Q_CHUNK, axis=2)
        qpos = q0 + jnp.arange(MOBA_Q_CHUNK)
        gate = jnp.einsum('bhqd,bhnd->bhqn', qc.astype(jnp.float32), kmean)
        gate = jnp.where(jnp.arange(nb) < blk, gate, -jnp.inf)
        _, top_i = lax.top_k(gate, k_eff)
        valid = jnp.arange(k_eff) < blk
        kg = kb[bi, hi, top_i]
        vg = vb[bi, hi, top_i]
        s_sel = jnp.einsum('bhqd,bhqjkd->bhqjk', qc, kg).astype(jnp.float32) * scale
        s_sel = jnp.where(valid[:, None], s_sel, -jnp.inf)
        s_sel = s_sel.reshape(bsz, h, MOBA_Q_CHUNK, k_eff * MOBA_BLOCK)
        k_own = lax.dynamic_slice_in_dim(kt, blk * MOBA_BLOCK, MOBA_BLOCK, axis=2)
        v_own = lax.dynamic_slice_in_dim(vt, blk * MOBA_BLOCK, MOBA_BLOCK, axis=2)
        kpos = blk * MOBA_BLOCK + jnp.arange(MOBA_BLOCK)
        s_own = jnp.einsum('bhqd,bhkd->bhqk', qc, k_own).astype(jnp.float32) * scale
        s_own = jnp.where(kpos[None, :] <= qpos[:, None], s_own, -jnp.inf)
        prob = jax.nn.softmax(jnp.concatenate([s_sel, s_own], axis=-1), axis=-1).astype(v.dtype)
        p_sel = prob[..., :k_eff * MOBA_BLOCK].reshape(bsz, h, MOBA_Q_CHUNK, k_eff, MOBA_BLOCK)
        p_own = prob[..., k_eff * MOBA_BLOCK:]
        return (jnp.einsum('bhqjk,bhqjkd->bhqd', p_sel, vg)
                + jnp.einsum('bhqk,bhkd->bhqd', p_own, v_own))

    out = lax.map(chunk, jnp.arange(s // MOBA_Q_CHUNK))
    return out.transpose(1, 0, 3, 2, 4).reshape(bsz, s, h * dh)

def _token_mixer(h, w_in, conf_conv_w, conf_conv_b, conf_ln_w, conf_ln_b, conf_out,
                 ssm_conv_w, ssm_conv_b, ssm_dt_bias, ssm_A_log, ssm_D, ssm_norm_w, ssm_out,
                 attn_out, mix_out):
    bsz, s, _ = h.shape
    proj = h @ w_in
    conf_in, z, xbc, dt_raw, qkv, gate_in = _split(proj, IN_SPLITS)
    val, glu_gate = jnp.split(conf_in, 2, axis=-1)
    u = _causal_dwconv(val * jax.nn.sigmoid(glu_gate), conf_conv_w, conf_conv_b)
    u = jax.nn.silu(_layernorm(u, conf_ln_w, conf_ln_b))
    out_a = u @ conf_out
    xbc = jax.nn.silu(_causal_dwconv(xbc, ssm_conv_w, ssm_conv_b))
    xs, bm, cm = _split(xbc, (SSM_D_INNER, SSM_GROUPS * SSM_STATE, SSM_GROUPS * SSM_STATE))
    dt = jax.nn.softplus((dt_raw + ssm_dt_bias).astype(jnp.float32))
    a = -jnp.exp(ssm_A_log.astype(jnp.float32))
    y = _ssd(xs.reshape(bsz, s, SSM_HEADS, SSM_HEADDIM), dt, a,
             bm.reshape(bsz, s, SSM_GROUPS, SSM_STATE), cm.reshape(bsz, s, SSM_GROUPS, SSM_STATE), ssm_D)
    out_b = _gated_group_rmsnorm(y.astype(h.dtype), z, ssm_norm_w) @ ssm_out
    q, k, v = [t.reshape(bsz, s, ATTN_HEADS, ATTN_HEAD_DIM) for t in jnp.split(qkv, 3, axis=-1)]
    out_c = _moba(q, k, v).astype(h.dtype) @ attn_out
    g_a, g_b, g_c = jnp.split(jax.nn.sigmoid(gate_in), 3, axis=-1)
    return (g_a * out_a + g_b * out_b + g_c * out_c) @ mix_out

def _moe(h, router_w, router_b, wg, wu, wd):
    logits = (h @ router_w + router_b).astype(jnp.float32)
    top_v, top_i = lax.top_k(logits, MOE_TOPK)
    top_w = jax.nn.softmax(top_v, axis=-1)
    gates = jnp.sum(top_w[..., None] * jax.nn.one_hot(top_i, N_EXPERTS, dtype=jnp.float32), axis=-2)
    gates = gates.astype(h.dtype)
    out = jnp.zeros_like(h)
    for e in range(N_EXPERTS):
        out = out + gates[..., e:e + 1] * _swiglu(h, wg[e], wu[e], wd[e])
    return out

def setup_inputs(seed: int = 0) -> dict:
    key = jax.random.key(seed)
    ks = jax.random.split(key, 40)
    f32 = jnp.float32
    L = DEPTH
    n_dense = (DEPTH + 1) // 2
    n_moe = DEPTH // 2

    def nrm(k, shape, scale):
        return jax.random.normal(k, shape, f32) * scale

    dt0 = jnp.exp(jax.random.uniform(ks[14], (L, SSM_HEADS), f32, math.log(1e-3), math.log(1e-1)))
    return {
        'x': nrm(ks[0], (BATCH, SEQ, D_MODEL), 1.0),
        'c': nrm(ks[1], (BATCH, D_MODEL), 1.0),
        'norm1_w': 1.0 + nrm(ks[2], (L, D_MODEL), 0.02),
        'norm2_w': 1.0 + nrm(ks[3], (L, D_MODEL), 0.02),
        'ada_w': nrm(ks[4], (L, D_MODEL, 6 * D_MODEL), D_MODEL ** -0.5),
        'ada_b': nrm(ks[5], (L, 6 * D_MODEL), 0.01),
        'w_in': nrm(ks[6], (L, D_MODEL, IN_WIDTH), D_MODEL ** -0.5),
        'conf_conv_w': nrm(ks[7], (L, CONF_KERNEL, CONF_WIDTH), CONF_KERNEL ** -0.5),
        'conf_conv_b': nrm(ks[8], (L, CONF_WIDTH), 0.01),
        'conf_ln_w': 1.0 + nrm(ks[9], (L, CONF_WIDTH), 0.02),
        'conf_ln_b': nrm(ks[10], (L, CONF_WIDTH), 0.01),
        'conf_out': nrm(ks[11], (L, CONF_WIDTH, D_MODEL), CONF_WIDTH ** -0.5),
        'ssm_conv_w': nrm(ks[12], (L, SSM_CONV, SSM_XBC), SSM_CONV ** -0.5),
        'ssm_conv_b': nrm(ks[13], (L, SSM_XBC), 0.01),
        'ssm_dt_bias': dt0 + jnp.log(-jnp.expm1(-dt0)),
        'ssm_A_log': jnp.log(jax.random.uniform(ks[15], (L, SSM_HEADS), f32, 1.0, 16.0)),
        'ssm_D': 1.0 + nrm(ks[16], (L, SSM_HEADS), 0.02),
        'ssm_norm_w': 1.0 + nrm(ks[17], (L, SSM_D_INNER), 0.02),
        'ssm_out': nrm(ks[18], (L, SSM_D_INNER, D_MODEL), SSM_D_INNER ** -0.5),
        'attn_out': nrm(ks[19], (L, ATTN_WIDTH, D_MODEL), ATTN_WIDTH ** -0.5),
        'mix_out': nrm(ks[20], (L, D_MODEL, D_MODEL), D_MODEL ** -0.5),
        'ffn_w_gate': nrm(ks[21], (n_dense, D_MODEL, FFN_DENSE), D_MODEL ** -0.5),
        'ffn_w_up': nrm(ks[22], (n_dense, D_MODEL, FFN_DENSE), D_MODEL ** -0.5),
        'ffn_w_down': nrm(ks[23], (n_dense, FFN_DENSE, D_MODEL), FFN_DENSE ** -0.5),
        'moe_router_w': nrm(ks[24], (n_moe, D_MODEL, N_EXPERTS), D_MODEL ** -0.5),
        'moe_router_b': nrm(ks[25], (n_moe, N_EXPERTS), 0.01),
        'moe_w_gate': nrm(ks[26], (n_moe, N_EXPERTS, D_MODEL, FFN_EXPERT), D_MODEL ** -0.5),
        'moe_w_up': nrm(ks[27], (n_moe, N_EXPERTS, D_MODEL, FFN_EXPERT), D_MODEL ** -0.5),
        'moe_w_down': nrm(ks[28], (n_moe, N_EXPERTS, FFN_EXPERT, D_MODEL), FFN_EXPERT ** -0.5),
        'final_norm_w': 1.0 + nrm(ks[29], (D_MODEL,), 0.02),
    }

def reference(x, c, norm1_w, norm2_w, ada_w, ada_b, w_in, conf_conv_w, conf_conv_b, conf_ln_w,
              conf_ln_b, conf_out, ssm_conv_w, ssm_conv_b, ssm_dt_bias, ssm_A_log, ssm_D, ssm_norm_w,
              ssm_out, attn_out, mix_out, ffn_w_gate, ffn_w_up, ffn_w_down, moe_router_w, moe_router_b,
              moe_w_gate, moe_w_up, moe_w_down, final_norm_w):
    c_act = jax.nn.silu(c)
    for l in range(DEPTH):
        mod = c_act @ ada_w[l] + ada_b[l]
        sh1, sc1, g1, sh2, sc2, g2 = [m[:, None, :] for m in jnp.split(mod, 6, axis=-1)]
        h = _rmsnorm(x, norm1_w[l]) * (1.0 + sc1) + sh1
        mix = _token_mixer(h, w_in[l], conf_conv_w[l], conf_conv_b[l], conf_ln_w[l], conf_ln_b[l],
                           conf_out[l], ssm_conv_w[l], ssm_conv_b[l], ssm_dt_bias[l], ssm_A_log[l],
                           ssm_D[l], ssm_norm_w[l], ssm_out[l], attn_out[l], mix_out[l])
        x = x + g1 * mix
        h = _rmsnorm(x, norm2_w[l]) * (1.0 + sc2) + sh2
        if l % 2 == 0:
            j = l // 2
            f = _swiglu(h, ffn_w_gate[j], ffn_w_up[j], ffn_w_down[j])
        else:
            j = l // 2
            f = _moe(h, moe_router_w[j], moe_router_b[j], moe_w_gate[j], moe_w_up[j], moe_w_down[j])
        x = x + g2 * f
    return _rmsnorm(x, final_norm_w)


_drawn_inputs = setup_inputs


def setup_inputs(seed=0):
    import zlib

    import numpy as np

    out = dict(_drawn_inputs(seed))
    spreads = {}
    factors = {'conf_conv_b': 8.0,
     'conf_ln_b': 8.0,
     'ssm_conv_b': 13.065,
     'ssm_D': 16.803,
     'final_norm_w': 8.587,
     'conf_ln_w': 2.794,
     'ssm_norm_w': 2.67}
    for name, (base, spread) in spreads.items():
        noise = np.random.default_rng([zlib.crc32(name.encode()), seed]).standard_normal(out[name].shape)
        drawn = base * np.exp(spread * noise) if base else spread * noise
        out[name] = __import__('jax').numpy.asarray(drawn.astype(out[name].dtype))
    for name, factor in factors.items():
        out[name] = (out[name] * factor).astype(out[name].dtype)
    return out
```

```python
import concourse.bass as bass
from concourse import mybir
from contextlib import ExitStack

P = 128
D_MODEL, SEQ, DEPTH = 1024, 256, 2
KT = D_MODEL // P
TT = SEQ // P
CONF_WIDTH, CONF_TAPS = 512, 31
CT = CONF_WIDTH // P
HEADS_S, GROUPS = 16, 2
DI = 1024
XT = 12
SSM_TAPS = 4
HEADS_A, DH = 8, 64
IN_WIDTH = 8208
DT_COL = 3584
FFN_DENSE, FFN_EXPERT, EXPERTS = 2816, 3584, 8
EPS = 1e-6
NEG = -1e30
PADC = CONF_TAPS - 1
VAL, GLU, Z, XBC, Q, K, V, GATE = 0, 4, 8, 16, 28, 32, 36, 40
W_CHUNKS = 32
LOOPED = 16
ADA_CHUNKS = 24
ADA_FIRST = 8
SLOTS = 8
GD, GE = FFN_DENSE // 256, FFN_EXPERT // 256
R_N1, R_N2, R_ADA, R_CB, R_LW, R_LB, R_SB, R_SN, R_FN, R_C = 0, 8, 16, 64, 68, 72, 76, 88, 96, 104
ROWS = 112


def ring_plan():
    order = []
    for l in range(DEPTH):
        if l == 0:
            order += [("ada", l, a) for a in range(ADA_FIRST)]
        order += [("w", l, n) for n in range(W_CHUNKS)]
        order += [("ada", l, a) for a in range(ADA_FIRST, ADA_CHUNKS)]
        order += [("conf", l, a) for a in range(2)] + [("attn", l, a) for a in range(2)]
        order += [("ssm", l, a) for a in range(4)] + [("mix", l, a) for a in range(4)]
        if l == 0:
            order += [("ada", 1, a) for a in range(ADA_FIRST)]
            for g in range(GD):
                order += [("g", 0, g), ("u", 0, g), ("d", 0, g)]
    plan, last, fills, nxt = {}, {}, [0] * SLOTS, 0
    for key in order:
        if key[0] in "gud":
            slot = {"g": 0, "u": 2, "d": 4}[key[0]] + key[2] % 2
        else:
            slot, nxt = nxt % SLOTS, nxt + 1
        fills[slot] += 1
        plan[key] = (slot, fills[slot], last.get(slot))
        last[slot] = key
    return order, plan, last, fills


def trunk(nc, x, c, norm1_w, norm2_w, ada_w, ada_b, w_in, conf_conv_w, conf_conv_b, conf_ln_w, conf_ln_b, conf_out,
          ssm_conv_w, ssm_conv_b, ssm_dt_bias, ssm_A_log, ssm_D, ssm_norm_w, ssm_out, attn_out, mix_out,
          ffn_w_gate, ffn_w_up, ffn_w_down, moe_router_w, moe_router_b, moe_w_gate, moe_w_up, moe_w_down,
          final_norm_w, out):
    fp32, i32 = mybir.dt.float32, mybir.dt.int32
    ALU, ACT, AX = mybir.AluOpType, mybir.ActivationFunctionType, mybir.AxisListType
    ds = bass.ds
    ORDER, PLAN, LAST, FILLS = ring_plan()
    moe_w_gate, moe_w_up, moe_w_down = moe_w_gate[0], moe_w_up[0], moe_w_down[0]

    ctx = ExitStack()
    with ctx:
        def sb(name, shape, dt=fp32):
            return ctx.enter_context(nc.sbuf_tensor(name, shape, dt))

        def sem(name):
            return ctx.enter_context(nc.semaphore(name))

        ring = sb("ring", [P, SLOTS, 2048])
        proj = sb("proj", [P, 64, SEQ])
        xT = sb("xT", [P, KT, SEQ])
        hT = sb("hT", [P, KT, SEQ])
        sq = sb("sq", [P, KT, SEQ])
        xc = sb("xc", [P, XT, SEQ])
        cpad = sb("cpad", [P, CT, PADC + SEQ])
        cacc = sb("cacc", [P, CT, SEQ])
        v_tm = sb("v_tm", [P, TT, 512])
        b_tm = sb("b_tm", [P, GROUPS, P])
        seg = sb("seg", [P, 2, 4, P])
        cdec = sb("cdec", [P, 4, P])
        cbm = sb("cbm", [P, GROUPS, TT, P])
        sc = sb("sc", [P, 2, 384])
        pT = sb("pT", [P, 2, 384])
        ident = sb("ident", [P, P])
        ones = sb("ones", [P, P])
        triu = sb("triu", [P, P])
        striu = sb("striu", [P, P])
        amask = sb("amask", [P, 384])
        slot_f = sb("slot_f", [P, SEQ])
        pcol = sb("pcol", [P, DEPTH, ROWS])
        cwcol = sb("cwcol", [P, DEPTH, CONF_TAPS * CT])
        swcol = sb("swcol", [P, DEPTH, SSM_TAPS * XT])
        ccol = sb("ccol", [P, KT])
        dcol = sb("dcol", [P, DEPTH, KT])
        dtb = sb("dtb", [P, DEPTH, HEADS_S])
        alog = sb("alog", [P, DEPTH, HEADS_S])
        wdt = sb("wdt", [P, DEPTH, KT, HEADS_S])
        rw = sb("rw", [P, KT, EXPERTS])
        rb = sb("rb", [P, EXPERTS])
        modc = sb("modc", [P, 48])
        acolw = sb("acolw", [P, 2, KT])
        rs = sb("rs", [P, 3, SEQ])
        dts = sb("dts", [P, 5, TT, HEADS_S])
        acum = sb("acum", [P, TT, HEADS_S])
        dec = sb("dec", [P, 2, HEADS_S])
        smx = sb("smx", [P, 2, 4, 2])
        key9 = sb("key9", [P, TT, EXPERTS + 1])
        gate9 = sb("gate9", [P, TT, EXPERTS + 1])
        cntf = sb("cntf", [1, EXPERTS + 1])
        cnt = sb("cnt", [1, EXPERTS + 1], i32)
        ps = ctx.enter_context(nc.psum_tensor("ps", [P, 8, 512], fp32))

        x_in = proj[:, 0:8, :].rearrange("p (t a) n -> p t (a n)", t=TT)
        xs_tm = proj[:, XBC:XBC + 8, :].rearrange("p (t a) n -> p t (a n)", t=TT)
        prev = proj[:, XBC + 8:XBC + 12, :].rearrange("p (g a) n -> p g (a n)", g=GROUPS)
        xdt = proj[:, 0:8, :].rearrange("p (t a) n -> p t (a n)", t=TT)
        xdtd = sq[:, 0:4, :].rearrange("p a n -> p (a n)")
        ao = proj[:, V:V + 4, :]
        ysq = proj[:, Q:Q + 8, :]
        merged = hT
        hm = proj[:, 0:4, :].rearrange("p (b j) n -> p b j n", b=2)
        sil = proj[:, 4:6, :]
        pg_m = proj[:, 6:8, :]
        ysb = proj[:, 8:16, :].rearrange("p (t a) n -> p t (a n)", t=TT)
        xg = proj[:, 16:24, :]
        h_tm = proj[:, 24:32, :].rearrange("p (t a) n -> p t (a n)", t=TT)
        moe = proj[:, 32:40, :]
        p_m = proj[:, 40:42, :]
        pgT = proj[:, 42:44, :]
        o_tm = proj[:, 48:56, :].rearrange("p (t a) n -> p t (a n)", t=TT)
        csq = cpad[:, :, 0:SEQ]
        slot_i = sc[:, 0, 0:SEQ].bitcast(i32)
        prow, cwrow, swrow = (v_tm[:, 0:2, 128 * i:128 * i + 128] for i in range(3))
        dall = v_tm[:, 0:2, 384:384 + HEADS_S]
        rt = cdec[:, :, :].rearrange("p a b -> p (a b)")[:, 0:20 * TT * EXPERTS].rearrange(
            "p (i t e) -> p i t e", t=TT, e=EXPERTS)
        gr = xc[:, 0:6, :].rearrange("p (a b) n -> p a b n", a=3)

        full = [sem(f"ring_full{s}") for s in range(SLOTS)]
        x_in_s = sem("x_loaded")
        par_s = sem("params_loaded")
        cst_s = sem("consts_made")
        pcst = sem("pool_step")
        prow_s = sem("param_rows_transposed")
        pcol_s = sem("param_cols_ready")
        ccol_s = sem("c_act_ready")
        xtr_s = sem("x_transposed")
        x_s = sem("x_ready")
        sq_s = sem("norm_squares")
        st_s = sem("norm_sums")
        var_s = sem("norm_var")
        sd_s = sem("norm_sd")
        h_s = sem("h_ready")
        ada_s = sem("ada_mm")
        mod_s = sem("mod_ready")
        dtmm_s = sem("dt_mm")
        dtin_s = sem("dt_biased")
        dtexp_s = sem("dt_exp")
        dt_s = sem("dt_ready")
        dtln_s = sem("dt_ln")
        proj_s = sem("proj_mm")
        ev_s = sem("proj_evacuated")
        sig_s = sem("glu_sigmoid")
        glu_s = sem("glu_ready")
        cv_s = sem("conf_conv_step")
        cm_s = sem("conf_mean_mm")
        cx_s = sem("conf_centered")
        csq_s = sem("conf_squares")
        cvar_s = sem("conf_var_mm")
        cvr_s = sem("conf_var")
        csd_s = sem("conf_sd")
        cn_s = sem("conf_normed")
        cu_s = sem("conf_u_ready")
        xv_s = sem("xbc_conv")
        xsil_s = sem("xbc_silu")
        zs_s = sem("z_silu")
        vt_s = sem("v_transposed")
        vtm_s = sem("v_tm_ready")
        sc_s = sem("scores_mm")
        msk_s = sem("scores_masked")
        mx_s = sem("scores_max")
        ex_s = sem("scores_exp")
        pr_s = sem("probs_ready")
        ptr_s = sem("probs_transposed")
        pte_s = sem("probs_T_ready")
        pv_s = sem("pv_mm")
        ao_s = sem("attn_ready")
        xst_s = sem("xs_transposed")
        xse_s = sem("xs_tm_ready")
        ac_s = sem("acum_mm")
        acs_s = sem("acum_ready")
        dcy_s = sem("decay_ready")
        cb_s = sem("cb_mm")
        cbm_s = sem("cb_masked")
        xd_s = sem("xdt_ready")
        stt_s = sem("state_mm")
        prev_s = sem("state_ready")
        bc_s = sem("acum_bcast_mm")
        seg_s = sem("seg_ready")
        ls_s = sem("lmat_exp")
        lm_s = sem("lmat_ready")
        y_s = sem("y_mm")
        yz_s = sem("y_gated")
        gsq_s = sem("group_squares")
        gst_s = sem("group_sums")
        gv_s = sem("group_var")
        gsd_s = sem("group_sd")
        gn_s = sem("group_normed")
        gate_s = sem("gates_sigmoid")
        om_s = sem("out_mm")
        mg_s = sem("merge_step")
        htr_s = sem("h_transposed")
        htm_s = sem("h_tm_ready")
        lg_s = sem("logits_mm")
        mk_s = sem("masks_ready")
        re_s = sem("router_exp_in")
        rx_s = sem("router_exp")
        cum_s = sem("slots_mm")
        rk_s = sem("slots_ready")
        p_s = sem("gather_matrix")
        pg_s = sem("scatter_matrix")
        c_s = sem("aux_bank_mm")
        cf_s = sem("aux_bank_free")
        gu_s = sem("gate_up_mm")
        sil_s = sem("silu_ready")
        hm_s = sem("h_mid_ready")
        dn_s = sem("down_mm")
        ye_s = sem("y_evacuated")
        fin_s = sem("final_transposed")
        o_s = sem("out_ready")
        od_s = sem("out_stored")
        vst = sem("vector_step")
        ast = sem("scalar_step")
        CV0 = 1
        HM0 = 2
        DN0 = 2
        CF0 = 2

        def released(key):
            kind, l, a = key
            if kind == "ada":
                return ada_s, ADA_CHUNKS * l + a + 1
            if kind == "w":
                return proj_s, W_CHUNKS * l + a + 1
            if kind == "conf":
                return om_s, 16 * l + 2 * a + 2
            if kind == "attn":
                return om_s, 16 * l + 4 + 2 * a + 2
            if kind == "ssm":
                return om_s, 16 * l + 8 + a + 1
            if kind == "mix":
                return om_s, 16 * l + 12 + a + 1
            if kind in "gu":
                return gu_s, 2 * a + 2
            return dn_s, DN0 + a + 1

        def slot_of(key):
            s, n, _ = PLAN[key]
            return s, 16 * n

        def wide(s):
            return ring[:, s, :].rearrange("p (k n) -> p k n", k=8)

        def half(s):
            return ring[:, s, :].rearrange("p (k n) -> p k n", k=4)

        def rows2(s):
            return ring[:, s, :].rearrange("p (j n) -> p j n", j=2)

        block = ctx.enter_context(nc.Block())

        @block.sync
        def _(sp):
            sp.dma_start(x_in[:, 0, :], x[0, 0:P, :]).then_inc(x_in_s, 16)
            sp.dma_start(x_in[:, 1, :], x[0, P:2 * P, :]).then_inc(x_in_s, 16)

            def columns(w, col, width):
                return w[:, col:col + width].rearrange("(k p) n -> p k n", p=P)

            for key in ORDER:
                kind, l, a = key
                s, _, before = PLAN[key]
                if before is not None:
                    sp.wait_ge(*released(before))
                if kind == "ada":
                    src, dst = columns(ada_w[l], 256 * a, 256), wide(s)
                elif kind == "w":
                    src, dst = columns(w_in[l], 256 * a + (HEADS_S if 256 * a >= DT_COL else 0), 256), wide(s)
                elif kind == "conf":
                    src, dst = columns(conf_out[l], 512 * a, 512), half(s)
                elif kind == "attn":
                    src, dst = columns(attn_out[l], 512 * a, 512), half(s)
                elif kind == "ssm":
                    src, dst = columns(ssm_out[l], 256 * a, 256), wide(s)
                elif kind == "mix":
                    src, dst = columns(mix_out[l], 256 * a, 256), wide(s)
                elif kind == "g":
                    src, dst = columns(ffn_w_gate[0], 256 * a, 256), wide(s)
                elif kind == "u":
                    src, dst = columns(ffn_w_up[0], 256 * a, 256), wide(s)
                else:
                    src, dst = ffn_w_down[0][256 * a:256 * a + 256, :].rearrange("(j p) n -> p j n", p=P), rows2(s)
                sp.dma_start(dst, src).then_inc(full[s], 16)

            for s in range(6):
                sp.wait_ge(*released(LAST[s]))

            def expert_loads(q, b):
                e = (q // GE) if isinstance(q, int) else q // GE
                col = (q % GE) * 256
                sp.dma_start(wide(b), moe_w_gate[ds(e, 1)].rearrange("e (k p) n -> p (e k) n", p=P)[:, :, ds(col, 256)]
                             ).then_inc(full[b], 16)
                sp.dma_start(wide(2 + b), moe_w_up[ds(e, 1)].rearrange("e (k p) n -> p (e k) n", p=P)[:, :, ds(col, 256)]
                             ).then_inc(full[2 + b], 16)

            def expert_down(q, b):
                sp.dma_start(rows2(4 + b), moe_w_down.rearrange("e r n -> (e r) n")[ds(q * 256, 256), :]
                             .rearrange("(j p) n -> p j n", p=P)).then_inc(full[4 + b], 16)

            for b in range(2):
                expert_loads(b, b)
                expert_down(b, b)
            with sp.Fori(1, EXPERTS * GE // 2) as i:
                for b in range(2):
                    sp.wait_ge(gu_s, i * 4 + 2 * GD + 2 * (b - 2) + 2)
                    expert_loads(i * 2 + b, b)
                    sp.wait_ge(dn_s, i * 2 + DN0 + GD + b - 2 + 1)
                    expert_down(i * 2 + b, b)

            for t in range(TT):
                sp.wait_ge(o_s, 2 * t + 2)
                sp.dma_start(out[0, t * P:(t + 1) * P, :], o_tm[:, t, :]).then_inc(od_s, 16)
            sp.wait_ge(od_s, 16 * TT)

        @block.gpsimd
        def _(pool):
            g = nc.gpsimd
            g.memset(ones[:, :], 1.0).then_inc(pcst, 1)
            g.memset(ident[:, :], 0.0).then_inc(pcst, 1)
            g.memset(amask[:, :], 0.0).then_inc(pcst, 1)
            g.iota(slot_i[:, :], pattern=[[1, SEQ]], base=0, channel_multiplier=0).then_inc(pcst, 1)
            pool.wait_ge(pcst, 4)
            g.affine_select(out=ident[:, :], in_=ident[:, :], compare_op=ALU.not_equal, fill=1.0, base=0,
                            pattern=[[-1, P]], channel_multiplier=1).then_inc(cst_s, 1)
            g.affine_select(out=triu[:, :], in_=ones[:, :], compare_op=ALU.is_ge, fill=0.0, base=0,
                            pattern=[[1, P]], channel_multiplier=-1).then_inc(cst_s, 1)
            g.affine_select(out=striu[:, :], in_=ones[:, :], compare_op=ALU.is_gt, fill=0.0, base=0,
                            pattern=[[1, P]], channel_multiplier=-1).then_inc(cst_s, 1)
            for c0 in (0, 256):
                g.affine_select(out=amask[:, c0:c0 + P], in_=amask[:, c0:c0 + P], compare_op=ALU.is_ge, fill=NEG,
                                base=0, pattern=[[-1, P]], channel_multiplier=1).then_inc(cst_s, 1)
            g.tensor_copy(slot_f[:, :], slot_i[:, :]).then_inc(cst_s, 1)
            g.memset(cpad[:, :, :], 0.0).then_inc(cst_s, 1)
        CONSTS = 7

        def param_loads():
            def rows(v):
                return v.rearrange("(m p) -> m p", p=P)
            for l in range(DEPTH):
                for src, r in ((norm1_w[l], R_N1), (norm2_w[l], R_N2), (ada_b[l], R_ADA), (conf_conv_b[l], R_CB),
                               (conf_ln_w[l], R_LW), (conf_ln_b[l], R_LB), (ssm_conv_b[l], R_SB),
                               (ssm_norm_w[l], R_SN), (final_norm_w, R_FN), (c[0], R_C)):
                    v = rows(src)
                    yield prow[r:r + v.shape[0], l, :], v
                yield cwrow[0:CONF_TAPS * CT, l, :], conf_conv_w[l].rearrange("k (m p) -> (k m) p", p=P)
                yield swrow[0:SSM_TAPS * XT, l, :], ssm_conv_w[l].rearrange("k (m p) -> (k m) p", p=P)
            for l in range(DEPTH):
                yield wdt[:, l, :, :], w_in[l][:, DT_COL:DT_COL + HEADS_S].rearrange("(k p) n -> p k n", p=P)
                yield dtb[:, l, :], ssm_dt_bias[l:l + 1, :].broadcast_to([P, HEADS_S])
                yield alog[:, l, :], ssm_A_log[l:l + 1, :].broadcast_to([P, HEADS_S])
                yield dall[:, l, :], ssm_D[l:l + 1, :].broadcast_to([P, HEADS_S])
            yield rw[:, :, :], moe_router_w[0].rearrange("(k p) n -> p k n", p=P)
            yield rb[:, :], moe_router_b[0:1, :].broadcast_to([P, EXPERTS])
        N_PARAMS = 12 * DEPTH + 4 * DEPTH + 2

        @block.tensor
        def _(pe):
            mm = nc.tensor.matmul
            pe.wait_ge(cst_s, CONSTS)
            pe.wait_ge(x_in_s, 32)
            for m in range(KT):
                for t in range(TT):
                    last = nc.tensor.transpose(ps[:, m // 2, (m % 2) * SEQ + t * P:(m % 2) * SEQ + (t + 1) * P],
                                               x_in[:, t, m * P:(m + 1) * P], ident[:, :])
            last.then_inc(xtr_s, 1)
            pe.wait_ge(par_s, 16 * N_PARAMS)
            for l in range(DEPTH):
                nc.tensor.transpose(ps[:, 4 + l, 0:ROWS], prow[0:ROWS, l, :], ident[0:ROWS, 0:ROWS])
                nc.tensor.transpose(ps[:, 4 + l, 128:128 + CONF_TAPS * CT], cwrow[0:CONF_TAPS * CT, l, :],
                                    ident[0:CONF_TAPS * CT, 0:CONF_TAPS * CT])
                last = nc.tensor.transpose(ps[:, 4 + l, 256:256 + SSM_TAPS * XT], swrow[0:SSM_TAPS * XT, l, :],
                                           ident[0:SSM_TAPS * XT, 0:SSM_TAPS * XT])
            last.then_inc(prow_s, 1)
            pe.wait_ge(ccol_s, 1)

            def norm_sums(ni):
                pe.wait_ge(sq_s, ni + 1)
                if ni < 2:
                    pe.wait_ge(mod_s, 2 * ni + 1)
                for k in range(KT):
                    last = mm(ps[:, 2, 0:SEQ], ones[:, :], sq[:, k, :], start=(k == 0), stop=(k == KT - 1))
                last.then_inc(st_s, 1)

            def ada(l, a):
                s, n = slot_of(("ada", l, a))
                pe.wait_ge(full[s], n)
                if a == 0 and l:
                    pe.wait_ge(mod_s, 2 * l)
                for j in range(2):
                    for k in range(KT):
                        last = mm(ps[:, 2, 288 + 2 * a + j:289 + 2 * a + j], wide(s)[:, k, j * P:(j + 1) * P],
                                  ccol[:, k:k + 1], start=(k == 0), stop=(k == KT - 1))
                last.then_inc(ada_s, 1)

            def w_chunk(l, n, s, fill):
                pe.wait_ge(full[s], fill)
                for j in range(2):
                    for k in range(KT):
                        last = mm(ps[:, n % 2, j * SEQ:(j + 1) * SEQ], wide(s)[:, k, j * P:(j + 1) * P], hT[:, k, :],
                                  start=(k == 0), stop=(k == KT - 1))
                last.then_inc(proj_s, 1)

            def scores(l, h):
                if h >= 2:
                    pe.wait_ge(msk_s, HEADS_A * l + h - 1)
                p0 = DH * (h % 2)
                q, k = proj[p0:p0 + DH, Q + h // 2, :], proj[p0:p0 + DH, K + h // 2, :]
                mm(ps[:, 3 + h % 2, 0:P], q[:, 0:P], k[:, 0:P], start=True, stop=True)
                mm(ps[:, 3 + h % 2, P:P + SEQ], q[:, P:SEQ], k[:, :], start=True, stop=True).then_inc(sc_s, 1)

            def probs_transpose(l, h):
                pe.wait_ge(pr_s, HEADS_A * l + h + 1)
                for i in range(3):
                    last = nc.tensor.transpose(ps[:, 5 + h % 2, i * P:(i + 1) * P], sc[:, h % 2, (0, 1, 2)[i] * P:
                                               ((0, 1, 2)[i] + 1) * P], ident[:, :])
                last.then_inc(ptr_s, 1)

            def pv(l, h):
                pe.wait_ge(pte_s, HEADS_A * l + h + 1)
                if h >= 2 and h % 2 == 0:
                    pe.wait_ge(ao_s, 4 * l + h // 2)
                c0, p0 = (h // 2) % 2 * SEQ, DH * (h % 2)
                mm(ps[p0:p0 + DH, 7, c0:c0 + SEQ], v_tm[:, 0, h * DH:(h + 1) * DH], pT[:, h % 2, 0:SEQ],
                   start=True, stop=False)
                mm(ps[p0:p0 + DH, 7, c0 + P:c0 + SEQ], v_tm[:, 1, h * DH:(h + 1) * DH], pT[:, h % 2, SEQ:384],
                   start=False, stop=True).then_inc(pv_s, 1)

            def acum_bcast(l, k):
                hb, cc = k // 2, k % 2
                if k >= 2:
                    pe.wait_ge(lm_s, 8 * l + k - 1)
                for r in range(4):
                    h = 4 * hb + r
                    last = mm(ps[:, 3 + k % 2, r * P:(r + 1) * P], dts[:, 4, cc, h:h + 1].broadcast_to([P, P]),
                              triu[:, :], start=True, stop=True)
                last.then_inc(bc_s, 1)

            def y_batch(l, k):
                hb, cc = k // 2, k % 2
                pe.wait_ge(lm_s, 8 * l + k + 1)
                if hb >= 2 and cc == 0:
                    pe.wait_ge(yz_s, 4 * l + hb - 1)
                for r in range(4):
                    h = 4 * hb + r
                    p0, c0 = DH * (h % 2), (r // 2) * SEQ + cc * P
                    dst = ps[p0:p0 + DH, 5 + hb % 2, c0:c0 + P]
                    last = mm(dst, xdt[:, cc, h * DH:(h + 1) * DH], seg[:, k % 2, r, :], start=True, stop=(cc == 0))
                    if cc == 1:
                        last = mm(dst, prev[:, hb // 2, (h % 8) * DH:(h % 8 + 1) * DH], cdec[:, r, :],
                                  start=False, stop=True)
                last.then_inc(y_s, 1)

            def out_pair(l, idx, s, view, kk, cols, rhs):
                pair = 16 * l + idx
                if pair >= 2:
                    pe.wait_ge(mg_s, pair - 1)
                for j in range(2):
                    for k in range(kk):
                        last = mm(ps[:, idx % 2, j * SEQ:(j + 1) * SEQ], view(s)[:, k, (cols + j) * P:(cols + j + 1) * P],
                                  rhs[:, k, :], start=(k == 0), stop=(k == kk - 1))
                last.then_inc(om_s, 1)

            def gate_up(g_slot, u_slot, j, x_src, n):
                for w, c0 in ((g_slot, 0), (u_slot, SEQ)):
                    for k in range(KT):
                        last = mm(ps[:, j, c0:c0 + n], wide(w)[:, k, j * P:(j + 1) * P], x_src[:, k, 0:n],
                                  start=(k == 0), stop=(k == KT - 1))
                last.then_inc(gu_s, 1)

            def down(slot, b, n, first, stop):
                for j in range(2):
                    for t in range(n // P):
                        for hf in range(2):
                            last = mm(ps[:, 2 + 2 * t + hf, :], hm[:, b, j, t * P:(t + 1) * P],
                                      rows2(slot)[:, j, hf * 512:(hf + 1) * 512],
                                      start=(first and j == 0), stop=(stop and j == 1))
                last.then_inc(dn_s, 1)

            for l in range(DEPTH):
                if l == 0:
                    for a in range(ADA_FIRST):
                        ada(l, a)
                norm_sums(2 * l)
                pe.wait_ge(h_s, 2 * l + 1)
                for t in range(TT):
                    for k in range(KT):
                        last = mm(ps[:, 2, 256 + t * HEADS_S:256 + (t + 1) * HEADS_S], hT[:, k, t * P:(t + 1) * P],
                                  wdt[:, l, k, :], start=(k == 0), stop=(k == KT - 1))
                last.then_inc(dtmm_s, 1)
                s0, f0, _ = PLAN[("w", l, 0)]
                with pe.Fori(0, LOOPED // SLOTS) as i:
                    for b in range(SLOTS):
                        s, f, _ = PLAN[("w", l, b)]
                        pe.wait_ge(ev_s, i * SLOTS + W_CHUNKS * l + b + 1)
                        w_chunk(l, b, s, i * 16 + 16 * f)
                pe.wait_ge(cv_s, CV0 + (l + 1) * CT * CONF_TAPS)
                for k in range(CT):
                    last = mm(ps[:, 2, 0:SEQ], ones[:, :], cacc[:, k, :], start=(k == 0), stop=(k == CT - 1))
                last.then_inc(cm_s, 1)
                for n in range(LOOPED, 20):
                    pe.wait_ge(ev_s, W_CHUNKS * l + n + 1)
                    w_chunk(l, n, *slot_of(("w", l, n)))
                pe.wait_ge(csq_s, l + 1)
                for k in range(CT):
                    last = mm(ps[:, 2, 0:SEQ], ones[:, :], csq[:, k, :], start=(k == 0), stop=(k == CT - 1))
                last.then_inc(cvar_s, 1)
                pe.wait_ge(ev_s, 2 + W_CHUNKS * l + 20)
                for t in range(TT):
                    for m in range(4):
                        last = nc.tensor.transpose(ps[:, 5 + t, m * P:(m + 1) * P], proj[:, V + m, t * P:(t + 1) * P],
                                                   ident[:, :])
                    last.then_inc(vt_s, 1)
                for i in range(12):
                    n = 20 + i
                    pe.wait_ge(ev_s, W_CHUNKS * l + n + 1)
                    w_chunk(l, n, *slot_of(("w", l, n)))
                    if 1 <= i <= 4:
                        if i == 1:
                            pe.wait_ge(vtm_s, 2 * (l + 1))
                        for h in (2 * i - 2, 2 * i - 1):
                            probs_transpose(l, h)
                    if i < 4:
                        for h in (2 * i, 2 * i + 1):
                            scores(l, h)
                    if 1 <= i <= 4:
                        for h in (2 * i - 2, 2 * i - 1):
                            pv(l, h)
                    if i == 5:
                        pe.wait_ge(xsil_s, 3 * (l + 1))
                        for t in range(TT):
                            for q in range(2):
                                for m in range(4):
                                    last = nc.tensor.transpose(ps[:, 3 + 2 * t + q, m * P:(m + 1) * P],
                                                               xc[:, 4 * q + m, t * P:(t + 1) * P], ident[:, :])
                                last.then_inc(xst_s, 1)
                        pe.wait_ge(ao_s, 4 * (l + 1))
                        for g in range(GROUPS):
                            last = nc.tensor.transpose(ps[:, 7, g * P:(g + 1) * P], xc[:, 8 + g, 0:P], ident[:, :])
                        last.then_inc(xst_s, 1)
                        pe.wait_ge(dt_s, l + 1)
                        for cc in range(TT):
                            mm(ps[:, 2, 336 + cc * HEADS_S:336 + (cc + 1) * HEADS_S], triu[:, :], dts[:, 4, cc, :],
                               start=True, stop=True)
                        mm(ps[:, 2, 368:384], ones[:, :], dts[:, 4, 0, :], start=True, stop=True).then_inc(ac_s, 1)
                    if i == 6:
                        pe.wait_ge(xse_s, 5 * (l + 1))
                        for g in range(GROUPS):
                            for cc in range(TT):
                                last = mm(ps[:, 7, (2 * g + cc) * P:(2 * g + cc + 1) * P],
                                          xc[:, 8 + g, cc * P:(cc + 1) * P], xc[:, 10 + g, cc * P:(cc + 1) * P],
                                          start=True, stop=True)
                        last.then_inc(cb_s, 1)
                    if i == 7:
                        pe.wait_ge(xd_s, l + 1)
                        for g in range(GROUPS):
                            mm(ps[:, 5 + g, :], b_tm[:, g, :], xdtd[:, g * 512:(g + 1) * 512],
                               start=True, stop=True).then_inc(stt_s, 1)
                        acum_bcast(l, 0)
                    if i >= 8:
                        if i == 8:
                            pe.wait_ge(prev_s, 2 * (l + 1))
                        acum_bcast(l, i - 7)
                        y_batch(l, i - 8)
                for k in range(4, 8):
                    for a in range(4):
                        ada(l, ADA_FIRST + 4 * (k - 4) + a)
                    if k < 7:
                        acum_bcast(l, k + 1)
                    y_batch(l, k)
                pe.wait_ge(cu_s, l + 1)
                pe.wait_ge(ev_s, 2 + W_CHUNKS * (l + 1))
                for idx in range(4):
                    s, n = slot_of(("conf", l, idx // 2))
                    pe.wait_ge(full[s], n)
                    out_pair(l, idx, s, half, CT, 2 * (idx % 2), cacc)
                pe.wait_ge(gsq_s, 2 * (l + 1))
                for g in range(GROUPS):
                    for k in range(4):
                        last = mm(ps[:, 7, g * SEQ:(g + 1) * SEQ], ones[:, :], ysq[:, 4 * g + k, :],
                                  start=(k == 0), stop=(k == 3))
                last.then_inc(gst_s, 1)
                for idx in range(4):
                    s, n = slot_of(("attn", l, idx // 2))
                    pe.wait_ge(full[s], n)
                    out_pair(l, 4 + idx, s, half, 4, 2 * (idx % 2), ao)
                pe.wait_ge(gn_s, l + 1)
                for idx in range(4):
                    s, n = slot_of(("ssm", l, idx))
                    pe.wait_ge(full[s], n)
                    out_pair(l, 8 + idx, s, wide, KT, 0, proj[:, Z:Z + 8, :])
                pe.wait_ge(mg_s, 16 * l + 12)
                for idx in range(4):
                    s, n = slot_of(("mix", l, idx))
                    pe.wait_ge(full[s], n)
                    out_pair(l, 12 + idx, s, wide, KT, 0, merged)
                if l == 0:
                    for a in range(ADA_FIRST):
                        ada(1, a)
                norm_sums(2 * l + 1)
                pe.wait_ge(h_s, 2 * l + 2)
                if l == 0:
                    for g in range(GD):
                        gs, gn = slot_of(("g", 0, g))
                        us, un = slot_of(("u", 0, g))
                        pe.wait_ge(full[gs], gn)
                        pe.wait_ge(full[us], un)
                        for j in range(2):
                            pe.wait_ge(hm_s, 2 * g + j + 1)
                            gate_up(gs, us, j, hT, SEQ)
                        if g:
                            dsl, dn = slot_of(("d", 0, g - 1))
                            pe.wait_ge(full[dsl], dn)
                            pe.wait_ge(hm_s, HM0 + 2 * g)
                            down(dsl, (g - 1) % 2, SEQ, g == 1, False)
                    dsl, dn = slot_of(("d", 0, GD - 1))
                    pe.wait_ge(full[dsl], dn)
                    pe.wait_ge(hm_s, HM0 + 2 * GD)
                    down(dsl, (GD - 1) % 2, SEQ, False, True)
                    pe.wait_ge(ye_s, 1)
                    for m in range(KT):
                        pe.wait_ge(cf_s, m + 1)
                        for t in range(TT):
                            last = nc.tensor.transpose(ps[:, 6 + m % 2, t * P:(t + 1) * P],
                                                       ysb[:, t, m * P:(m + 1) * P], ident[:, :])
                        last.then_inc(c_s, 1)

            for t in range(TT):
                for m in range(KT):
                    last = nc.tensor.transpose(ps[:, 2 + 2 * t + m // 4, (m % 4) * P:(m % 4 + 1) * P],
                                               hT[:, m, t * P:(t + 1) * P], ident[:, :])
                last.then_inc(htr_s, 1)
            for t in range(TT):
                for k in range(KT):
                    last = mm(ps[:, 0, t * EXPERTS:(t + 1) * EXPERTS], hT[:, k, t * P:(t + 1) * P], rw[:, k, :],
                              start=(k == 0), stop=(k == KT - 1))
            last.then_inc(lg_s, 1)
            pe.wait_ge(mk_s, 1)
            mask = rt[:, 12, :, :]
            mm(ps[:, 1, 0:8], striu[:, :], mask[:, 0, :], start=True, stop=True)
            mm(ps[:, 1, 8:16], ones[:, :], mask[:, 0, :], start=True, stop=False)
            mm(ps[:, 1, 8:16], striu[:, :], mask[:, 1, :], start=False, stop=True)
            mm(ps[:, 1, 16:24], ones[:, :], mask[:, 0, :], start=True, stop=False)
            mm(ps[:, 1, 16:24], ones[:, :], mask[:, 1, :], start=False, stop=True).then_inc(cum_s, 1)

            C_BASE, PER = KT, 1 + 2 * KT

            def gather(free_at):
                for m in range(KT):
                    pe.wait_ge(cf_s, free_at + m)
                    for t in range(TT):
                        last = mm(ps[:, 6 + (m + 1) % 2, 0:SEQ], h_tm[:, t, m * P:(m + 1) * P], p_m[:, t, :],
                                  start=(t == 0), stop=(t == TT - 1))
                    last.then_inc(c_s, 1)

            pe.wait_ge(htm_s, TT)
            pe.wait_ge(p_s, 1)
            gather(CF0 + C_BASE - 1)
            pe.wait_ge(rk_s, 2)
            C1 = C_BASE + KT
            with pe.Fori(0, EXPERTS) as e:
                count = pe.value_load(cnt[0:1, ds(e, 1)], min_val=0, max_val=SEQ)
                pe.wait_ge(cf_s, e * PER + CF0 + C1)
                pe.wait_ge(ye_s, e + 1)

                def expert(n):
                    def group(gi, b, wait_tiles):
                        pe.wait_ge(full[b], gi * 16 + 16 * FILLS[b] + 16)
                        pe.wait_ge(full[2 + b], gi * 16 + 16 * FILLS[2 + b] + 16)
                        for j in range(2):
                            pe.wait_ge(hm_s, wait_tiles + j + 1)
                            gate_up(b, 2 + b, j, xg, n)

                    def group_down(gi, b, tiles, first, stop):
                        pe.wait_ge(full[4 + b], gi * 16 + 16 * FILLS[4 + b] + 16)
                        pe.wait_ge(hm_s, tiles + HM0)
                        down(4 + b, b, n, first, stop)

                    T0 = e * (2 * GE) + 2 * GD
                    half_e = e * (GE // 2)
                    group(half_e, 0, T0)
                    group(half_e, 1, T0 + 2)
                    group_down(half_e, 0, T0 + 2, True, False)
                    with pe.Fori(1, GE // 2) as i:
                        for b in range(2):
                            group(half_e + i, b, T0 + i * 4 + 2 * b)
                            if b == 0:
                                group_down(half_e + i - 1, 1, T0 + i * 4, False, False)
                            else:
                                group_down(half_e + i, 0, T0 + i * 4 + 2, False, False)
                    group_down(half_e + GE // 2 - 1, 1, T0 + 2 * GE, False, True)

                with pe.If(count <= P):
                    expert(P)
                with pe.Else():
                    expert(SEQ)
                pe.wait_ge(pg_s, e + 1)
                pe.wait_ge(cf_s, e * PER + CF0 + C1)
                for st in range(2):
                    for t in range(TT):
                        last = nc.tensor.transpose(ps[:, 6, st * SEQ + t * P:st * SEQ + (t + 1) * P],
                                                   pg_m[:, t, st * P:(st + 1) * P], ident[:, :])
                last.then_inc(c_s, 1)
                pe.wait_ge(p_s, e + 2)
                gather(e * PER + CF0 + C1)
                pe.wait_ge(ye_s, e + 2)
                for m in range(KT):
                    pe.wait_ge(cf_s, e * PER + CF0 + C1 + KT + m)
                    mm(ps[:, 6 + (m + 1) % 2, 0:SEQ], ysb[:, 0, m * P:(m + 1) * P], pgT[:, 0, :], start=True, stop=False)
                    mm(ps[:, 6 + (m + 1) % 2, 0:SEQ], ysb[:, 1, m * P:(m + 1) * P], pgT[:, 1, :], start=False,
                       stop=True).then_inc(c_s, 1)

            norm_sums(2 * DEPTH)
            pe.wait_ge(h_s, 2 * DEPTH + 1)
            for t in range(TT):
                for m in range(KT):
                    last = nc.tensor.transpose(ps[:, 4 + 2 * t + m // 4, (m % 4) * P:(m % 4 + 1) * P],
                                               hT[:, m, t * P:(t + 1) * P], ident[:, :])
                    if m % 4 == 3:
                        last.then_inc(fin_s, 1)

        @block.scalar
        def _(act):
            a_ = nc.scalar.activation
            steps = [0]

            def then_wait(ins):
                steps[0] += 1
                ins.then_inc(ast, 1)
                act.wait_ge(ast, steps[0])

            for dst, src in param_loads():
                act.dma_start(dst, src).then_inc(par_s, 16)
            act.wait_ge(pcol_s, 1)
            a_(ccol[:, :], pcol[:, 0, R_C:R_C + KT], ACT.Silu).then_inc(ccol_s, 1)

            def norm(ni):
                act.wait_ge(x_s, ni + 1)
                a_(sq[:, :, :], xT[:, :, :], ACT.Square).then_inc(sq_s, 1)
                act.wait_ge(var_s, ni + 1)
                a_(rs[:, 1, :], rs[:, 0, :], ACT.Sqrt).then_inc(sd_s, 1)

            def evac(l, n):
                act.wait_ge(proj_s, W_CHUNKS * l + n + 1)
                a_(proj[:, 2 * n:2 * n + 2, :], ps[:, n % 2, :].rearrange("p (a b) -> p a b", a=2),
                   ACT.Copy).then_inc(ev_s, 1)

            def evac_y(n, idx):
                for t in range(n // P):
                    for hf in range(2):
                        last = a_(ysb[:, t, hf * 512:(hf + 1) * 512], ps[:, 2 + 2 * t + hf, :], ACT.Copy)
                last.then_inc(ye_s, 1)

            for l in range(DEPTH):
                norm(2 * l)
                act.wait_ge(dtin_s, l + 1)
                a_(dts[:, 1, :, :], dts[:, 1, :, :], ACT.Exp, scale=-1.0).then_inc(dtexp_s, 1)
                a_(alog[:, l, :], alog[:, l, :], ACT.Exp).then_inc(dtexp_s, 1)
                act.wait_ge(dtexp_s, 2 * l + 2)
                a_(dts[:, 2, :, :], dts[:, 1, :, :], ACT.Ln, bias=1.0).then_inc(dtln_s, 1)
                for n in range(4):
                    evac(l, n)
                act.wait_ge(ev_s, 2 + W_CHUNKS * l + 4)
                a_(proj[:, GLU:GLU + CT, :], proj[:, GLU:GLU + CT, :], ACT.Sigmoid).then_inc(sig_s, 1)
                for n in range(4, 18):
                    evac(l, n)
                for q in range(3):
                    act.wait_ge(xv_s, 3 * l + q + 1)
                    a_(xc[:, 4 * q:4 * q + 4, :], xc[:, 4 * q:4 * q + 4, :], ACT.Silu).then_inc(xsil_s, 1)
                a_(proj[:, Z:Z + 8, :], proj[:, Z:Z + 8, :], ACT.Silu).then_inc(zs_s, 1)
                act.wait_ge(cx_s, l + 1)
                a_(csq[:, :, :], cacc[:, :, :], ACT.Square).then_inc(csq_s, 1)
                evac(l, 18)
                evac(l, 19)
                for t in range(TT):
                    act.wait_ge(vt_s, 2 * l + t + 1)
                    a_(v_tm[:, t, :], ps[:, 5 + t, :], ACT.Copy).then_inc(vtm_s, 1)
                act.wait_ge(cvr_s, l + 1)
                a_(rs[:, 1, :], rs[:, 0, :], ACT.Sqrt).then_inc(csd_s, 1)
                act.wait_ge(cn_s, l + 1)
                for m in range(CT):
                    last = a_(cacc[:, m, :], cacc[:, m, :], ACT.Silu, bias=pcol[:, l, R_LB + m:R_LB + m + 1],
                              scale=pcol[:, l, R_LW + m:R_LW + m + 1])
                last.then_inc(cu_s, 1)
                for i in range(12):
                    if 1 <= i <= 4:
                        for h in (2 * i - 2, 2 * i - 1):
                            b = h % 2
                            act.wait_ge(mx_s, HEADS_A * l + h + 1)
                            a_(sc[:, b, 0:P], sc[:, b, 0:P], ACT.Exp, bias=smx[:, b, 1, 0:1], accum_out=smx[:, b, 2, 0:1])
                            a_(sc[:, b, P:384], sc[:, b, P:384], ACT.Exp, bias=smx[:, b, 1, 1:2],
                               accum_out=smx[:, b, 2, 1:2]).then_inc(ex_s, 1)
                    if i >= 8:
                        k = i - 8
                        act.wait_ge(seg_s, 8 * l + k + 1)
                        if k % 2:
                            a_(cdec[:, :, :], ps[:, 3 + k % 2, :].rearrange("p (a b) -> p a b", a=4), ACT.Exp)
                        a_(seg[:, k % 2, :, :], seg[:, k % 2, :, :], ACT.Exp).then_inc(ls_s, 1)
                    evac(l, 20 + i)
                    if 1 <= i <= 4:
                        for h in (2 * i - 2, 2 * i - 1):
                            act.wait_ge(ptr_s, HEADS_A * l + h + 1)
                            a_(pT[:, h % 2, :], ps[:, 5 + h % 2, 0:384], ACT.Copy).then_inc(pte_s, 1)
                    if i == 5:
                        for q in range(4):
                            act.wait_ge(xst_s, 5 * l + q + 1)
                            a_(xs_tm[:, q // 2, (q % 2) * 512:(q % 2 + 1) * 512], ps[:, 3 + q, :],
                               ACT.Copy).then_inc(xse_s, 1)
                        act.wait_ge(xst_s, 5 * l + 5)
                        a_(b_tm[:, :, :], ps[:, 7, 0:SEQ].rearrange("p (a b) -> p a b", a=2), ACT.Copy).then_inc(xse_s, 1)
                        act.wait_ge(acs_s, l + 1)
                        a_(dec[:, 1, :], dec[:, 0, :], ACT.Exp).then_inc(dcy_s, 1)
                    if i == 7:
                        for g in range(GROUPS):
                            act.wait_ge(stt_s, 2 * l + g + 1)
                            a_(prev[:, g, :], ps[:, 5 + g, :], ACT.Copy).then_inc(prev_s, 1)
                for k in range(4, 8):
                    act.wait_ge(seg_s, 8 * l + k + 1)
                    if k % 2:
                        a_(cdec[:, :, :], ps[:, 3 + k % 2, :].rearrange("p (a b) -> p a b", a=4), ACT.Exp)
                    a_(seg[:, k % 2, :, :], seg[:, k % 2, :, :], ACT.Exp).then_inc(ls_s, 1)
                act.wait_ge(ev_s, 2 + W_CHUNKS * (l + 1))
                for g in range(3):
                    a_(proj[:, GATE + 8 * g:GATE + 8 * g + 8, :], proj[:, GATE + 8 * g:GATE + 8 * g + 8, :],
                       ACT.Sigmoid).then_inc(gate_s, 1)
                for g in range(GROUPS):
                    act.wait_ge(yz_s, 4 * l + 2 * g + 2)
                    a_(ysq[:, 4 * g:4 * g + 4, :], proj[:, Z + 4 * g:Z + 4 * g + 4, :], ACT.Square).then_inc(gsq_s, 1)
                act.wait_ge(gv_s, l + 1)
                a_(gr[:, 1, :, :], gr[:, 0, :, :], ACT.Sqrt).then_inc(gsd_s, 1)
                norm(2 * l + 1)
                if l == 0:
                    for T in range(2 * GD):
                        act.wait_ge(gu_s, T + 1)
                        a_(sil[:, T % 2, :], ps[:, T % 2, 0:SEQ], ACT.Silu).then_inc(sil_s, 1)
                    act.wait_ge(dn_s, DN0 + GD)
                    evac_y(SEQ, 0)

            for t in range(TT):
                act.wait_ge(htr_s, t + 1)
                for hf in range(2):
                    last = a_(h_tm[:, t, hf * 512:(hf + 1) * 512], ps[:, 2 + 2 * t + hf, :], ACT.Copy)
                last.then_inc(htm_s, 1)
            act.wait_ge(re_s, 1)
            a_(rt[:, 8, :, 1:2], rt[:, 8, :, 0:1], ACT.Exp).then_inc(rx_s, 1)
            act.wait_ge(rk_s, 2)
            with act.Fori(0, EXPERTS) as e:
                count = act.value_load(cnt[0:1, ds(e, 1)], min_val=0, max_val=SEQ)

                def expert(n):
                    with act.Fori(0, GE) as i:
                        for j in range(2):
                            act.wait_ge(gu_s, e * (2 * GE) + i * 2 + 2 * GD + j + 1)
                            a_(sil[:, j, 0:n], ps[:, j, 0:n], ACT.Silu).then_inc(sil_s, 1)
                    act.wait_ge(dn_s, e * GE + DN0 + GD + GE)
                    evac_y(n, 0)

                with act.If(count <= P):
                    expert(P)
                with act.Else():
                    expert(SEQ)
            norm(2 * DEPTH)
            for q in range(2 * TT):
                act.wait_ge(fin_s, q + 1)
                a_(o_tm[:, q // 2, (q % 2) * 512:(q % 2 + 1) * 512], ps[:, 4 + q, :], ACT.Copy).then_inc(o_s, 1)

        @block.vector
        def _(dve):
            v = nc.vector
            steps = [0]

            def then_wait(ins):
                steps[0] += 1
                ins.then_inc(vst, 1)
                dve.wait_ge(vst, steps[0])

            for s, n in ((ev_s, 2), (cv_s, CV0), (hm_s, HM0), (dn_s, DN0), (cf_s, CF0)):
                dve.sem_inc(s, n)
            v.memset(key9[:, :, EXPERTS:EXPERTS + 1], -1.0)
            v.memset(gate9[:, :, EXPERTS:EXPERTS + 1], 0.0)
            then_wait(v.memset(cntf[:, :], 0.0))

            dve.wait_ge(xtr_s, 1)
            for b in range(4):
                last = v.tensor_copy(xT[:, 2 * b:2 * b + 2, :], ps[:, b, :].rearrange("p (a b) -> p a b", a=2))
            last.then_inc(x_s, 1)
            dve.wait_ge(prow_s, 1)
            for l in range(DEPTH):
                v.tensor_copy(pcol[:, l, :], ps[:, 4 + l, 0:ROWS])
                v.tensor_copy(cwcol[:, l, :], ps[:, 4 + l, 128:128 + CONF_TAPS * CT])
                last = v.tensor_copy(swcol[:, l, :], ps[:, 4 + l, 256:256 + SSM_TAPS * XT])
            last.then_inc(pcol_s, 1)
            dve.wait_ge(pcol_s, 1)
            dve.wait_ge(par_s, 16 * N_PARAMS)
            for hh in range(2):
                p0 = DH * hh
                v.tensor_copy(dcol[p0:p0 + DH, :, :], dall[p0:p0 + DH, :, hh:HEADS_S:2])

            def bc(ap, n):
                return ap.unsqueeze(1).broadcast_to([P, n, ap.shape[-1]])

            def modulation(l, part):
                c0, c1 = (0, 16) if part == 0 else (16, 48)
                dve.wait_ge(ada_s, ADA_CHUNKS * l + (ADA_FIRST if part == 0 else ADA_CHUNKS))
                v.tensor_tensor(modc[:, c0:c1], ps[:, 2, 288 + c0:288 + c1], pcol[:, l, R_ADA + c0:R_ADA + c1],
                                ALU.add).then_inc(mod_s, 1)
                dve.wait_ge(mod_s, 2 * l + part + 1)
                s0, w0 = (8, R_N1) if part == 0 else (32, R_N2)
                then_wait(v.scalar_tensor_tensor(acolw[:, part, :], modc[:, s0:s0 + KT], 1.0,
                                                 pcol[:, l, w0:w0 + KT], ALU.add, ALU.mult))

            def rms(ni, factor, shift):
                dve.wait_ge(st_s, ni + 1)
                v.tensor_scalar(rs[:, 0, :], ps[:, 2, 0:SEQ], 1.0 / D_MODEL, EPS, ALU.mult, ALU.add).then_inc(var_s, 1)
                dve.wait_ge(sd_s, ni + 1)
                then_wait(v.reciprocal(rs[:, 2, :], rs[:, 1, :]))
                then_wait(v.tensor_tensor(sq[:, :, :], xT[:, :, :], bc(rs[:, 2, :], KT), ALU.mult))
                for m in range(KT):
                    if shift is None:
                        last = v.tensor_scalar(hT[:, m, :], sq[:, m, :], factor[:, m:m + 1], None, ALU.mult)
                    else:
                        last = v.tensor_scalar(hT[:, m, :], sq[:, m, :], factor[:, m:m + 1], shift[:, m:m + 1],
                                               ALU.mult, ALU.add)
                last.then_inc(h_s, 1)

            def head_scores(l, h):
                b, n = h % 2, HEADS_A * l + h
                dve.wait_ge(sc_s, n + 1)
                if n >= 2:
                    dve.wait_ge(ptr_s, n - 1)
                v.scalar_tensor_tensor(sc[:, b, :], ps[:, 3 + b, 0:384], DH ** -0.5, amask[:, :],
                                       ALU.mult, ALU.add).then_inc(msk_s, 1)
                dve.wait_ge(msk_s, n + 1)
                v.reduce_max(smx[:, b, 0, 0:1], sc[:, b, 0:P], AX.X)
                then_wait(v.reduce_max(smx[:, b, 0, 1:2], sc[:, b, P:384], AX.X))
                v.tensor_scalar(smx[:, b, 1, :], smx[:, b, 0, :], -1.0, None, ALU.mult).then_inc(mx_s, 1)

            def head_probs(l, h):
                b, n = h % 2, HEADS_A * l + h
                dve.wait_ge(ex_s, n + 1)
                then_wait(v.reciprocal(smx[:, b, 3, :], smx[:, b, 2, :]))
                v.tensor_scalar(sc[:, b, 0:P], sc[:, b, 0:P], smx[:, b, 3, 0:1], None, ALU.mult)
                v.tensor_scalar(sc[:, b, P:384], sc[:, b, P:384], smx[:, b, 3, 1:2], None, ALU.mult).then_inc(pr_s, 1)

            def seg_of(l, k):
                hb, cc = k // 2, k % 2
                dve.wait_ge(bc_s, 8 * l + k + 1)
                if 8 * l + k >= 2:
                    dve.wait_ge(y_s, 8 * l + k - 1)
                for r in range(4):
                    last = v.tensor_scalar(seg[:, k % 2, r, :], ps[:, 3 + k % 2, r * P:(r + 1) * P],
                                           acum[:, cc, 4 * hb + r:4 * hb + r + 1], 0.0, ALU.subtract, ALU.min)
                last.then_inc(seg_s, 1)

            def lmat(l, k):
                hb, cc = k // 2, k % 2
                dve.wait_ge(ls_s, 8 * l + k + 1)
                if cc:
                    v.tensor_tensor(cdec[:, :, :], cdec[:, :, :], bc(xc[:, 10 + hb // 2, P:SEQ], 4), ALU.mult)
                v.tensor_tensor(seg[:, k % 2, :, :], seg[:, k % 2, :, :], bc(cbm[:, hb // 2, cc, :], 4),
                                ALU.mult).then_inc(lm_s, 1)

            def y_out(l, hb):
                dve.wait_ge(y_s, 8 * l + 2 * hb + 2)
                for j in range(2):
                    m = 2 * hb + j
                    last = v.scalar_tensor_tensor(xc[:, m, :], xc[:, m, :], dcol[:, l, m:m + 1],
                                                  ps[:, 5 + hb % 2, j * SEQ:(j + 1) * SEQ], ALU.mult, ALU.add)
                then_wait(last)
                z = proj[:, Z + 2 * hb:Z + 2 * hb + 2, :]
                v.tensor_tensor(z, xc[:, 2 * hb:2 * hb + 2, :], z, ALU.mult).then_inc(yz_s, 1)

            def residual(l, idx, first_col):
                for j in range(2):
                    m = 2 * idx + j
                    last = v.scalar_tensor_tensor(xT[:, m, :], ps[:, idx % 2, j * SEQ:(j + 1) * SEQ],
                                                  modc[:, first_col + m:first_col + m + 1], xT[:, m, :],
                                                  ALU.mult, ALU.add)
                return last

            for l in range(DEPTH):
                if l == 0:
                    modulation(l, 0)
                rms(2 * l, acolw[:, 0, :], modc[:, 0:KT])
                dve.wait_ge(dtmm_s, l + 1)
                then_wait(v.tensor_tensor(dts[:, 0, :, :], ps[:, 2, 256:288].rearrange("p (a b) -> p a b", a=2),
                                          bc(dtb[:, l, :], TT), ALU.add))
                then_wait(v.tensor_scalar(dts[:, 3, :, :], dts[:, 0, :, :], -1.0, None, ALU.mult))
                v.tensor_tensor(dts[:, 1, :, :], dts[:, 0, :, :], dts[:, 3, :, :], ALU.max).then_inc(dtin_s, 1)
                dve.wait_ge(dtln_s, l + 1)
                then_wait(v.scalar_tensor_tensor(dts[:, 3, :, :], dts[:, 0, :, :], 0.0, dts[:, 2, :, :], ALU.max, ALU.add))
                v.scalar_tensor_tensor(dts[:, 4, :, :], dts[:, 3, :, :], -1.0, bc(alog[:, l, :], TT),
                                       ALU.mult, ALU.mult).then_inc(dt_s, 1)
                dve.wait_ge(sig_s, l + 1)
                if l:
                    dve.wait_ge(cvar_s, l)
                    v.memset(cpad[:, :, 0:PADC], 0.0)
                then_wait(v.tensor_tensor(cpad[:, :, PADC:], proj[:, VAL:VAL + CT, :], proj[:, GLU:GLU + CT, :], ALU.mult))
                for m in range(CT):
                    v.tensor_scalar(cacc[:, m, :], cpad[:, m, 0:SEQ], cwcol[:, l, m:m + 1],
                                    pcol[:, l, R_CB + m:R_CB + m + 1], ALU.mult, ALU.add).then_inc(cv_s, 1)
                C0 = CV0 + l * CT * CONF_TAPS
                with dve.Fori(1, CONF_TAPS) as k:
                    for m in range(CT):
                        dve.wait_ge(cv_s, k * CT + C0 + m + 1 - CT)
                        v.scalar_tensor_tensor(cacc[:, m, :], cpad[:, m, ds(k, SEQ)], cwcol[:, l, ds(k * CT + m, 1)],
                                               cacc[:, m, :], ALU.mult, ALU.add).then_inc(cv_s, 1)
                for q in range(3):
                    dve.wait_ge(ev_s, 2 + W_CHUNKS * l + XBC // 2 + 2 * q + 2)
                    for tap in range(SSM_TAPS - 1, -1, -1):
                        sh = SSM_TAPS - 1 - tap
                        for m in range(4 * q, 4 * q + 4):
                            w = swcol[:, l, tap * XT + m:tap * XT + m + 1]
                            if sh == 0:
                                last = v.tensor_scalar(xc[:, m, :], proj[:, XBC + m, :], w,
                                                       pcol[:, l, R_SB + m:R_SB + m + 1], ALU.mult, ALU.add)
                            else:
                                last = v.scalar_tensor_tensor(xc[:, m, sh:], proj[:, XBC + m, 0:SEQ - sh], w,
                                                              xc[:, m, sh:], ALU.mult, ALU.add)
                        if sh < SSM_TAPS - 1:
                            then_wait(last)
                    last.then_inc(xv_s, 1)
                dve.wait_ge(cm_s, l + 1)
                then_wait(v.tensor_scalar(rs[:, 2, :], ps[:, 2, 0:SEQ], 1.0 / CONF_WIDTH, None, ALU.mult))
                v.tensor_tensor(cacc[:, :, :], cacc[:, :, :], bc(rs[:, 2, :], CT), ALU.subtract).then_inc(cx_s, 1)
                dve.wait_ge(cvar_s, l + 1)
                v.tensor_scalar(rs[:, 0, :], ps[:, 2, 0:SEQ], 1.0 / CONF_WIDTH, EPS, ALU.mult, ALU.add).then_inc(cvr_s, 1)
                dve.wait_ge(csd_s, l + 1)
                then_wait(v.reciprocal(rs[:, 2, :], rs[:, 1, :]))
                v.tensor_tensor(cacc[:, :, :], cacc[:, :, :], bc(rs[:, 2, :], CT), ALU.mult).then_inc(cn_s, 1)
                for i in range(1, 5):
                    for h in (2 * i - 2, 2 * i - 1):
                        head_scores(l, h)
                    for h in (2 * i - 2, 2 * i - 1):
                        head_probs(l, h)
                    dve.wait_ge(pv_s, HEADS_A * l + 2 * i)
                    v.tensor_copy(ao[:, i - 1, :], ps[:, 7, (i - 1) % 2 * SEQ:(i - 1) % 2 * SEQ + SEQ]).then_inc(ao_s, 1)
                dve.wait_ge(ac_s, l + 1)
                then_wait(v.tensor_copy(acum[:, :, :], ps[:, 2, 336:368].rearrange("p (a b) -> p a b", a=2)))
                v.tensor_tensor(dec[:, 0, :], ps[:, 2, 368:384], acum[:, 0, :], ALU.subtract).then_inc(acs_s, 1)
                dve.wait_ge(xse_s, 5 * (l + 1))
                for t in range(TT):
                    last = v.tensor_tensor(xdt[:, t, :].rearrange("p (h d) -> p h d", d=DH),
                                           xs_tm[:, t, :].rearrange("p (h d) -> p h d", d=DH),
                                           dts[:, 3, t, :].unsqueeze(2).broadcast_to([P, HEADS_S, DH]), ALU.mult)
                then_wait(last)
                dve.wait_ge(dcy_s, l + 1)
                v.tensor_tensor(xdtd.rearrange("p (h d) -> p h d", d=DH), xdt[:, 0, :].rearrange("p (h d) -> p h d", d=DH),
                                dec[:, 1, :].unsqueeze(2).broadcast_to([P, HEADS_S, DH]), ALU.mult).then_inc(xd_s, 1)
                dve.wait_ge(cb_s, l + 1)
                then_wait(v.tensor_tensor(cbm[:, :, :, :].rearrange("p a b c -> p (a b) c"),
                                          ps[:, 7, :].rearrange("p (a b) -> p a b", a=4), bc(triu[:, :], 4), ALU.mult))
                for k in range(8):
                    seg_of(l, k)
                    lmat(l, k)
                    if k >= 2 and k % 2 == 0:
                        y_out(l, k // 2 - 1)
                dve.wait_ge(zs_s, l + 1)
                y_out(l, 3)
                modulation(l, 1)
                dve.wait_ge(gate_s, 3 * (l + 1))
                for idx in range(4):
                    dve.wait_ge(om_s, 16 * l + idx + 1)
                    v.tensor_tensor(merged[:, 2 * idx:2 * idx + 2, :], ps[:, idx % 2, :].rearrange("p (a b) -> p a b", a=2),
                                    proj[:, GATE + 2 * idx:GATE + 2 * idx + 2, :], ALU.mult).then_inc(mg_s, 1)
                dve.wait_ge(gst_s, l + 1)
                v.tensor_scalar(gr[:, 0, :, :], ps[:, 7, :].rearrange("p (a b) -> p a b", a=2), 1.0 / 512, EPS,
                                ALU.mult, ALU.add).then_inc(gv_s, 1)
                dve.wait_ge(gsd_s, l + 1)
                then_wait(v.reciprocal(gr[:, 2, :, :], gr[:, 1, :, :]))
                for m in range(KT):
                    last = v.scalar_tensor_tensor(proj[:, Z + m, :], proj[:, Z + m, :], pcol[:, l, R_SN + m:R_SN + m + 1],
                                                  gr[:, 2, m // 4, :], ALU.mult, ALU.mult)
                last.then_inc(gn_s, 1)
                for idx, g0 in [(i, GATE + 16) for i in range(4)] + [(i, GATE + 8) for i in range(4)]:
                    n = 4 + idx + (4 if g0 == GATE + 8 else 0)
                    dve.wait_ge(om_s, 16 * l + n + 1)
                    g = proj[:, g0 + 2 * idx:g0 + 2 * idx + 2, :]
                    then_wait(v.tensor_tensor(g, ps[:, idx % 2, :].rearrange("p (a b) -> p a b", a=2), g, ALU.mult))
                    v.tensor_tensor(merged[:, 2 * idx:2 * idx + 2, :], merged[:, 2 * idx:2 * idx + 2, :], g,
                                    ALU.add).then_inc(mg_s, 1)
                for idx in range(4):
                    dve.wait_ge(om_s, 16 * l + 12 + idx + 1)
                    last = residual(l, idx, 16)
                    last.then_inc(mg_s, 1)
                dve.wait_ge(mg_s, 16 * (l + 1))
                dve.sem_inc(x_s, 1)
                if l == 0:
                    modulation(1, 0)
                rms(2 * l + 1, acolw[:, 1, :], modc[:, 24:32])
                if l == 0:
                    for T in range(2 * GD):
                        g = T // 2
                        dve.wait_ge(sil_s, T + 1)
                        dve.wait_ge(dn_s, g + 1)
                        v.tensor_tensor(hm[:, g % 2, T % 2, :], sil[:, T % 2, :], ps[:, T % 2, SEQ:2 * SEQ],
                                        ALU.mult).then_inc(hm_s, 1)
                    for m in range(KT):
                        dve.wait_ge(c_s, m + 1)
                        v.scalar_tensor_tensor(xT[:, m, :], ps[:, 6 + m % 2, 0:SEQ], modc[:, 40 + m:41 + m], xT[:, m, :],
                                               ALU.mult, ALU.add).then_inc(cf_s, 1)
                    dve.wait_ge(cf_s, CF0 + KT)
                    dve.sem_inc(x_s, 1)

            R = [rt[:, i, :, :] for i in range(20)]
            dve.wait_ge(lg_s, 1)
            then_wait(v.tensor_tensor(R[0], ps[:, 0, 0:16].rearrange("p (a b) -> p a b", a=2), bc(rb[:, :], TT), ALU.add))
            then_wait(v.tensor_scalar(R[1], bc(slot_f[:, 0:EXPERTS], TT), -1.0, float(EXPERTS), ALU.mult, ALU.add))
            logits = R[0]
            for pick, (m_, mask_) in enumerate(((2, 10), (3, 11))):
                then_wait(v.tensor_reduce(rt[:, m_, :, 0:1], logits, AX.X, ALU.max))
                then_wait(v.tensor_tensor(R[4], logits, rt[:, m_, :, 0:1].broadcast_to([P, TT, EXPERTS]), ALU.is_equal))
                then_wait(v.tensor_tensor(R[5], R[4], R[1], ALU.mult))
                then_wait(v.tensor_reduce(rt[:, 6, :, 0:1], R[5], AX.X, ALU.max))
                then_wait(v.tensor_tensor(R[mask_], R[1], rt[:, 6, :, 0:1].broadcast_to([P, TT, EXPERTS]), ALU.is_equal))
                if pick == 0:
                    then_wait(v.scalar_tensor_tensor(R[7], R[10], NEG, logits, ALU.mult, ALU.add))
                    logits = R[7]
            v.tensor_tensor(R[12], R[10], R[11], ALU.add).then_inc(mk_s, 1)
            v.tensor_tensor(rt[:, 8, :, 0:1], rt[:, 3, :, 0:1], rt[:, 2, :, 0:1], ALU.subtract).then_inc(re_s, 1)
            dve.wait_ge(rx_s, 1)
            then_wait(v.tensor_scalar(rt[:, 8, :, 2:3], rt[:, 8, :, 1:2], 1.0, None, ALU.add))
            then_wait(v.reciprocal(rt[:, 8, :, 3:4], rt[:, 8, :, 2:3]))
            then_wait(v.tensor_tensor(rt[:, 8, :, 4:5], rt[:, 8, :, 1:2], rt[:, 8, :, 3:4], ALU.mult))
            then_wait(v.tensor_tensor(R[13], R[10], rt[:, 8, :, 3:4].broadcast_to([P, TT, EXPERTS]), ALU.mult))
            then_wait(v.tensor_tensor(R[14], R[11], rt[:, 8, :, 4:5].broadcast_to([P, TT, EXPERTS]), ALU.mult))
            then_wait(v.tensor_tensor(gate9[:, :, 0:EXPERTS], R[13], R[14], ALU.add))
            dve.wait_ge(cum_s, 1)
            v.tensor_copy(cntf[0:1, 0:EXPERTS], ps[0:1, 1, 16:24])
            then_wait(v.scalar_tensor_tensor(R[15], ps[:, 1, 0:16].rearrange("p (a b) -> p a b", a=2), 1.0, R[12],
                                             ALU.add, ALU.mult))
            v.tensor_copy(cnt[:, :], cntf[:, :]).then_inc(rk_s, 1)
            v.tensor_scalar(key9[:, :, 0:EXPERTS], R[15], -1.0, None, ALU.add).then_inc(rk_s, 1)
            dve.wait_ge(rk_s, 2)
            v.memset(moe[:, :, :], 0.0)
            for t in range(TT):
                last = v.tensor_scalar(p_m[:, t, :], slot_f[:, :], key9[:, t, 0:1], None, ALU.is_equal)
            last.then_inc(p_s, 1)
            then_wait(v.memset(ysb[:, 1, :], 0.0))
            for m in range(KT):
                dve.wait_ge(c_s, KT + m + 1)
                v.tensor_copy(xg[:, m, :], ps[:, 6 + (m + 1) % 2, 0:SEQ]).then_inc(cf_s, 1)
            C1, PER = 2 * KT, 1 + 2 * KT
            with dve.Fori(0, EXPERTS) as e:
                count = dve.value_load(cnt[0:1, ds(e, 1)], min_val=0, max_val=SEQ)
                for t in range(TT):
                    v.tensor_scalar(p_m[:, t, :], slot_f[:, :], key9[:, t, ds(e + 1, 1)], None, ALU.is_equal)
                    last = v.tensor_scalar(pg_m[:, t, :], slot_f[:, :], key9[:, t, ds(e, 1)], gate9[:, t, ds(e, 1)],
                                           ALU.is_equal, ALU.mult)
                    if t == 0:
                        continue
                last.then_inc(pg_s, 1)
                dve.wait_ge(pg_s, e + 1)
                dve.sem_inc(p_s, 1)

                def expert(n):
                    with dve.Fori(0, GE // 2) as i:
                        for b in range(2):
                            dve.wait_ge(dn_s, e * GE + i * 2 + GD + b + 1)
                            for j in range(2):
                                dve.wait_ge(sil_s, e * (2 * GE) + i * 4 + 2 * GD + 2 * b + j + 1)
                                v.tensor_tensor(hm[:, b, j, 0:n], sil[:, j, 0:n], ps[:, j, SEQ:SEQ + n],
                                                ALU.mult).then_inc(hm_s, 1)

                with dve.If(count <= P):
                    expert(P)
                with dve.Else():
                    expert(SEQ)
                dve.wait_ge(c_s, e * PER + C1 + 1)
                v.tensor_copy(pgT[:, :, :], ps[:, 6, :].rearrange("p (a b) -> p a b", a=2)).then_inc(cf_s, 1)
                for m in range(KT):
                    dve.wait_ge(c_s, e * PER + C1 + 2 + m)
                    v.tensor_copy(xg[:, m, :], ps[:, 6 + (m + 1) % 2, 0:SEQ]).then_inc(cf_s, 1)
                for m in range(KT):
                    dve.wait_ge(c_s, e * PER + C1 + 2 + KT + m)
                    v.tensor_tensor(moe[:, m, :], ps[:, 6 + (m + 1) % 2, 0:SEQ], moe[:, m, :], ALU.add).then_inc(cf_s, 1)
            dve.wait_ge(cf_s, CF0 + C1 + PER * EXPERTS)
            for m in range(KT):
                last = v.scalar_tensor_tensor(xT[:, m, :], moe[:, m, :], modc[:, 40 + m:41 + m], xT[:, m, :],
                                              ALU.mult, ALU.add)
            last.then_inc(x_s, 1)
            rms(2 * DEPTH, pcol[:, 0, R_FN:R_FN + KT], None)


_INS = ['x', 'c', 'norm1_w', 'norm2_w', 'ada_w', 'ada_b', 'w_in', 'conf_conv_w', 'conf_conv_b', 'conf_ln_w',
        'conf_ln_b', 'conf_out', 'ssm_conv_w', 'ssm_conv_b', 'ssm_dt_bias', 'ssm_A_log', 'ssm_D', 'ssm_norm_w',
        'ssm_out', 'attn_out', 'mix_out', 'ffn_w_gate', 'ffn_w_up', 'ffn_w_down', 'moe_router_w', 'moe_router_b',
        'moe_w_gate', 'moe_w_up', 'moe_w_down', 'final_norm_w']


def kernel(**inputs):
    import numpy as np
    import concourse.bacc as bacc
    from concourse.bass_utils import run_bass_kernel_spmd

    nc = bacc.Bacc("TRN2", target_bir_lowering=False, num_devices=1)
    arrays, args = {}, []
    for name in _INS:
        a = np.ascontiguousarray(inputs[name])
        arrays[f"in_{name}"] = a
        args.append(nc.dram_tensor(f"in_{name}", a.shape, mybir.dt.from_np(a.dtype), kind="ExternalInput").ap())
    out = nc.dram_tensor("out_0", (1, SEQ, D_MODEL), mybir.dt.float32, kind="ExternalOutput").ap()
    trunk(nc, *args, out)
    r = run_bass_kernel_spmd(nc, [arrays], core_ids=[0])
    return r.results[0]["out_0"]
```

```python
import concourse.bass as bass
from concourse import mybir
from contextlib import ExitStack

P = 128
D_MODEL, SEQ, DEPTH = 1024, 256, 2
KT = D_MODEL // P
TT = SEQ // P
CONF_WIDTH, CONF_TAPS = 512, 31
CT = CONF_WIDTH // P
HEADS_S, GROUPS = 16, 2
DI = 1024
XT = 12
SSM_TAPS = 4
HEADS_A, DH = 8, 64
IN_WIDTH = 8208
DT_COL = 3584
FFN_DENSE, FFN_EXPERT, EXPERTS = 2816, 3584, 8
EPS = 1e-6
NEG = -1e30
PADC = CONF_TAPS - 1
VAL, GLU, Z, XBC, Q, K, V, GATE = 0, 4, 8, 16, 28, 32, 36, 40
W_CHUNKS = 32
LOOPED = 12
ADA_CHUNKS = 24
ADA_FIRST = 8
SLOTS = 6
ADA_SLOTS = 2
HALF = 64
SIZES = (HALF, 128, 160, 192, 256)
GD, GE = FFN_DENSE // 256, FFN_EXPERT // 256
R_N1, R_N2, R_ADA, R_CB, R_LW, R_LB, R_SB, R_SN, R_FN, R_C = 0, 8, 16, 64, 68, 72, 76, 88, 96, 104
ROWS = 112


def ring_plan():
    order = []
    for l in range(DEPTH):
        order += [("w", l, n) for n in range(W_CHUNKS)]
        order += [("conf", l, a) for a in range(2)] + [("attn", l, a) for a in range(2)]
        order += [("ssm", l, a) for a in range(4)] + [("mix", l, a) for a in range(4)]
        if l == 0:
            for g in range(GD):
                order += [("g", 0, g), ("u", 0, g)] + ([("d", 0, g - 1)] if g else [])
            order += [("d", 0, GD - 1)]
    plan, last, fills, nxt = {}, {}, [0] * SLOTS, 0
    for key in order:
        if key[0] in "gud":
            slot = {"g": 0, "u": 2, "d": 4}[key[0]] + key[2] % 2
        else:
            slot, nxt = nxt % SLOTS, nxt + 1
        fills[slot] += 1
        plan[key] = (slot, fills[slot], last.get(slot))
        last[slot] = key
    return order, plan, last, fills


def trunk(nc, x, c, norm1_w, norm2_w, ada_w, ada_b, w_in, conf_conv_w, conf_conv_b, conf_ln_w, conf_ln_b, conf_out,
          ssm_conv_w, ssm_conv_b, ssm_dt_bias, ssm_A_log, ssm_D, ssm_norm_w, ssm_out, attn_out, mix_out,
          ffn_w_gate, ffn_w_up, ffn_w_down, moe_router_w, moe_router_b, moe_w_gate, moe_w_up, moe_w_down,
          final_norm_w, out):
    fp32, i32 = mybir.dt.float32, mybir.dt.int32
    ALU, ACT, AX = mybir.AluOpType, mybir.ActivationFunctionType, mybir.AxisListType
    ds = bass.ds
    ORDER, PLAN, LAST, FILLS = ring_plan()
    moe_w_gate, moe_w_up, moe_w_down = moe_w_gate[0], moe_w_up[0], moe_w_down[0]

    ctx = ExitStack()
    with ctx:
        def sb(name, shape, dt=fp32):
            return ctx.enter_context(nc.sbuf_tensor(name, shape, dt))

        def sem(name):
            return ctx.enter_context(nc.semaphore(name))

        ring = sb("ring", [P, SLOTS, 2048])
        proj = sb("proj", [P, 64, SEQ])
        aring = sb("aring", [P, ADA_SLOTS, 2048])
        xT = sb("xT", [P, KT, SEQ])
        hT = sb("hT", [P, KT, SEQ])
        sq = sb("sq", [P, KT, SEQ])
        xc = sb("xc", [P, XT, SEQ])
        cpad = sb("cpad", [P, CT, PADC + SEQ])
        cacc = sb("cacc", [P, CT, SEQ])
        v_tm = sb("v_tm", [P, TT, 512])
        b_tm = sb("b_tm", [P, GROUPS, P])
        heads = sb("heads", [P, 1536])
        cbm = sb("cbm", [P, GROUPS, TT, P])
        ident = sb("ident", [P, P])
        ones = sb("ones", [P, P])
        triu = sb("triu", [P, P])
        striu = sb("striu", [P, P])
        amask = sb("amask", [P, 384])
        slot_f = sb("slot_f", [P, SEQ])
        pcol = sb("pcol", [P, DEPTH, ROWS])
        cwcol = sb("cwcol", [P, DEPTH, CONF_TAPS * CT])
        swcol = sb("swcol", [P, DEPTH, SSM_TAPS * XT])
        ccol = sb("ccol", [P, KT])
        dcol = sb("dcol", [P, DEPTH, KT])
        dtb = sb("dtb", [P, DEPTH, HEADS_S])
        alog = sb("alog", [P, DEPTH, HEADS_S])
        wdt = sb("wdt", [P, DEPTH, KT, HEADS_S])
        rw = sb("rw", [P, KT, EXPERTS])
        rb = sb("rb", [P, EXPERTS])
        modc = sb("modc", [P, 48])
        acolw = sb("acolw", [P, 2, KT])
        rs = sb("rs", [P, 3, SEQ])
        dts = sb("dts", [P, 5, TT, HEADS_S])
        acum = sb("acum", [P, TT, HEADS_S])
        dec = sb("dec", [P, 2, HEADS_S])
        smx = sb("smx", [P, 2, 4, 2])
        key9 = sb("key9", [P, TT, EXPERTS + 1])
        gate9 = sb("gate9", [P, TT, EXPERTS + 1])
        cntf = sb("cntf", [1, EXPERTS + 1])
        cnt = sb("cnt", [1, EXPERTS + 1], i32)
        ps = ctx.enter_context(nc.psum_tensor("ps", [P, 8, 512], fp32))

        x_in = proj[:, 0:8, :].rearrange("p (t a) n -> p t (a n)", t=TT)
        xs_tm = proj[:, XBC:XBC + 8, :].rearrange("p (t a) n -> p t (a n)", t=TT)
        prev = proj[:, XBC + 8:XBC + 12, :].rearrange("p (g a) n -> p g (a n)", g=GROUPS)
        xdt = proj[:, 0:8, :].rearrange("p (t a) n -> p t (a n)", t=TT)
        xdtd = sq[:, 0:4, :].rearrange("p a n -> p (a n)")
        ao = proj[:, V:V + 4, :]
        ysq = proj[:, Q:Q + 8, :]
        merged = hT
        xg_next = hT
        hm = proj[:, 0:4, :].rearrange("p (b j) n -> p b j n", b=2)
        sil = proj[:, 4:6, :]
        hsm = proj[:, 44:46, 0:P]
        pg_m = proj[:, 6:8, :]
        ysb = proj[:, 8:16, :].rearrange("p (t a) n -> p t (a n)", t=TT)
        xg = proj[:, 16:24, :]
        h_tm = proj[:, 24:32, :].rearrange("p (t a) n -> p t (a n)", t=TT)
        p_m = proj[:, 40:42, :]
        pgT = proj[:, 42:44, :]
        o_tm = proj[:, 48:56, :].rearrange("p (t a) n -> p t (a n)", t=TT)
        csq = cpad[:, :, 0:SEQ]
        seg = heads[:, 0:1024].rearrange("p (b r n) -> p b r n", b=2, r=4)
        cdec = heads[:, 1024:1536].rearrange("p (r n) -> p r n", r=4)
        sc = heads[:, 0:768].rearrange("p (b n) -> p b n", b=2)
        pT = heads[:, 768:1536].rearrange("p (b n) -> p b n", b=2)
        aacc = proj[:, GATE:GATE + ADA_CHUNKS, :]
        slot_i = sc[:, 0, 0:SEQ].bitcast(i32)
        prow, cwrow, swrow = (v_tm[:, 0:2, 128 * i:128 * i + 128] for i in range(3))
        dall = v_tm[:, 0:2, 384:384 + HEADS_S]
        rt = cdec[:, :, :].rearrange("p a b -> p (a b)")[:, 0:20 * TT * EXPERTS].rearrange(
            "p (i t e) -> p i t e", t=TT, e=EXPERTS)
        gr = xc[:, 0:6, :].rearrange("p (a b) n -> p a b n", a=3)

        full = [sem(f"ring_full{s}") for s in range(SLOTS)]
        x_in_s = sem("x_loaded")
        par_s = [sem(f"params_loaded{l}") for l in range(DEPTH)]
        cst_s = sem("consts_made")
        pcst = sem("pool_step")
        prow_s = sem("param_rows_transposed")
        pcol_s = sem("param_cols_ready")
        ccol_s = sem("c_act_ready")
        xtr_s = sem("x_transposed")
        x_s = sem("x_ready")
        sq_s = sem("norm_squares")
        st_s = sem("norm_sums")
        var_s = sem("norm_var")
        sd_s = sem("norm_sd")
        nx_s = sem("normed_tiles")
        h_s = sem("h_ready")
        afull = [sem(f"ada_ring_full{s}") for s in range(ADA_SLOTS)]
        aacc_s = sem("ada_partial_ready")
        atr_s = sem("ada_transposed")
        ared_s = sem("ada_reduced")
        mod_s = sem("mod_ready")
        dtmm_s = sem("dt_mm")
        dtin_s = sem("dt_biased")
        dtexp_s = sem("dt_exp")
        dt_s = sem("dt_ready")
        dtln_s = sem("dt_ln")
        proj_s = sem("proj_mm")
        ev_s = sem("proj_evacuated")
        sig_s = sem("glu_sigmoid")
        glu_s = sem("glu_ready")
        cv_s = sem("conf_conv_step")
        cm_s = sem("conf_mean_mm")
        cx_s = sem("conf_centered")
        csq_s = sem("conf_squares")
        cvar_s = sem("conf_var_mm")
        cvr_s = sem("conf_var")
        csd_s = sem("conf_sd")
        cn_s = sem("conf_normed")
        cu_s = sem("conf_u_ready")
        xv_s = sem("xbc_conv")
        xsil_s = sem("xbc_silu")
        zs_s = sem("z_silu")
        vt_s = sem("v_transposed")
        vtm_s = sem("v_tm_ready")
        sc_s = sem("scores_mm")
        msk_s = sem("scores_masked")
        mx_s = sem("scores_max")
        ex_s = sem("scores_exp")
        pr_s = sem("probs_ready")
        ptr_s = sem("probs_transposed")
        pte_s = sem("probs_T_ready")
        pv_s = sem("pv_mm")
        ao_s = sem("attn_ready")
        xst_s = sem("xs_transposed")
        xse_s = sem("xs_tm_ready")
        ac_s = sem("acum_mm")
        acs_s = sem("acum_ready")
        dcy_s = sem("decay_ready")
        cb_s = sem("cb_mm")
        cbm_s = sem("cb_masked")
        xd_s = sem("xdt_ready")
        stt_s = sem("state_mm")
        prev_s = sem("state_ready")
        bc_s = sem("acum_bcast_mm")
        seg_s = sem("seg_ready")
        ls_s = sem("lmat_exp")
        lm_s = sem("lmat_ready")
        y_s = sem("y_mm")
        yz_s = sem("y_gated")
        gsq_s = sem("group_squares")
        gst_s = sem("group_sums")
        gv_s = sem("group_var")
        gsd_s = sem("group_sd")
        gn_s = sem("group_normed")
        gate_s = sem("gates_sigmoid")
        om_s = sem("out_mm")
        mg_s = sem("merge_step")
        htr_s = sem("h_transposed")
        htm_s = sem("h_tm_ready")
        lg_s = sem("logits_mm")
        mk_s = sem("masks_ready")
        re_s = sem("router_exp_in")
        rx_s = sem("router_exp")
        cum_s = sem("slots_mm")
        rk_s = sem("slots_ready")
        p_s = sem("gather_matrix")
        pg_s = sem("scatter_matrix")
        xg_s = sem("expert_tokens_ready")
        c_s = sem("aux_bank_mm")
        cf_s = sem("aux_bank_free")
        gu_s = sem("gate_up_mm")
        sil_s = sem("silu_ready")
        hm_s = sem("h_mid_ready")
        dn_s = sem("down_mm")
        ht_s = sem("h_small_transposed")
        hte_s = sem("h_small_T_ready")
        ye_s = sem("y_evacuated")
        fin_s = sem("final_transposed")
        o_s = sem("out_ready")
        od_s = sem("out_stored")
        vst = sem("vector_step")
        ast = sem("scalar_step")
        CV0 = 1
        HM0 = 2
        DN0 = 2
        CF0 = 2

        def released(key):
            kind, l, a = key
            if kind == "w":
                return proj_s, W_CHUNKS * l + a + 1
            if kind == "conf":
                return om_s, 16 * l + 2 * a + 2
            if kind == "attn":
                return om_s, 16 * l + 4 + 2 * a + 2
            if kind == "ssm":
                return om_s, 16 * l + 8 + a + 1
            if kind == "mix":
                return om_s, 16 * l + 12 + a + 1
            if kind in "gu":
                return gu_s, 2 * a + 2
            return dn_s, DN0 + a + 1

        def slot_of(key):
            s, n, _ = PLAN[key]
            return s, 16 * n

        def wide(s):
            return ring[:, s, :].rearrange("p (k n) -> p k n", k=8)

        def half(s):
            return ring[:, s, :].rearrange("p (k n) -> p k n", k=4)

        def rows2(s):
            return ring[:, s, :].rearrange("p (j n) -> p j n", j=2)

        block = ctx.enter_context(nc.Block())

        def by_size(eng, count, body):
            def at(i):
                if i == len(SIZES) - 1:
                    body(SIZES[i])
                    return
                with eng.If(count <= SIZES[i]):
                    body(SIZES[i])
                with eng.Else():
                    at(i + 1)
                    eng.nop()
            at(0)

        @block.sync
        def _(sp):
            sp.dma_start(x_in[:, 0, :], x[0, 0:P, :]).then_inc(x_in_s, 16)
            sp.dma_start(x_in[:, 1, :], x[0, P:2 * P, :]).then_inc(x_in_s, 16)

            def columns(w, col, width):
                return w[:, col:col + width].rearrange("(k p) n -> p k n", p=P)

            for key in ORDER:
                kind, l, a = key
                s, _, before = PLAN[key]
                if before is not None:
                    sp.wait_ge(*released(before))
                if kind == "w":
                    src, dst = columns(w_in[l], 256 * a + (HEADS_S if 256 * a >= DT_COL else 0), 256), wide(s)
                elif kind == "conf":
                    src, dst = columns(conf_out[l], 512 * a, 512), half(s)
                elif kind == "attn":
                    src, dst = columns(attn_out[l], 512 * a, 512), half(s)
                elif kind == "ssm":
                    src, dst = columns(ssm_out[l], 256 * a, 256), wide(s)
                elif kind == "mix":
                    src, dst = columns(mix_out[l], 256 * a, 256), wide(s)
                elif kind == "g":
                    src, dst = columns(ffn_w_gate[0], 256 * a, 256), wide(s)
                elif kind == "u":
                    src, dst = columns(ffn_w_up[0], 256 * a, 256), wide(s)
                else:
                    src, dst = ffn_w_down[0][256 * a:256 * a + 256, :].rearrange("(j p) n -> p j n", p=P), rows2(s)
                sp.dma_start(dst, src).then_inc(full[s], 16)

            for s in range(6):
                sp.wait_ge(*released(LAST[s]))

            def expert_loads(e, g, b):
                sp.wait_ge(gu_s, e * (2 * GE) + g * 2 + 2 * GD - 2)
                col = g * 256
                sp.dma_start(wide(b), moe_w_gate[ds(e, 1)].rearrange("e (k p) n -> p (e k) n", p=P)[:, :, ds(col, 256)]
                             ).then_inc(full[b], 16)
                sp.dma_start(wide(2 + b), moe_w_up[ds(e, 1)].rearrange("e (k p) n -> p (e k) n", p=P)[:, :, ds(col, 256)]
                             ).then_inc(full[2 + b], 16)

            def expert_down(e, g, b):
                sp.wait_ge(dn_s, e * GE + g + DN0 + GD - 1)
                q = e * GE + g
                sp.dma_start(rows2(4 + b), moe_w_down.rearrange("e r n -> (e r) n")[ds(q * 256, 256), :]
                             .rearrange("(j p) n -> p j n", p=P)).then_inc(full[4 + b], 16)

            with sp.Fori(0, EXPERTS) as e:
                expert_loads(e, 0, 0)
                expert_loads(e, 1, 1)
                expert_down(e, 0, 0)
                with sp.Fori(1, GE // 2) as i:
                    for b in range(2):
                        expert_loads(e, i * 2 + b, b)
                        expert_down(e, i * 2 + b - 1, 1 - b)
                expert_down(e, GE - 1, 1)

            for t in range(TT):
                sp.wait_ge(o_s, 2 * t + 2)
                sp.dma_start(out[0, t * P:(t + 1) * P, :], o_tm[:, t, :]).then_inc(od_s, 16)
            sp.wait_ge(od_s, 16 * TT)

        @block.gpsimd
        def _(pool):
            g = nc.gpsimd
            g.memset(ones[:, :], 1.0).then_inc(pcst, 1)
            g.memset(ident[:, :], 0.0).then_inc(pcst, 1)
            g.memset(amask[:, :], 0.0).then_inc(pcst, 1)
            g.iota(slot_i[:, :], pattern=[[1, SEQ]], base=0, channel_multiplier=0).then_inc(pcst, 1)
            pool.wait_ge(pcst, 4)
            g.affine_select(out=ident[:, :], in_=ident[:, :], compare_op=ALU.not_equal, fill=1.0, base=0,
                            pattern=[[-1, P]], channel_multiplier=1).then_inc(cst_s, 1)
            g.affine_select(out=triu[:, :], in_=ones[:, :], compare_op=ALU.is_ge, fill=0.0, base=0,
                            pattern=[[1, P]], channel_multiplier=-1).then_inc(cst_s, 1)
            g.affine_select(out=striu[:, :], in_=ones[:, :], compare_op=ALU.is_gt, fill=0.0, base=0,
                            pattern=[[1, P]], channel_multiplier=-1).then_inc(cst_s, 1)
            for c0 in (0, 256):
                g.affine_select(out=amask[:, c0:c0 + P], in_=amask[:, c0:c0 + P], compare_op=ALU.is_ge, fill=NEG,
                                base=0, pattern=[[-1, P]], channel_multiplier=1).then_inc(cst_s, 1)
            g.tensor_copy(slot_f[:, :], slot_i[:, :]).then_inc(cst_s, 1)
            g.memset(cpad[:, :, :], 0.0).then_inc(cst_s, 1)

            for n in range(DEPTH * ADA_CHUNKS):
                l, a = n // ADA_CHUNKS, n % ADA_CHUNKS
                if n >= ADA_SLOTS:
                    pool.wait_ge(aacc_s, n - ADA_SLOTS + 1)
                g.dma_start(aring[:, n % ADA_SLOTS, :].rearrange("p (k n) -> p k n", k=KT),
                            ada_w[l][:, 256 * a:256 * a + 256].rearrange("(k p) n -> p k n", p=P)
                            ).then_inc(afull[n % ADA_SLOTS], 16)
        CONSTS = 7

        def param_loads(layer):
            def rows(v):
                return v.rearrange("(m p) -> m p", p=P)
            for l in (layer,):
                for src, r in ((norm1_w[l], R_N1), (norm2_w[l], R_N2), (ada_b[l], R_ADA), (conf_conv_b[l], R_CB),
                               (conf_ln_w[l], R_LW), (conf_ln_b[l], R_LB), (ssm_conv_b[l], R_SB),
                               (ssm_norm_w[l], R_SN), (final_norm_w, R_FN), (c[0], R_C)):
                    v = rows(src)
                    yield prow[r:r + v.shape[0], l, :], v
                yield cwrow[0:CONF_TAPS * CT, l, :], conf_conv_w[l].rearrange("k (m p) -> (k m) p", p=P)
                yield swrow[0:SSM_TAPS * XT, l, :], ssm_conv_w[l].rearrange("k (m p) -> (k m) p", p=P)
            for l in (layer,):
                yield wdt[:, l, :, :], w_in[l][:, DT_COL:DT_COL + HEADS_S].rearrange("(k p) n -> p k n", p=P)
                yield dtb[:, l, :], ssm_dt_bias[l:l + 1, :].broadcast_to([P, HEADS_S])
                yield alog[:, l, :], ssm_A_log[l:l + 1, :].broadcast_to([P, HEADS_S])
                yield dall[:, l, :], ssm_D[l:l + 1, :].broadcast_to([P, HEADS_S])
            if layer == 0:
                return
            yield rw[:, :, :], moe_router_w[0].rearrange("(k p) n -> p k n", p=P)
            yield rb[:, :], moe_router_b[0:1, :].broadcast_to([P, EXPERTS])
        N_PARAMS = [16, 16 + 2]

        @block.tensor
        def _(pe):
            mm = nc.tensor.matmul
            pe.wait_ge(cst_s, CONSTS)
            pe.wait_ge(x_in_s, 32)
            for m in range(KT):
                for t in range(TT):
                    last = nc.tensor.transpose(ps[:, m // 2, (m % 2) * SEQ + t * P:(m % 2) * SEQ + (t + 1) * P],
                                               x_in[:, t, m * P:(m + 1) * P], ident[:, :])
            last.then_inc(xtr_s, 1)
            for l in range(DEPTH):
                pe.wait_ge(par_s[l], 16 * N_PARAMS[l])
                nc.tensor.transpose(ps[:, 4 + l, 0:ROWS], prow[0:ROWS, l, :], ident[0:ROWS, 0:ROWS])
                nc.tensor.transpose(ps[:, 4 + l, 128:128 + CONF_TAPS * CT], cwrow[0:CONF_TAPS * CT, l, :],
                                    ident[0:CONF_TAPS * CT, 0:CONF_TAPS * CT])
                nc.tensor.transpose(ps[:, 4 + l, 256:256 + SSM_TAPS * XT], swrow[0:SSM_TAPS * XT, l, :],
                                    ident[0:SSM_TAPS * XT, 0:SSM_TAPS * XT]).then_inc(prow_s, 1)

            def norm_sums(ni):
                pe.wait_ge(sq_s, ni + 1)
                for k in range(KT):
                    last = mm(ps[:, 2, 0:SEQ], ones[:, :], sq[:, k, :], start=(k == 0), stop=(k == KT - 1))
                last.then_inc(st_s, 1)

            def ada_transpose(l, q):
                n = ADA_CHUNKS // 2 * l + q
                pe.wait_ge(aacc_s, ADA_CHUNKS * l + 2 * q + 2)
                if n >= 2:
                    pe.wait_ge(ared_s, n - 1)
                for j in range(4):
                    last = nc.tensor.transpose(ps[:, 3 + q % 2, j * P:(j + 1) * P],
                                               aacc[:, 2 * q + j // 2, (j % 2) * P:(j % 2 + 1) * P], ident[:, :])
                last.then_inc(atr_s, 1)

            def w_chunk(l, n, s, fill):
                pe.wait_ge(full[s], fill)
                for j in range(2):
                    for k in range(KT):
                        last = mm(ps[:, n % 2, j * SEQ:(j + 1) * SEQ], wide(s)[:, k, j * P:(j + 1) * P], hT[:, k, :],
                                  start=(k == 0), stop=(k == KT - 1))
                last.then_inc(proj_s, 1)

            def scores(l, h):
                if h >= 2:
                    pe.wait_ge(msk_s, HEADS_A * l + h - 1)
                p0 = DH * (h % 2)
                q, k = proj[p0:p0 + DH, Q + h // 2, :], proj[p0:p0 + DH, K + h // 2, :]
                mm(ps[:, 3 + h % 2, 0:P], q[:, 0:P], k[:, 0:P], start=True, stop=True)
                mm(ps[:, 3 + h % 2, P:P + SEQ], q[:, P:SEQ], k[:, :], start=True, stop=True).then_inc(sc_s, 1)

            def probs_transpose(l, h):
                pe.wait_ge(pr_s, HEADS_A * l + h + 1)
                for i in range(3):
                    last = nc.tensor.transpose(ps[:, 5 + h % 2, i * P:(i + 1) * P], sc[:, h % 2, (0, 1, 2)[i] * P:
                                               ((0, 1, 2)[i] + 1) * P], ident[:, :])
                last.then_inc(ptr_s, 1)

            def pv(l, h):
                pe.wait_ge(pte_s, HEADS_A * l + h + 1)
                if h >= 2 and h % 2 == 0:
                    pe.wait_ge(ao_s, 4 * l + h // 2)
                c0, p0 = (h // 2) % 2 * SEQ, DH * (h % 2)
                mm(ps[p0:p0 + DH, 7, c0:c0 + SEQ], v_tm[:, 0, h * DH:(h + 1) * DH], pT[:, h % 2, 0:SEQ],
                   start=True, stop=False)
                mm(ps[p0:p0 + DH, 7, c0 + P:c0 + SEQ], v_tm[:, 1, h * DH:(h + 1) * DH], pT[:, h % 2, SEQ:384],
                   start=False, stop=True).then_inc(pv_s, 1)

            def acum_bcast(l, k):
                hb, cc = k // 2, k % 2
                if k >= 2:
                    pe.wait_ge(lm_s, 8 * l + k - 1)
                for r in range(4):
                    h = 4 * hb + r
                    last = mm(ps[:, 3 + k % 2, r * P:(r + 1) * P], dts[:, 4, cc, h:h + 1].broadcast_to([P, P]),
                              triu[:, :], start=True, stop=True)
                last.then_inc(bc_s, 1)

            def y_batch(l, k):
                hb, cc = k // 2, k % 2
                pe.wait_ge(lm_s, 8 * l + k + 1)
                if hb >= 2 and cc == 0:
                    pe.wait_ge(yz_s, 4 * l + hb - 1)
                for r in range(4):
                    h = 4 * hb + r
                    p0, c0 = DH * (h % 2), (r // 2) * SEQ + cc * P
                    dst = ps[p0:p0 + DH, 5 + hb % 2, c0:c0 + P]
                    last = mm(dst, xdt[:, cc, h * DH:(h + 1) * DH], seg[:, k % 2, r, :], start=True, stop=(cc == 0))
                    if cc == 1:
                        last = mm(dst, prev[:, hb // 2, (h % 8) * DH:(h % 8 + 1) * DH], cdec[:, r, :],
                                  start=False, stop=True)
                last.then_inc(y_s, 1)

            def out_pair(l, idx, s, view, kk, cols, rhs):
                pair = 16 * l + idx
                if pair >= 2:
                    pe.wait_ge(mg_s, pair - 1)
                for j in range(2):
                    for k in range(kk):
                        last = mm(ps[:, idx % 2, j * SEQ:(j + 1) * SEQ], view(s)[:, k, (cols + j) * P:(cols + j + 1) * P],
                                  rhs[:, k, :], start=(k == 0), stop=(k == kk - 1))
                last.then_inc(om_s, 1)

            def gate_up(g_slot, u_slot, j, x_src, n, first=False):
                for w, c0 in ((g_slot, 0), (u_slot, SEQ)):
                    for k in range(KT):
                        if first and w == g_slot:
                            pe.wait_ge(h_s, KT + k + 1)
                        last = mm(ps[:, j, c0:c0 + n], wide(w)[:, k, j * P:(j + 1) * P], x_src[:, k, 0:n],
                                  start=(k == 0), stop=(k == KT - 1))
                last.then_inc(gu_s, 1)

            def down(slot, b, n, first, stop):
                for j in range(2):
                    for t in range((n + P - 1) // P):
                        rows = min(P, n - t * P)
                        for hf in range(2):
                            dst = ps[0:rows, 2 + 2 * t + hf, :] if rows > HALF else ps[HALF * hf:HALF * hf + rows, 4, :]
                            last = mm(dst, hm[:, b, j, t * P:t * P + rows],
                                      rows2(slot)[:, j, hf * 512:(hf + 1) * 512],
                                      start=(first and j == 0), stop=(stop and j == 1))
                last.then_inc(dn_s, 1)

            for l in range(DEPTH):
                if l == 0:
                    for q in range(ADA_FIRST // 2):
                        ada_transpose(0, q)
                norm_sums(2 * l)
                for t in range(TT):
                    for k in range(KT):
                        if t == 0:
                            pe.wait_ge(h_s, 2 * KT * l + k + 1)
                        last = mm(ps[:, 2, 256 + t * HEADS_S:256 + (t + 1) * HEADS_S], hT[:, k, t * P:(t + 1) * P],
                                  wdt[:, l, k, :], start=(k == 0), stop=(k == KT - 1))
                last.then_inc(dtmm_s, 1)
                with pe.Fori(0, LOOPED // SLOTS) as i:
                    for b in range(SLOTS):
                        s, f, _ = PLAN[("w", l, b)]
                        pe.wait_ge(ev_s, i * SLOTS + W_CHUNKS * l + b + 1)
                        w_chunk(l, b, s, i * 16 + 16 * f)

                def w_next(n):
                    pe.wait_ge(ev_s, W_CHUNKS * l + n + 1)
                    w_chunk(l, n, *slot_of(("w", l, n)))

                for n in range(LOOPED, 16):
                    w_next(n)
                pe.wait_ge(cv_s, CV0 + (l + 1) * CT * CONF_TAPS)
                for k in range(CT):
                    last = mm(ps[:, 2, 0:SEQ], ones[:, :], cacc[:, k, :], start=(k == 0), stop=(k == CT - 1))
                last.then_inc(cm_s, 1)
                w_next(16)
                w_next(17)
                w_next(18)
                if l == 0:
                    for q in range(ADA_FIRST // 2, ADA_CHUNKS // 2):
                        ada_transpose(0, q)
                    pe.wait_ge(ared_s, ADA_CHUNKS // 2)
                pe.wait_ge(xsil_s, 3 * (l + 1))
                for t in range(TT):
                    for q in range(2):
                        for m in range(4):
                            last = nc.tensor.transpose(ps[:, 3 + 2 * t + q, m * P:(m + 1) * P],
                                                       xc[:, 4 * q + m, t * P:(t + 1) * P], ident[:, :])
                        last.then_inc(xst_s, 1)
                for g in range(GROUPS):
                    last = nc.tensor.transpose(ps[:, 7, g * P:(g + 1) * P], xc[:, 8 + g, 0:P], ident[:, :])
                last.then_inc(xst_s, 1)
                pe.wait_ge(dt_s, l + 1)
                pe.wait_ge(cx_s, l + 1)
                for cc in range(TT):
                    mm(ps[:, 2, 336 + cc * HEADS_S:336 + (cc + 1) * HEADS_S], triu[:, :], dts[:, 4, cc, :],
                       start=True, stop=True)
                mm(ps[:, 2, 368:384], ones[:, :], dts[:, 4, 0, :], start=True, stop=True).then_inc(ac_s, 1)
                w_next(19)
                pe.wait_ge(csq_s, l + 1)
                pe.wait_ge(acs_s, l + 1)
                for k in range(CT):
                    last = mm(ps[:, 2, 0:SEQ], ones[:, :], csq[:, k, :], start=(k == 0), stop=(k == CT - 1))
                last.then_inc(cvar_s, 1)
                for i in range(12):
                    w_next(20 + i)
                    if i == 0:
                        pe.wait_ge(xse_s, 5 * (l + 1))
                        for g in range(GROUPS):
                            for cc in range(TT):
                                last = mm(ps[:, 7, (2 * g + cc) * P:(2 * g + cc + 1) * P],
                                          xc[:, 8 + g, cc * P:(cc + 1) * P], xc[:, 10 + g, cc * P:(cc + 1) * P],
                                          start=True, stop=True)
                        last.then_inc(cb_s, 1)
                        pe.wait_ge(ev_s, 2 + W_CHUNKS * l + 20)
                        for t in range(TT):
                            for m in range(4):
                                last = nc.tensor.transpose(ps[:, 5 + t, m * P:(m + 1) * P],
                                                           proj[:, V + m, t * P:(t + 1) * P], ident[:, :])
                            last.then_inc(vt_s, 1)
                    if 1 <= i <= 4:
                        if i == 1:
                            pe.wait_ge(vtm_s, 2 * (l + 1))
                            pe.wait_ge(cbm_s, l + 1)
                        for h in (2 * i - 2, 2 * i - 1):
                            probs_transpose(l, h)
                    if i < 4:
                        for h in (2 * i, 2 * i + 1):
                            scores(l, h)
                    if 1 <= i <= 4:
                        for h in (2 * i - 2, 2 * i - 1):
                            pv(l, h)
                    if i == 4:
                        pe.wait_ge(xd_s, l + 1)
                        for g in range(GROUPS):
                            mm(ps[:, 5 + g, :], b_tm[:, g, :], xdtd[:, g * 512:(g + 1) * 512],
                               start=True, stop=True).then_inc(stt_s, 1)
                        acum_bcast(l, 0)
                    if i >= 5:
                        if i == 5:
                            pe.wait_ge(prev_s, 2 * (l + 1))
                        acum_bcast(l, i - 4)
                        y_batch(l, i - 5)
                y_batch(l, 7)
                pe.wait_ge(cu_s, l + 1)
                pe.wait_ge(ev_s, 2 + W_CHUNKS * (l + 1))
                for idx in range(4):
                    s, n = slot_of(("conf", l, idx // 2))
                    pe.wait_ge(full[s], n)
                    out_pair(l, idx, s, half, CT, 2 * (idx % 2), cacc)
                pe.wait_ge(gsq_s, 2 * (l + 1))
                for g in range(GROUPS):
                    for k in range(4):
                        last = mm(ps[:, 7, g * SEQ:(g + 1) * SEQ], ones[:, :], ysq[:, 4 * g + k, :],
                                  start=(k == 0), stop=(k == 3))
                last.then_inc(gst_s, 1)
                for idx in range(4):
                    s, n = slot_of(("attn", l, idx // 2))
                    pe.wait_ge(full[s], n)
                    out_pair(l, 4 + idx, s, half, 4, 2 * (idx % 2), ao)
                pe.wait_ge(gn_s, l + 1)
                for idx in range(4):
                    s, n = slot_of(("ssm", l, idx))
                    pe.wait_ge(full[s], n)
                    out_pair(l, 8 + idx, s, wide, KT, 0, proj[:, Z:Z + 8, :])
                pe.wait_ge(mg_s, 16 * l + 12)
                for idx in range(4):
                    s, n = slot_of(("mix", l, idx))
                    pe.wait_ge(full[s], n)
                    out_pair(l, 12 + idx, s, wide, KT, 0, merged)
                norm_sums(2 * l + 1)
                if l == 0:
                    for g in range(GD):
                        gs, gn = slot_of(("g", 0, g))
                        us, un = slot_of(("u", 0, g))
                        pe.wait_ge(full[gs], gn)
                        pe.wait_ge(full[us], un)
                        for j in range(2):
                            pe.wait_ge(hm_s, 2 * g + j + 1)
                            gate_up(gs, us, j, hT, SEQ, g == 0 and j == 0)
                        if g:
                            dsl, dn = slot_of(("d", 0, g - 1))
                            pe.wait_ge(full[dsl], dn)
                            pe.wait_ge(hm_s, HM0 + 2 * g)
                            down(dsl, (g - 1) % 2, SEQ, g == 1, False)
                    dsl, dn = slot_of(("d", 0, GD - 1))
                    pe.wait_ge(full[dsl], dn)
                    pe.wait_ge(hm_s, HM0 + 2 * GD)
                    down(dsl, (GD - 1) % 2, SEQ, False, True)
                    pe.wait_ge(ye_s, 1)
                    for m in range(KT):
                        pe.wait_ge(cf_s, m + 1)
                        for t in range(TT):
                            last = nc.tensor.transpose(ps[:, 6 + m % 2, t * P:(t + 1) * P],
                                                       ysb[:, t, m * P:(m + 1) * P], ident[:, :])
                        last.then_inc(c_s, 1)
                    for q in range(ADA_CHUNKS // 2):
                        ada_transpose(1, q)

            pe.wait_ge(h_s, 4 * KT)
            for t in range(TT):
                for m in range(KT):
                    last = nc.tensor.transpose(ps[:, 2 + 2 * t + m // 4, (m % 4) * P:(m % 4 + 1) * P],
                                               hT[:, m, t * P:(t + 1) * P], ident[:, :])
                last.then_inc(htr_s, 1)
            for t in range(TT):
                for k in range(KT):
                    last = mm(ps[:, 0, t * EXPERTS:(t + 1) * EXPERTS], hT[:, k, t * P:(t + 1) * P], rw[:, k, :],
                              start=(k == 0), stop=(k == KT - 1))
            last.then_inc(lg_s, 1)
            pe.wait_ge(mk_s, 1)
            mask = rt[:, 12, :, :]
            mm(ps[:, 1, 0:8], striu[:, :], mask[:, 0, :], start=True, stop=True)
            mm(ps[:, 1, 8:16], ones[:, :], mask[:, 0, :], start=True, stop=False)
            mm(ps[:, 1, 8:16], striu[:, :], mask[:, 1, :], start=False, stop=True)
            mm(ps[:, 1, 16:24], ones[:, :], mask[:, 0, :], start=True, stop=False)
            mm(ps[:, 1, 16:24], ones[:, :], mask[:, 1, :], start=False, stop=True).then_inc(cum_s, 1)

            C_BASE, PER = KT, 1 + 2 * KT

            def gather(free_at):
                for m in range(KT):
                    pe.wait_ge(cf_s, free_at + m)
                    for t in range(TT):
                        last = mm(ps[:, 6 + (m + 1) % 2, 0:SEQ], h_tm[:, t, m * P:(m + 1) * P], p_m[:, t, :],
                                  start=(t == 0), stop=(t == TT - 1))
                    last.then_inc(c_s, 1)

            pe.wait_ge(htm_s, TT)
            pe.wait_ge(p_s, 1)
            gather(CF0 + C_BASE - 1)
            pe.wait_ge(rk_s, 2)
            C1 = C_BASE + KT
            with pe.Fori(0, EXPERTS) as e:
                count = pe.value_load(cnt[0:1, ds(e, 1)], min_val=0, max_val=SEQ)
                pe.wait_ge(xg_s, e + 1)
                pe.wait_ge(ye_s, e + 1)

                def small_expert():
                    def group(gi, b, tiles):
                        pe.wait_ge(full[b], gi * 16 + 16 * FILLS[b] + 16)
                        pe.wait_ge(full[2 + b], gi * 16 + 16 * FILLS[2 + b] + 16)
                        pe.wait_ge(hm_s, tiles)
                        for w, c0 in ((b, 0), (2 + b, P)):
                            for k in range(KT):
                                for j in range(2):
                                    last = mm(ps[HALF * j:HALF * (j + 1), b, c0:c0 + P], xg[:, k, 0:HALF],
                                              wide(w)[:, k, j * P:(j + 1) * P], start=(k == 0), stop=(k == KT - 1))
                            last.then_inc(gu_s, 1)

                    def group_down(gi, b, tiles, groups, first, stop):
                        pe.wait_ge(hm_s, tiles + HM0)
                        nc.tensor.transpose(ps[:, 4 + b, 0:P], hsm[:, b, :], ident[:, :]).then_inc(ht_s, 1)
                        pe.wait_ge(full[4 + b], gi * 16 + 16 * FILLS[4 + b] + 16)
                        pe.wait_ge(hte_s, groups)
                        for j in range(2):
                            for hf in range(2):
                                last = mm(ps[HALF * hf:HALF * (hf + 1), 2, :], hm[:, b, 0, HALF * j:HALF * (j + 1)],
                                          rows2(4 + b)[:, j, hf * 512:(hf + 1) * 512],
                                          start=(first and j == 0), stop=(stop and j == 1))
                        last.then_inc(dn_s, 1)

                    T0 = e * (2 * GE) + 2 * GD
                    G0 = e * GE
                    half_e = e * (GE // 2)
                    group(half_e, 0, T0)
                    group(half_e, 1, T0 + 2)
                    prepare(HALF)
                    group_down(half_e, 0, T0 + 2, G0 + 1, True, False)
                    with pe.Fori(1, GE // 2) as i:
                        for b in range(2):
                            group(half_e + i, b, T0 + i * 4 + 2 * b)
                            if b == 0:
                                group_down(half_e + i - 1, 1, T0 + i * 4, G0 + i * 2, False, False)
                            else:
                                group_down(half_e + i, 0, T0 + i * 4 + 2, G0 + i * 2 + 1, False, False)
                    group_down(half_e + GE // 2 - 1, 1, T0 + 2 * GE, G0 + GE, False, True)

                def expert(n):
                    if n == HALF:
                        small_expert()
                    else:
                        large_expert(n)
                        pe.sem_inc(ht_s, GE)
                    merge(n)

                def large_expert(n):
                    def group(gi, b, wait_tiles):
                        pe.wait_ge(full[b], gi * 16 + 16 * FILLS[b] + 16)
                        pe.wait_ge(full[2 + b], gi * 16 + 16 * FILLS[2 + b] + 16)
                        for j in range(2):
                            pe.wait_ge(hm_s, wait_tiles + j + 1)
                            gate_up(b, 2 + b, j, xg, n)

                    def group_down(gi, b, tiles, first, stop):
                        pe.wait_ge(full[4 + b], gi * 16 + 16 * FILLS[4 + b] + 16)
                        pe.wait_ge(hm_s, tiles + HM0)
                        down(4 + b, b, n, first, stop)

                    T0 = e * (2 * GE) + 2 * GD
                    half_e = e * (GE // 2)
                    group(half_e, 0, T0)
                    group(half_e, 1, T0 + 2)
                    prepare(n)
                    group_down(half_e, 0, T0 + 2, True, False)
                    with pe.Fori(1, GE // 2) as i:
                        for b in range(2):
                            group(half_e + i, b, T0 + i * 4 + 2 * b)
                            if b == 0:
                                group_down(half_e + i - 1, 1, T0 + i * 4, False, False)
                            else:
                                group_down(half_e + i, 0, T0 + i * 4 + 2, False, False)
                    group_down(half_e + GE // 2 - 1, 1, T0 + 2 * GE, False, True)

                def prepare(n):
                    slot_tiles = (n + P - 1) // P
                    pe.wait_ge(pg_s, e + 1)
                    pe.wait_ge(cf_s, e * PER + CF0 + C1)
                    for st in range(slot_tiles):
                        for t in range(TT):
                            last = nc.tensor.transpose(ps[:, 6, st * SEQ + t * P:st * SEQ + (t + 1) * P],
                                                       pg_m[:, t, st * P:(st + 1) * P], ident[:, :])
                    last.then_inc(c_s, 1)
                    pe.wait_ge(p_s, e + 2)
                    gather(e * PER + CF0 + C1)

                def merge(n):
                    slot_tiles = (n + P - 1) // P
                    pe.wait_ge(ye_s, e + 2)
                    for m in range(KT):
                        pe.wait_ge(cf_s, e * PER + CF0 + C1 + KT + m)
                        for st in range(slot_tiles):
                            rows = min(P, n - st * P)
                            last = mm(ps[:, 6 + (m + 1) % 2, 0:SEQ], ysb[0:rows, st, m * P:(m + 1) * P],
                                      pgT[0:rows, st, :], start=(st == 0), stop=(st == slot_tiles - 1))
                        last.then_inc(c_s, 1)

                by_size(pe, count, expert)

            norm_sums(2 * DEPTH)
            pe.wait_ge(h_s, (2 * DEPTH + 1) * KT)
            for t in range(TT):
                for m in range(KT):
                    last = nc.tensor.transpose(ps[:, 4 + 2 * t + m // 4, (m % 4) * P:(m % 4 + 1) * P],
                                               hT[:, m, t * P:(t + 1) * P], ident[:, :])
                    if m % 4 == 3:
                        last.then_inc(fin_s, 1)

        @block.scalar
        def _(act):
            a_ = nc.scalar.activation
            steps = [0]

            def then_wait(ins):
                steps[0] += 1
                ins.then_inc(ast, 1)
                act.wait_ge(ast, steps[0])

            for l in range(DEPTH):
                for dst, src in param_loads(l):
                    act.dma_start(dst, src).then_inc(par_s[l], 16)
            act.wait_ge(pcol_s, 1)
            a_(ccol[:, :], pcol[:, 0, R_C:R_C + KT], ACT.Silu).then_inc(ccol_s, 1)

            def norm(ni):
                act.wait_ge(x_s, ni + 1)
                a_(sq[:, :, :], xT[:, :, :], ACT.Square).then_inc(sq_s, 1)
                act.wait_ge(var_s, ni + 1)
                a_(rs[:, 1, :], rs[:, 0, :], ACT.Sqrt).then_inc(sd_s, 1)

            def shift(ni, factor, shift_cols):
                for m in range(KT):
                    act.wait_ge(nx_s, KT * ni + m + 1)
                    a_(hT[:, m, :], sq[:, m, :], ACT.Identity, bias=shift_cols[:, m:m + 1],
                       scale=factor[:, m:m + 1]).then_inc(h_s, 1)

            def evac(l, n):
                act.wait_ge(proj_s, W_CHUNKS * l + n + 1)
                a_(proj[:, 2 * n:2 * n + 2, :], ps[:, n % 2, :].rearrange("p (a b) -> p a b", a=2),
                   ACT.Copy).then_inc(ev_s, 1)

            def evac_y(n):
                if n == HALF:
                    for hf in range(2):
                        last = a_(ysb[0:HALF, 0, hf * 512:(hf + 1) * 512], ps[HALF * hf:HALF * (hf + 1), 2, :], ACT.Copy)
                    last.then_inc(ye_s, 1)
                    return
                for t in range((n + P - 1) // P):
                    rows = min(P, n - t * P)
                    for hf in range(2):
                        src = ps[0:rows, 2 + 2 * t + hf, :] if rows > HALF else ps[HALF * hf:HALF * hf + rows, 4, :]
                        last = a_(ysb[0:rows, t, hf * 512:(hf + 1) * 512], src, ACT.Copy)
                last.then_inc(ye_s, 1)

            for l in range(DEPTH):
                norm(2 * l)
                shift(2 * l, acolw[:, 0, :], modc[:, 0:KT])
                act.wait_ge(dtin_s, l + 1)
                a_(dts[:, 1, :, :], dts[:, 1, :, :], ACT.Exp, scale=-1.0).then_inc(dtexp_s, 1)
                a_(alog[:, l, :], alog[:, l, :], ACT.Exp).then_inc(dtexp_s, 1)
                act.wait_ge(dtexp_s, 2 * l + 2)
                a_(dts[:, 2, :, :], dts[:, 1, :, :], ACT.Ln, bias=1.0).then_inc(dtln_s, 1)
                for n in range(4):
                    evac(l, n)
                act.wait_ge(ev_s, 2 + W_CHUNKS * l + 4)
                a_(proj[:, GLU:GLU + CT, :], proj[:, GLU:GLU + CT, :], ACT.Sigmoid).then_inc(sig_s, 1)
                for n in range(4, 17):
                    evac(l, n)
                for q in range(3):
                    act.wait_ge(xv_s, 3 * l + q + 1)
                    a_(xc[:, 4 * q:4 * q + 4, :], xc[:, 4 * q:4 * q + 4, :], ACT.Silu).then_inc(xsil_s, 1)
                evac(l, 17)
                a_(proj[:, Z:Z + 8, :], proj[:, Z:Z + 8, :], ACT.Silu).then_inc(zs_s, 1)
                act.wait_ge(cx_s, l + 1)
                a_(csq[:, :, :], cacc[:, :, :], ACT.Square).then_inc(csq_s, 1)
                evac(l, 18)
                for q in range(4):
                    act.wait_ge(xst_s, 5 * l + q + 1)
                    a_(xs_tm[:, q // 2, (q % 2) * 512:(q % 2 + 1) * 512], ps[:, 3 + q, :],
                       ACT.Copy).then_inc(xse_s, 1)
                act.wait_ge(xst_s, 5 * l + 5)
                a_(b_tm[:, :, :], ps[:, 7, 0:SEQ].rearrange("p (a b) -> p a b", a=2), ACT.Copy).then_inc(xse_s, 1)
                act.wait_ge(acs_s, l + 1)
                a_(dec[:, 1, :], dec[:, 0, :], ACT.Exp).then_inc(dcy_s, 1)
                evac(l, 19)
                act.wait_ge(cvr_s, l + 1)
                a_(rs[:, 1, :], rs[:, 0, :], ACT.Sqrt).then_inc(csd_s, 1)
                act.wait_ge(cn_s, l + 1)
                for m in range(CT):
                    last = a_(cacc[:, m, :], cacc[:, m, :], ACT.Silu, bias=pcol[:, l, R_LB + m:R_LB + m + 1],
                              scale=pcol[:, l, R_LW + m:R_LW + m + 1])
                last.then_inc(cu_s, 1)

                def lmat_exp(k):
                    act.wait_ge(seg_s, 8 * l + k + 1)
                    if k % 2:
                        a_(cdec[:, :, :], ps[:, 3 + k % 2, :].rearrange("p (a b) -> p a b", a=4), ACT.Exp)
                    a_(seg[:, k % 2, :, :], seg[:, k % 2, :, :], ACT.Exp).then_inc(ls_s, 1)

                for i in range(12):
                    if 1 <= i <= 4:
                        for h in (2 * i - 2, 2 * i - 1):
                            b = h % 2
                            act.wait_ge(mx_s, HEADS_A * l + h + 1)
                            a_(sc[:, b, 0:P], sc[:, b, 0:P], ACT.Exp, bias=smx[:, b, 1, 0:1], accum_out=smx[:, b, 2, 0:1])
                            a_(sc[:, b, P:384], sc[:, b, P:384], ACT.Exp, bias=smx[:, b, 1, 1:2],
                               accum_out=smx[:, b, 2, 1:2]).then_inc(ex_s, 1)
                    if i >= 5:
                        lmat_exp(i - 5)
                    evac(l, 20 + i)
                    if i == 0:
                        for t in range(TT):
                            act.wait_ge(vt_s, 2 * l + t + 1)
                            a_(v_tm[:, t, :], ps[:, 5 + t, :], ACT.Copy).then_inc(vtm_s, 1)
                    if 1 <= i <= 4:
                        for h in (2 * i - 2, 2 * i - 1):
                            act.wait_ge(ptr_s, HEADS_A * l + h + 1)
                            a_(pT[:, h % 2, :], ps[:, 5 + h % 2, 0:384], ACT.Copy).then_inc(pte_s, 1)
                    if i == 4:
                        for g in range(GROUPS):
                            act.wait_ge(stt_s, 2 * l + g + 1)
                            a_(prev[:, g, :], ps[:, 5 + g, :], ACT.Copy).then_inc(prev_s, 1)
                lmat_exp(7)
                act.wait_ge(ev_s, 2 + W_CHUNKS * (l + 1))
                for g in range(3):
                    a_(proj[:, GATE + 8 * g:GATE + 8 * g + 8, :], proj[:, GATE + 8 * g:GATE + 8 * g + 8, :],
                       ACT.Sigmoid).then_inc(gate_s, 1)
                for g in range(GROUPS):
                    act.wait_ge(yz_s, 4 * l + 2 * g + 2)
                    a_(ysq[:, 4 * g:4 * g + 4, :], proj[:, Z + 4 * g:Z + 4 * g + 4, :], ACT.Square).then_inc(gsq_s, 1)
                act.wait_ge(gv_s, l + 1)
                a_(gr[:, 1, :, :], gr[:, 0, :, :], ACT.Sqrt).then_inc(gsd_s, 1)
                norm(2 * l + 1)
                shift(2 * l + 1, acolw[:, 1, :], modc[:, 24:32])
                if l == 0:
                    for T in range(2 * GD):
                        act.wait_ge(gu_s, T + 1)
                        a_(sil[:, T % 2, :], ps[:, T % 2, 0:SEQ], ACT.Silu).then_inc(sil_s, 1)
                    act.wait_ge(dn_s, DN0 + GD)
                    evac_y(SEQ)

            for t in range(TT):
                act.wait_ge(htr_s, t + 1)
                for hf in range(2):
                    last = a_(h_tm[:, t, hf * 512:(hf + 1) * 512], ps[:, 2 + 2 * t + hf, :], ACT.Copy)
                last.then_inc(htm_s, 1)
            act.wait_ge(re_s, 1)
            a_(rt[:, 8, :, 1:2], rt[:, 8, :, 0:1], ACT.Exp).then_inc(rx_s, 1)
            act.wait_ge(rk_s, 2)
            with act.Fori(0, EXPERTS) as e:
                count = act.value_load(cnt[0:1, ds(e, 1)], min_val=0, max_val=SEQ)

                def expert(n):
                    if n == HALF:
                        with act.Fori(0, GE // 2) as i:
                            for b in range(2):
                                act.wait_ge(gu_s, e * (2 * GE) + i * 4 + 2 * GD + 2 * b + 2)
                                for j in range(2):
                                    a_(sil[:, b, HALF * j:HALF * (j + 1)], ps[:, b, HALF * j:HALF * (j + 1)],
                                       ACT.Silu).then_inc(sil_s, 1)
                        act.wait_ge(dn_s, e * GE + DN0 + GD + GE)
                        evac_y(n)
                        return
                    with act.Fori(0, GE) as i:
                        for j in range(2):
                            act.wait_ge(gu_s, e * (2 * GE) + i * 2 + 2 * GD + j + 1)
                            a_(sil[:, j, 0:n], ps[:, j, 0:n], ACT.Silu).then_inc(sil_s, 1)
                    act.wait_ge(dn_s, e * GE + DN0 + GD + GE)
                    evac_y(n)

                by_size(act, count, expert)
            norm(2 * DEPTH)
            for m in range(KT):
                act.wait_ge(nx_s, KT * 2 * DEPTH + m + 1)
                a_(hT[:, m, :], sq[:, m, :], ACT.Copy, scale=pcol[:, 0, R_FN + m:R_FN + m + 1]).then_inc(h_s, 1)
            for q in range(2 * TT):
                act.wait_ge(fin_s, q + 1)
                a_(o_tm[:, q // 2, (q % 2) * 512:(q % 2 + 1) * 512], ps[:, 4 + q, :], ACT.Copy).then_inc(o_s, 1)

        @block.vector
        def _(dve):
            v = nc.vector
            steps = [0]

            def then_wait(ins):
                steps[0] += 1
                ins.then_inc(vst, 1)
                dve.wait_ge(vst, steps[0])

            for s, n in ((ev_s, 2), (cv_s, CV0), (hm_s, HM0), (dn_s, DN0), (cf_s, CF0)):
                dve.sem_inc(s, n)
            v.memset(key9[:, :, EXPERTS:EXPERTS + 1], -1.0)
            v.memset(gate9[:, :, EXPERTS:EXPERTS + 1], 0.0)
            then_wait(v.memset(cntf[:, :], 0.0))

            dve.wait_ge(xtr_s, 1)
            for b in range(4):
                last = v.tensor_copy(xT[:, 2 * b:2 * b + 2, :], ps[:, b, :].rearrange("p (a b) -> p a b", a=2))
            last.then_inc(x_s, 1)
            for l in range(DEPTH):
                dve.wait_ge(prow_s, l + 1)
                v.tensor_copy(pcol[:, l, :], ps[:, 4 + l, 0:ROWS])
                v.tensor_copy(cwcol[:, l, :], ps[:, 4 + l, 128:128 + CONF_TAPS * CT])
                v.tensor_copy(swcol[:, l, :], ps[:, 4 + l, 256:256 + SSM_TAPS * XT]).then_inc(pcol_s, 1)
                dve.wait_ge(par_s[l], 16 * N_PARAMS[l])
                for hh in range(2):
                    p0 = DH * hh
                    v.tensor_copy(dcol[p0:p0 + DH, l, :], dall[p0:p0 + DH, l, hh:HEADS_S:2])
            dve.wait_ge(ccol_s, 1)

            def bc(ap, n):
                return ap.unsqueeze(1).broadcast_to([P, n, ap.shape[-1]])

            def ada_chunk(l, a):
                n = ADA_CHUNKS * l + a
                dve.wait_ge(afull[n % ADA_SLOTS], 16 * (n // ADA_SLOTS + 1))
                w = aring[:, n % ADA_SLOTS, :].rearrange("p (k n) -> p k n", k=KT)
                then_wait(v.tensor_scalar(aacc[:, a, :], w[:, 0, :], ccol[:, 0:1], None, ALU.mult))
                for k in range(1, KT):
                    ins = v.scalar_tensor_tensor(aacc[:, a, :], w[:, k, :], ccol[:, k:k + 1], aacc[:, a, :],
                                                 ALU.mult, ALU.add)
                    if k < KT - 1:
                        then_wait(ins)
                ins.then_inc(aacc_s, 1)

            def modulation(l, q0, q1):
                for q in range(q0, q1):
                    dve.wait_ge(atr_s, ADA_CHUNKS // 2 * l + q + 1)
                    v.tensor_reduce(modc[:, 4 * q:4 * q + 4], ps[:, 3 + q % 2, :].rearrange("p (a b) -> p a b", a=4),
                                    AX.X, ALU.add).then_inc(ared_s, 1)
                dve.wait_ge(ared_s, ADA_CHUNKS // 2 * l + q1)
                c0, c1 = 4 * q0, 4 * q1
                then_wait(v.tensor_tensor(modc[:, c0:c1], modc[:, c0:c1], pcol[:, l, R_ADA + c0:R_ADA + c1], ALU.add))

            def factor(l, part):
                s0, w0 = (8, R_N1) if part == 0 else (32, R_N2)
                then_wait(v.scalar_tensor_tensor(acolw[:, part, :], modc[:, s0:s0 + KT], 1.0,
                                                 pcol[:, l, w0:w0 + KT], ALU.add, ALU.mult))

            def rms(ni):
                dve.wait_ge(st_s, ni + 1)
                v.tensor_scalar(rs[:, 0, :], ps[:, 2, 0:SEQ], 1.0 / D_MODEL, EPS, ALU.mult, ALU.add).then_inc(var_s, 1)
                dve.wait_ge(sd_s, ni + 1)
                then_wait(v.reciprocal(rs[:, 2, :], rs[:, 1, :]))
                for m in range(KT):
                    v.tensor_tensor(sq[:, m, :], xT[:, m, :], rs[:, 2, :], ALU.mult).then_inc(nx_s, 1)

            def head_scores(l, h):
                b, n = h % 2, HEADS_A * l + h
                dve.wait_ge(sc_s, n + 1)
                if n >= 2:
                    dve.wait_ge(ptr_s, n - 1)
                v.scalar_tensor_tensor(sc[:, b, :], ps[:, 3 + b, 0:384], DH ** -0.5, amask[:, :],
                                       ALU.mult, ALU.add).then_inc(msk_s, 1)
                dve.wait_ge(msk_s, n + 1)
                v.reduce_max(smx[:, b, 0, 0:1], sc[:, b, 0:P], AX.X)
                then_wait(v.reduce_max(smx[:, b, 0, 1:2], sc[:, b, P:384], AX.X))
                v.tensor_scalar(smx[:, b, 1, :], smx[:, b, 0, :], -1.0, None, ALU.mult).then_inc(mx_s, 1)

            def head_probs(l, h):
                b, n = h % 2, HEADS_A * l + h
                dve.wait_ge(ex_s, n + 1)
                then_wait(v.reciprocal(smx[:, b, 3, :], smx[:, b, 2, :]))
                v.tensor_scalar(sc[:, b, 0:P], sc[:, b, 0:P], smx[:, b, 3, 0:1], None, ALU.mult)
                v.tensor_scalar(sc[:, b, P:384], sc[:, b, P:384], smx[:, b, 3, 1:2], None, ALU.mult).then_inc(pr_s, 1)

            def seg_of(l, k):
                hb, cc = k // 2, k % 2
                dve.wait_ge(bc_s, 8 * l + k + 1)
                if 8 * l + k >= 2:
                    dve.wait_ge(y_s, 8 * l + k - 1)
                for r in range(4):
                    last = v.tensor_scalar(seg[:, k % 2, r, :], ps[:, 3 + k % 2, r * P:(r + 1) * P],
                                           acum[:, cc, 4 * hb + r:4 * hb + r + 1], 0.0, ALU.subtract, ALU.min)
                last.then_inc(seg_s, 1)

            def lmat(l, k):
                hb, cc = k // 2, k % 2
                dve.wait_ge(ls_s, 8 * l + k + 1)
                if cc:
                    v.tensor_tensor(cdec[:, :, :], cdec[:, :, :], bc(xc[:, 10 + hb // 2, P:SEQ], 4), ALU.mult)
                v.tensor_tensor(seg[:, k % 2, :, :], seg[:, k % 2, :, :], bc(cbm[:, hb // 2, cc, :], 4),
                                ALU.mult).then_inc(lm_s, 1)

            def y_out(l, hb):
                dve.wait_ge(y_s, 8 * l + 2 * hb + 2)
                for j in range(2):
                    m = 2 * hb + j
                    last = v.scalar_tensor_tensor(xc[:, m, :], xc[:, m, :], dcol[:, l, m:m + 1],
                                                  ps[:, 5 + hb % 2, j * SEQ:(j + 1) * SEQ], ALU.mult, ALU.add)
                then_wait(last)
                z = proj[:, Z + 2 * hb:Z + 2 * hb + 2, :]
                v.tensor_tensor(z, xc[:, 2 * hb:2 * hb + 2, :], z, ALU.mult).then_inc(yz_s, 1)

            def residual(l, idx, first_col):
                for j in range(2):
                    m = 2 * idx + j
                    last = v.scalar_tensor_tensor(xT[:, m, :], ps[:, idx % 2, j * SEQ:(j + 1) * SEQ],
                                                  modc[:, first_col + m:first_col + m + 1], xT[:, m, :],
                                                  ALU.mult, ALU.add)
                return last

            for l in range(DEPTH):
                if l == 0:
                    for a in range(ADA_FIRST):
                        ada_chunk(0, a)
                    modulation(0, 0, ADA_FIRST // 2)
                factor(l, 0)
                rms(2 * l)
                dve.wait_ge(dtmm_s, l + 1)
                then_wait(v.tensor_tensor(dts[:, 0, :, :], ps[:, 2, 256:288].rearrange("p (a b) -> p a b", a=2),
                                          bc(dtb[:, l, :], TT), ALU.add))
                then_wait(v.tensor_scalar(dts[:, 3, :, :], dts[:, 0, :, :], -1.0, None, ALU.mult))
                v.tensor_tensor(dts[:, 1, :, :], dts[:, 0, :, :], dts[:, 3, :, :], ALU.max).then_inc(dtin_s, 1)
                dve.wait_ge(dtln_s, l + 1)
                then_wait(v.scalar_tensor_tensor(dts[:, 3, :, :], dts[:, 0, :, :], 0.0, dts[:, 2, :, :], ALU.max, ALU.add))
                v.scalar_tensor_tensor(dts[:, 4, :, :], dts[:, 3, :, :], -1.0, bc(alog[:, l, :], TT),
                                       ALU.mult, ALU.mult).then_inc(dt_s, 1)
                if l == 0:
                    for a in range(ADA_FIRST, 14):
                        ada_chunk(0, a)
                dve.wait_ge(sig_s, l + 1)
                if l:
                    dve.wait_ge(cvar_s, l)
                    v.memset(cpad[:, :, 0:PADC], 0.0)
                then_wait(v.tensor_tensor(cpad[:, :, PADC:], proj[:, VAL:VAL + CT, :], proj[:, GLU:GLU + CT, :], ALU.mult))
                for m in range(CT):
                    v.tensor_scalar(cacc[:, m, :], cpad[:, m, 0:SEQ], cwcol[:, l, m:m + 1],
                                    pcol[:, l, R_CB + m:R_CB + m + 1], ALU.mult, ALU.add).then_inc(cv_s, 1)
                C0 = CV0 + l * CT * CONF_TAPS
                with dve.Fori(1, CONF_TAPS) as k:
                    for m in range(CT):
                        dve.wait_ge(cv_s, k * CT + C0 + m + 1 - CT)
                        v.scalar_tensor_tensor(cacc[:, m, :], cpad[:, m, ds(k, SEQ)], cwcol[:, l, ds(k * CT + m, 1)],
                                               cacc[:, m, :], ALU.mult, ALU.add).then_inc(cv_s, 1)
                if l == 0:
                    for a in range(14, 21):
                        ada_chunk(0, a)
                for q in range(3):
                    dve.wait_ge(ev_s, 2 + W_CHUNKS * l + XBC // 2 + 2 * q + 2)
                    for tap in range(SSM_TAPS - 1, -1, -1):
                        sh = SSM_TAPS - 1 - tap
                        for m in range(4 * q, 4 * q + 4):
                            w = swcol[:, l, tap * XT + m:tap * XT + m + 1]
                            if sh == 0:
                                last = v.tensor_scalar(xc[:, m, :], proj[:, XBC + m, :], w,
                                                       pcol[:, l, R_SB + m:R_SB + m + 1], ALU.mult, ALU.add)
                            else:
                                last = v.scalar_tensor_tensor(xc[:, m, sh:], proj[:, XBC + m, 0:SEQ - sh], w,
                                                              xc[:, m, sh:], ALU.mult, ALU.add)
                        if sh < SSM_TAPS - 1:
                            then_wait(last)
                    last.then_inc(xv_s, 1)
                dve.wait_ge(cm_s, l + 1)
                then_wait(v.tensor_scalar(rs[:, 2, :], ps[:, 2, 0:SEQ], 1.0 / CONF_WIDTH, None, ALU.mult))
                v.tensor_tensor(cacc[:, :, :], cacc[:, :, :], bc(rs[:, 2, :], CT), ALU.subtract).then_inc(cx_s, 1)
                if l == 0:
                    for a in range(21, ADA_CHUNKS):
                        ada_chunk(0, a)
                    modulation(0, ADA_FIRST // 2, ADA_CHUNKS // 2)
                factor(l, 1)
                dve.wait_ge(ac_s, l + 1)
                then_wait(v.tensor_copy(acum[:, :, :], ps[:, 2, 336:368].rearrange("p (a b) -> p a b", a=2)))
                v.tensor_tensor(dec[:, 0, :], ps[:, 2, 368:384], acum[:, 0, :], ALU.subtract).then_inc(acs_s, 1)
                dve.wait_ge(cvar_s, l + 1)
                v.tensor_scalar(rs[:, 0, :], ps[:, 2, 0:SEQ], 1.0 / CONF_WIDTH, EPS, ALU.mult, ALU.add).then_inc(cvr_s, 1)
                dve.wait_ge(csd_s, l + 1)
                then_wait(v.reciprocal(rs[:, 2, :], rs[:, 1, :]))
                v.tensor_tensor(cacc[:, :, :], cacc[:, :, :], bc(rs[:, 2, :], CT), ALU.mult).then_inc(cn_s, 1)
                dve.wait_ge(cb_s, l + 1)
                v.tensor_tensor(cbm[:, :, :, :].rearrange("p a b c -> p (a b) c"),
                                ps[:, 7, :].rearrange("p (a b) -> p a b", a=4), bc(triu[:, :], 4),
                                ALU.mult).then_inc(cbm_s, 1)
                for i in range(1, 5):
                    for h in (2 * i - 2, 2 * i - 1):
                        head_scores(l, h)
                    for h in (2 * i - 2, 2 * i - 1):
                        head_probs(l, h)
                    if i == 1:
                        for t in range(TT):
                            last = v.tensor_tensor(xdt[:, t, :].rearrange("p (h d) -> p h d", d=DH),
                                                   xs_tm[:, t, :].rearrange("p (h d) -> p h d", d=DH),
                                                   dts[:, 3, t, :].unsqueeze(2).broadcast_to([P, HEADS_S, DH]), ALU.mult)
                        then_wait(last)
                        dve.wait_ge(dcy_s, l + 1)
                        v.tensor_tensor(xdtd.rearrange("p (h d) -> p h d", d=DH),
                                        xdt[:, 0, :].rearrange("p (h d) -> p h d", d=DH),
                                        dec[:, 1, :].unsqueeze(2).broadcast_to([P, HEADS_S, DH]), ALU.mult).then_inc(xd_s, 1)
                    dve.wait_ge(pv_s, HEADS_A * l + 2 * i)
                    v.tensor_copy(ao[:, i - 1, :], ps[:, 7, (i - 1) % 2 * SEQ:(i - 1) % 2 * SEQ + SEQ]).then_inc(ao_s, 1)
                for k in range(8):
                    seg_of(l, k)
                    lmat(l, k)
                    if k >= 2 and k % 2 == 0:
                        y_out(l, k // 2 - 1)
                dve.wait_ge(zs_s, l + 1)
                y_out(l, 3)
                dve.wait_ge(gate_s, 3 * (l + 1))
                for idx in range(4):
                    dve.wait_ge(om_s, 16 * l + idx + 1)
                    v.tensor_tensor(merged[:, 2 * idx:2 * idx + 2, :], ps[:, idx % 2, :].rearrange("p (a b) -> p a b", a=2),
                                    proj[:, GATE + 2 * idx:GATE + 2 * idx + 2, :], ALU.mult).then_inc(mg_s, 1)
                dve.wait_ge(gst_s, l + 1)
                v.tensor_scalar(gr[:, 0, :, :], ps[:, 7, :].rearrange("p (a b) -> p a b", a=2), 1.0 / 512, EPS,
                                ALU.mult, ALU.add).then_inc(gv_s, 1)
                dve.wait_ge(gsd_s, l + 1)
                then_wait(v.reciprocal(gr[:, 2, :, :], gr[:, 1, :, :]))
                for m in range(KT):
                    last = v.scalar_tensor_tensor(proj[:, Z + m, :], proj[:, Z + m, :], pcol[:, l, R_SN + m:R_SN + m + 1],
                                                  gr[:, 2, m // 4, :], ALU.mult, ALU.mult)
                last.then_inc(gn_s, 1)
                for idx, g0 in [(i, GATE + 16) for i in range(4)] + [(i, GATE + 8) for i in range(4)]:
                    n = 4 + idx + (4 if g0 == GATE + 8 else 0)
                    dve.wait_ge(om_s, 16 * l + n + 1)
                    g = proj[:, g0 + 2 * idx:g0 + 2 * idx + 2, :]
                    then_wait(v.tensor_tensor(g, ps[:, idx % 2, :].rearrange("p (a b) -> p a b", a=2), g, ALU.mult))
                    v.tensor_tensor(merged[:, 2 * idx:2 * idx + 2, :], merged[:, 2 * idx:2 * idx + 2, :], g,
                                    ALU.add).then_inc(mg_s, 1)
                for idx in range(4):
                    dve.wait_ge(om_s, 16 * l + 12 + idx + 1)
                    last = residual(l, idx, 16)
                    last.then_inc(mg_s, 1)
                dve.wait_ge(mg_s, 16 * (l + 1))
                dve.sem_inc(x_s, 1)
                rms(2 * l + 1)
                if l == 0:
                    for T in range(2 * GD):
                        g = T // 2
                        dve.wait_ge(sil_s, T + 1)
                        dve.wait_ge(dn_s, g + 1)
                        v.tensor_tensor(hm[:, g % 2, T % 2, :], sil[:, T % 2, :], ps[:, T % 2, SEQ:2 * SEQ],
                                        ALU.mult).then_inc(hm_s, 1)
                        for a in range(ADA_CHUNKS * T // (2 * GD), ADA_CHUNKS * (T + 1) // (2 * GD)):
                            ada_chunk(1, a)
                    for m in range(KT):
                        dve.wait_ge(c_s, m + 1)
                        v.scalar_tensor_tensor(xT[:, m, :], ps[:, 6 + m % 2, 0:SEQ], modc[:, 40 + m:41 + m], xT[:, m, :],
                                               ALU.mult, ALU.add).then_inc(cf_s, 1)
                    dve.wait_ge(cf_s, CF0 + KT)
                    dve.sem_inc(x_s, 1)
                    modulation(1, 0, ADA_CHUNKS // 2)

            R = [rt[:, i, :, :] for i in range(20)]
            dve.wait_ge(lg_s, 1)
            then_wait(v.tensor_tensor(R[0], ps[:, 0, 0:16].rearrange("p (a b) -> p a b", a=2), bc(rb[:, :], TT), ALU.add))
            then_wait(v.tensor_scalar(R[1], bc(slot_f[:, 0:EXPERTS], TT), -1.0, float(EXPERTS), ALU.mult, ALU.add))
            logits = R[0]
            for pick, (m_, mask_) in enumerate(((2, 10), (3, 11))):
                then_wait(v.tensor_reduce(rt[:, m_, :, 0:1], logits, AX.X, ALU.max))
                then_wait(v.tensor_tensor(R[4], logits, rt[:, m_, :, 0:1].broadcast_to([P, TT, EXPERTS]), ALU.is_equal))
                then_wait(v.tensor_tensor(R[5], R[4], R[1], ALU.mult))
                then_wait(v.tensor_reduce(rt[:, 6, :, 0:1], R[5], AX.X, ALU.max))
                then_wait(v.tensor_tensor(R[mask_], R[1], rt[:, 6, :, 0:1].broadcast_to([P, TT, EXPERTS]), ALU.is_equal))
                if pick == 0:
                    then_wait(v.scalar_tensor_tensor(R[7], R[10], NEG, logits, ALU.mult, ALU.add))
                    logits = R[7]
            v.tensor_tensor(R[12], R[10], R[11], ALU.add).then_inc(mk_s, 1)
            v.tensor_tensor(rt[:, 8, :, 0:1], rt[:, 3, :, 0:1], rt[:, 2, :, 0:1], ALU.subtract).then_inc(re_s, 1)
            dve.wait_ge(rx_s, 1)
            then_wait(v.tensor_scalar(rt[:, 8, :, 2:3], rt[:, 8, :, 1:2], 1.0, None, ALU.add))
            then_wait(v.reciprocal(rt[:, 8, :, 3:4], rt[:, 8, :, 2:3]))
            then_wait(v.tensor_tensor(rt[:, 8, :, 4:5], rt[:, 8, :, 1:2], rt[:, 8, :, 3:4], ALU.mult))
            then_wait(v.tensor_tensor(R[13], R[10], rt[:, 8, :, 3:4].broadcast_to([P, TT, EXPERTS]), ALU.mult))
            then_wait(v.tensor_tensor(R[14], R[11], rt[:, 8, :, 4:5].broadcast_to([P, TT, EXPERTS]), ALU.mult))
            then_wait(v.tensor_tensor(gate9[:, :, 0:EXPERTS], R[13], R[14], ALU.add))
            dve.wait_ge(cum_s, 1)
            v.tensor_copy(cntf[0:1, 0:EXPERTS], ps[0:1, 1, 16:24])
            then_wait(v.scalar_tensor_tensor(R[15], ps[:, 1, 0:16].rearrange("p (a b) -> p a b", a=2), 1.0, R[12],
                                             ALU.add, ALU.mult))
            v.tensor_copy(cnt[:, :], cntf[:, :]).then_inc(rk_s, 1)
            v.tensor_scalar(key9[:, :, 0:EXPERTS], R[15], -1.0, None, ALU.add).then_inc(rk_s, 1)
            dve.wait_ge(rk_s, 2)
            for t in range(TT):
                last = v.tensor_scalar(p_m[:, t, :], slot_f[:, :], key9[:, t, 0:1], None, ALU.is_equal)
            last.then_inc(p_s, 1)
            for m in range(KT):
                dve.wait_ge(c_s, KT + m + 1)
                v.tensor_copy(xg[:, m, :], ps[:, 6 + (m + 1) % 2, 0:SEQ]).then_inc(cf_s, 1)
            dve.wait_ge(cf_s, CF0 + 2 * KT)
            dve.sem_inc(xg_s, 1)
            C1, PER = 2 * KT, 1 + 2 * KT
            with dve.Fori(0, EXPERTS) as e:
                count = dve.value_load(cnt[0:1, ds(e, 1)], min_val=0, max_val=SEQ)
                for t in range(TT):
                    v.tensor_scalar(p_m[:, t, :], slot_f[:, :], key9[:, t, ds(e + 1, 1)], None, ALU.is_equal)
                    last = v.tensor_scalar(pg_m[:, t, :], slot_f[:, :], key9[:, t, ds(e, 1)], gate9[:, t, ds(e, 1)],
                                           ALU.is_equal, ALU.mult)
                    if t == 0:
                        continue
                last.then_inc(pg_s, 1)
                dve.wait_ge(pg_s, e + 1)
                dve.sem_inc(p_s, 1)

                def small_hidden():
                    def multiply(b, tiles, groups):
                        dve.wait_ge(dn_s, groups + 1)
                        dve.wait_ge(sil_s, tiles + 2)
                        for j in range(2):
                            v.tensor_tensor(hsm[:, b, HALF * j:HALF * (j + 1)], sil[:, b, HALF * j:HALF * (j + 1)],
                                            ps[:, b, P + HALF * j:P + HALF * (j + 1)], ALU.mult).then_inc(hm_s, 1)

                    def evacuate(b, groups):
                        dve.wait_ge(ht_s, groups)
                        v.tensor_copy(hm[:, b, 0, 0:P], ps[:, 4 + b, 0:P]).then_inc(hte_s, 1)

                    T0 = e * (2 * GE) + 2 * GD
                    G0 = e * GE
                    multiply(0, T0, G0 + GD)
                    multiply(1, T0 + 2, G0 + GD + 1)
                    prepared(HALF)
                    evacuate(0, G0 + 1)
                    with dve.Fori(1, GE // 2) as i:
                        multiply(0, T0 + i * 4, G0 + i * 2 + GD)
                        evacuate(1, G0 + i * 2)
                        multiply(1, T0 + i * 4 + 2, G0 + i * 2 + GD + 1)
                        evacuate(0, G0 + i * 2 + 1)
                    next_tokens()
                    evacuate(1, G0 + GE)

                def expert(n):
                    if n == HALF:
                        small_hidden()
                    else:
                        hidden(n)
                        next_tokens()
                        dve.sem_inc(hte_s, GE)

                def prepared(n):
                    dve.wait_ge(c_s, e * PER + C1 + 1)
                    st = (n + P - 1) // P
                    v.tensor_copy(pgT[:, 0:st, :], ps[:, 6, 0:st * SEQ].rearrange("p (a b) -> p a b", a=st)).then_inc(cf_s, 1)
                    for m in range(KT):
                        dve.wait_ge(c_s, e * PER + C1 + 2 + m)
                        v.tensor_copy(xg_next[:, m, :], ps[:, 6 + (m + 1) % 2, 0:SEQ]).then_inc(cf_s, 1)

                def next_tokens():
                    dve.wait_ge(cf_s, e * PER + CF0 + C1 + 1 + KT)
                    v.tensor_copy(xg[:, :, :], xg_next[:, :, :]).then_inc(xg_s, 1)

                def hidden(n):
                    def multiply(b, downs, tiles):
                        dve.wait_ge(dn_s, downs)
                        for j in range(2):
                            dve.wait_ge(sil_s, tiles + j + 1)
                            v.tensor_tensor(hm[:, b, j, 0:n], sil[:, j, 0:n], ps[:, j, SEQ:SEQ + n],
                                            ALU.mult).then_inc(hm_s, 1)

                    T0 = e * (2 * GE) + 2 * GD
                    for b in range(2):
                        multiply(b, e * GE + GD + b + 1, T0 + 2 * b)
                    prepared(n)
                    with dve.Fori(1, GE // 2) as i:
                        for b in range(2):
                            multiply(b, e * GE + i * 2 + GD + b + 1, T0 + i * 4 + 2 * b)

                by_size(dve, count, expert)
                for m in range(KT):
                    dve.wait_ge(c_s, e * PER + C1 + 2 + KT + m)
                    v.scalar_tensor_tensor(xT[:, m, :], ps[:, 6 + (m + 1) % 2, 0:SEQ], modc[:, 40 + m:41 + m],
                                           xT[:, m, :], ALU.mult, ALU.add).then_inc(cf_s, 1)
            dve.wait_ge(cf_s, CF0 + C1 + PER * EXPERTS)
            dve.sem_inc(x_s, 1)
            rms(2 * DEPTH)


_INS = ['x', 'c', 'norm1_w', 'norm2_w', 'ada_w', 'ada_b', 'w_in', 'conf_conv_w', 'conf_conv_b', 'conf_ln_w',
        'conf_ln_b', 'conf_out', 'ssm_conv_w', 'ssm_conv_b', 'ssm_dt_bias', 'ssm_A_log', 'ssm_D', 'ssm_norm_w',
        'ssm_out', 'attn_out', 'mix_out', 'ffn_w_gate', 'ffn_w_up', 'ffn_w_down', 'moe_router_w', 'moe_router_b',
        'moe_w_gate', 'moe_w_up', 'moe_w_down', 'final_norm_w']


def kernel(**inputs):
    import numpy as np
    import concourse.bacc as bacc
    from concourse.bass_utils import run_bass_kernel_spmd

    nc = bacc.Bacc("TRN2", target_bir_lowering=False, num_devices=1)
    arrays, args = {}, []
    for name in _INS:
        a = np.ascontiguousarray(inputs[name])
        arrays[f"in_{name}"] = a
        args.append(nc.dram_tensor(f"in_{name}", a.shape, mybir.dt.from_np(a.dtype), kind="ExternalInput").ap())
    out = nc.dram_tensor("out_0", (1, SEQ, D_MODEL), mybir.dt.float32, kind="ExternalOutput").ap()
    trunk(nc, *args, out)
    r = run_bass_kernel_spmd(nc, [arrays], core_ids=[0])
    return r.results[0]["out_0"]
```

```python
import concourse.bass as bass
from concourse import mybir
from contextlib import ExitStack

P = 128
D_MODEL, SEQ, DEPTH = 1024, 256, 2
KT = D_MODEL // P
TT = SEQ // P
CONF_WIDTH, CONF_TAPS = 512, 31
CT = CONF_WIDTH // P
HEADS_S, GROUPS = 16, 2
DI = 1024
XT = 12
SSM_TAPS = 4
HEADS_A, DH = 8, 64
IN_WIDTH = 8208
DT_COL = 3584
FFN_DENSE, FFN_EXPERT, EXPERTS = 2816, 3584, 8
EPS = 1e-6
NEG = -1e30
PADC = CONF_TAPS - 1
VAL, GLU, Z, XBC, Q, K, V, GATE = 0, 4, 8, 16, 28, 32, 36, 40
W_CHUNKS = 32
LOOPED = 12
ADA_CHUNKS = 24
ADA_FIRST = 8
SLOTS = 6
ADA_SLOTS = 2
ADA_BANK = (3, 6)
HALF = 64
SIZES = (HALF, 128, 160, 192, 256)
GD, GE = FFN_DENSE // 256, FFN_EXPERT // 256
R_N1, R_N2, R_ADA, R_CB, R_LW, R_LB, R_SB, R_SN, R_FN = 0, 8, 16, 64, 68, 72, 76, 88, 96
ROWS = 104


def ring_plan():
    order = []
    for l in range(DEPTH):
        order += [("w", l, n) for n in range(W_CHUNKS)]
        order += [("conf", l, a) for a in range(2)] + [("attn", l, a) for a in range(2)]
        order += [("ssm", l, a) for a in range(4)] + [("mix", l, a) for a in range(4)]
        if l == 0:
            for g in range(GD):
                order += [("g", 0, g), ("u", 0, g)] + ([("d", 0, g - 1)] if g else [])
            order += [("d", 0, GD - 1)]
    plan, last, fills, nxt = {}, {}, [0] * SLOTS, 0
    for key in order:
        if key[0] in "gud":
            slot = {"g": 0, "u": 2, "d": 4}[key[0]] + key[2] % 2
        else:
            slot, nxt = nxt % SLOTS, nxt + 1
        fills[slot] += 1
        plan[key] = (slot, fills[slot], last.get(slot))
        last[slot] = key
    return order, plan, last, fills


def trunk(nc, x, c, norm1_w, norm2_w, ada_w, ada_b, w_in, conf_conv_w, conf_conv_b, conf_ln_w, conf_ln_b, conf_out,
          ssm_conv_w, ssm_conv_b, ssm_dt_bias, ssm_A_log, ssm_D, ssm_norm_w, ssm_out, attn_out, mix_out,
          ffn_w_gate, ffn_w_up, ffn_w_down, moe_router_w, moe_router_b, moe_w_gate, moe_w_up, moe_w_down,
          final_norm_w, out):
    fp32, i32 = mybir.dt.float32, mybir.dt.int32
    ALU, ACT, AX = mybir.AluOpType, mybir.ActivationFunctionType, mybir.AxisListType
    ds = bass.ds
    ORDER, PLAN, LAST, FILLS = ring_plan()
    moe_w_gate, moe_w_up, moe_w_down = moe_w_gate[0], moe_w_up[0], moe_w_down[0]

    ctx = ExitStack()
    with ctx:
        def sb(name, shape, dt=fp32):
            return ctx.enter_context(nc.sbuf_tensor(name, shape, dt))

        def sem(name):
            return ctx.enter_context(nc.semaphore(name))

        ring = sb("ring", [P, SLOTS, 2048])
        proj = sb("proj", [P, 64, SEQ])
        aring = sb("aring", [P, ADA_SLOTS, 2048])
        xT = sb("xT", [P, KT, SEQ])
        hT = sb("hT", [P, KT, SEQ])
        sq = sb("sq", [P, KT, SEQ])
        xc = sb("xc", [P, XT, SEQ])
        cpad = sb("cpad", [P, CT, PADC + SEQ])
        cacc = sb("cacc", [P, CT, SEQ])
        v_tm = sb("v_tm", [P, TT, 512])
        b_tm = sb("b_tm", [P, GROUPS, P])
        heads = sb("heads", [P, 1536])
        cbm = sb("cbm", [P, GROUPS, TT, P])
        ident = sb("ident", [P, P])
        ones = sb("ones", [P, P])
        triu = sb("triu", [P, P])
        striu = sb("striu", [P, P])
        amask = sb("amask", [P, 384])
        slot_f = sb("slot_f", [P, SEQ])
        pcol = sb("pcol", [P, DEPTH, ROWS])
        cwcol = sb("cwcol", [P, DEPTH, CONF_TAPS * CT])
        swcol = sb("swcol", [P, DEPTH, SSM_TAPS * XT])
        ccol = sb("ccol", [P, KT])
        dcol = sb("dcol", [P, DEPTH, KT])
        dtb = sb("dtb", [P, DEPTH, HEADS_S])
        alog = sb("alog", [P, DEPTH, HEADS_S])
        wdt = sb("wdt", [P, DEPTH, KT, HEADS_S])
        rw = sb("rw", [P, KT, EXPERTS])
        rb = sb("rb", [P, EXPERTS])
        modc = sb("modc", [P, 48])
        modn = sb("modn", [P, 48])
        acolw = sb("acolw", [P, 2, KT])
        rs = sb("rs", [P, 3, SEQ])
        dts = sb("dts", [P, 5, TT, HEADS_S])
        acum = sb("acum", [P, TT, HEADS_S])
        dec = sb("dec", [P, 2, HEADS_S])
        smx = sb("smx", [P, 2, 4, 2])
        key9 = sb("key9", [P, TT, EXPERTS + 1])
        gate9 = sb("gate9", [P, TT, EXPERTS + 1])
        cntf = sb("cntf", [1, EXPERTS + 2])
        cnt = sb("cnt", [1, EXPERTS + 2], i32)
        ps = ctx.enter_context(nc.psum_tensor("ps", [P, 8, 512], fp32))

        x_in = proj[:, 0:8, :].rearrange("p (t a) n -> p t (a n)", t=TT)
        xs_tm = proj[:, XBC:XBC + 8, :].rearrange("p (t a) n -> p t (a n)", t=TT)
        prev = proj[:, XBC + 8:XBC + 12, :].rearrange("p (g a) n -> p g (a n)", g=GROUPS)
        xdt = proj[:, 0:8, :].rearrange("p (t a) n -> p t (a n)", t=TT)
        xdtd = sq[:, 0:4, :].rearrange("p a n -> p (a n)")
        ao = proj[:, V:V + 4, :]
        ysq = proj[:, Q:Q + 8, :]
        merged = hT
        hm = proj[:, 0:4, :].rearrange("p (b j) n -> p b j n", b=2)
        sil = proj[:, 4:6, :]
        hsm = proj[:, 44:46, 0:P]
        pg_m = proj[:, 6:8, :]
        ysb = proj[:, 8:16, :].rearrange("p (t a) n -> p t (a n)", t=TT)
        xg = proj[:, 16:24, :]
        h_tm = proj[:, 24:32, :].rearrange("p (t a) n -> p t (a n)", t=TT)
        p_m = proj[:, 40:42, :]
        pgT = proj[:, 42:44, :]
        o_tm = proj[:, 48:56, :].rearrange("p (t a) n -> p t (a n)", t=TT)
        csq = cpad[:, :, 0:SEQ]
        crow = b_tm[0:KT, 0, :]
        ada_first = ([aring[:, i, :] for i in range(ADA_SLOTS)]
                     + [proj[:, 8 * i:8 * i + 8, :].rearrange("p a n -> p (a n)") for i in range(1, 5)]
                     + [xc[:, 0:8, :].rearrange("p a n -> p (a n)"), aring[:, 0, :]])
        seg = heads[:, 0:1024].rearrange("p (b r n) -> p b r n", b=2, r=4)
        cdec = heads[:, 1024:1536].rearrange("p (r n) -> p r n", r=4)
        sc = heads[:, 0:768].rearrange("p (b n) -> p b n", b=2)
        pT = heads[:, 768:1536].rearrange("p (b n) -> p b n", b=2)
        aacc = proj[:, GATE:GATE + ADA_CHUNKS, :]
        slot_i = sc[:, 0, 0:SEQ].bitcast(i32)
        prow, cwrow, swrow = (v_tm[:, 0:2, 128 * i:128 * i + 128] for i in range(3))
        dall = v_tm[:, 0:2, 384:384 + HEADS_S]
        rt = cdec[:, :, :].rearrange("p a b -> p (a b)")[:, 0:20 * TT * EXPERTS].rearrange(
            "p (i t e) -> p i t e", t=TT, e=EXPERTS)
        gr = xc[:, 0:6, :].rearrange("p (a b) n -> p a b n", a=3)

        full = [sem(f"ring_full{s}") for s in range(SLOTS)]
        x_in_s = sem("x_loaded")
        par_s = [sem(f"params_loaded{l}") for l in range(DEPTH)]
        cst_s = sem("consts_made")
        pcst = sem("pool_step")
        prow_s = sem("param_rows_transposed")
        pcol_s = sem("param_cols_ready")
        ccol_s = sem("c_act_ready")
        xtr_s = sem("x_transposed")
        x_s = sem("x_ready")
        sq_s = sem("norm_squares")
        st_s = sem("norm_sums")
        var_s = sem("norm_var")
        sd_s = sem("norm_sd")
        nx_s = sem("normed_tiles")
        h_s = sem("h_ready")
        c_in_s = sem("c_loaded")
        ctr_s = sem("c_transposed")
        afirst = [sem(f"ada_first_loaded{i}") for i in range(ADA_FIRST)]
        afull = [sem(f"ada_ring_full{s}") for s in range(ADA_SLOTS)]
        aacc_s = sem("ada_partial_ready")
        apool_s = sem("ada_partial_ready_pool")
        pstep = sem("pool_ada_step")
        atr_s = sem("ada_transposed")
        ared_s = sem("ada_reduced")
        mod_s = sem("mod_ready")
        dtmm_s = sem("dt_mm")
        dtin_s = sem("dt_biased")
        dtexp_s = sem("dt_exp")
        dt_s = sem("dt_ready")
        dtln_s = sem("dt_ln")
        proj_s = sem("proj_mm")
        ev_s = sem("proj_evacuated")
        sig_s = sem("glu_sigmoid")
        glu_s = sem("glu_ready")
        cv_s = sem("conf_conv_step")
        cm_s = sem("conf_mean_mm")
        cx_s = sem("conf_centered")
        csq_s = sem("conf_squares")
        cvar_s = sem("conf_var_mm")
        cvr_s = sem("conf_var")
        csd_s = sem("conf_sd")
        cn_s = sem("conf_normed")
        cu_s = sem("conf_u_ready")
        xv_s = sem("xbc_conv")
        xsil_s = sem("xbc_silu")
        zs_s = sem("z_silu")
        vt_s = sem("v_transposed")
        vtm_s = sem("v_tm_ready")
        sc_s = sem("scores_mm")
        msk_s = sem("scores_masked")
        mx_s = sem("scores_max")
        ex_s = sem("scores_exp")
        pr_s = sem("probs_ready")
        ptr_s = sem("probs_transposed")
        pte_s = sem("probs_T_ready")
        pv_s = sem("pv_mm")
        ao_s = sem("attn_ready")
        xst_s = sem("xs_transposed")
        xse_s = sem("xs_tm_ready")
        ac_s = sem("acum_mm")
        acs_s = sem("acum_ready")
        dcy_s = sem("decay_ready")
        cb_s = sem("cb_mm")
        cbm_s = sem("cb_masked")
        xd_s = sem("xdt_ready")
        stt_s = sem("state_mm")
        prev_s = sem("state_ready")
        bc_s = sem("acum_bcast_mm")
        seg_s = sem("seg_ready")
        ls_s = sem("lmat_exp")
        lm_s = sem("lmat_ready")
        y_s = sem("y_mm")
        yz_s = sem("y_gated")
        gsq_s = sem("group_squares")
        gst_s = sem("group_sums")
        gv_s = sem("group_var")
        gsd_s = sem("group_sd")
        gn_s = sem("group_normed")
        gate_s = sem("gates_sigmoid")
        om_s = sem("out_mm")
        mg_s = sem("merge_step")
        htr_s = sem("h_transposed")
        htm_s = sem("h_tm_ready")
        lg_s = sem("logits_mm")
        mk_s = sem("masks_ready")
        re_s = sem("router_exp_in")
        rx_s = sem("router_exp")
        cum_s = sem("slots_mm")
        rk_s = sem("slots_ready")
        p_s = sem("gather_matrix")
        pg_s = sem("scatter_matrix")
        c_s = sem("aux_bank_mm")
        cf_s = sem("aux_bank_free")
        gu_s = sem("gate_up_mm")
        sil_s = sem("silu_ready")
        hm_s = sem("h_mid_ready")
        dn_s = sem("down_mm")
        ht_s = sem("h_small_transposed")
        hte_s = sem("h_small_T_ready")
        ye_s = sem("y_evacuated")
        fin_s = sem("final_transposed")
        o_s = sem("out_ready")
        od_s = sem("out_stored")
        vst = sem("vector_step")
        CV0 = 1
        HM0 = 2
        DN0 = 2
        CF0 = 2

        def released(key):
            kind, l, a = key
            if kind == "w":
                return proj_s, W_CHUNKS * l + a + 1
            if kind == "conf":
                return om_s, 16 * l + 2 * a + 2
            if kind == "attn":
                return om_s, 16 * l + 4 + 2 * a + 2
            if kind == "ssm":
                return om_s, 16 * l + 8 + a + 1
            if kind == "mix":
                return om_s, 16 * l + 12 + a + 1
            if kind in "gu":
                return gu_s, 2 * a + 2
            return dn_s, DN0 + a + 1

        def slot_of(key):
            s, n, _ = PLAN[key]
            return s, 16 * n

        def wide(s):
            return ring[:, s, :].rearrange("p (k n) -> p k n", k=8)

        def half(s):
            return ring[:, s, :].rearrange("p (k n) -> p k n", k=4)

        def rows2(s):
            return ring[:, s, :].rearrange("p (j n) -> p j n", j=2)

        block = ctx.enter_context(nc.Block())

        def by_size(eng, count, body):
            def at(i):
                if i == len(SIZES) - 1:
                    body(SIZES[i])
                    return
                with eng.If(count <= SIZES[i]):
                    body(SIZES[i])
                with eng.Else():
                    at(i + 1)
                    eng.nop()
            at(0)

        @block.sync
        def _(sp):
            def columns(w, col, width):
                return w[:, col:col + width].rearrange("(k p) n -> p k n", p=P)

            sp.dma_start(crow, c[0].rearrange("(m p) -> m p", p=P)).then_inc(c_in_s, 16)
            for a in range(ADA_FIRST):
                if a == 2:
                    sp.dma_start(x_in[:, 0, :], x[0, 0:P, :]).then_inc(x_in_s, 16)
                    sp.dma_start(x_in[:, 1, :], x[0, P:2 * P, :]).then_inc(x_in_s, 16)
                if a == ADA_FIRST - 1:
                    sp.wait_ge(aacc_s, 1)
                sp.dma_start(ada_first[a].rearrange("p (k n) -> p k n", k=KT), columns(ada_w[0], 256 * a, 256)
                             ).then_inc(afirst[a], 16)

            for key in ORDER:
                kind, l, a = key
                s, _, before = PLAN[key]
                if before is not None:
                    sp.wait_ge(*released(before))
                if kind == "w":
                    src, dst = columns(w_in[l], 256 * a + (HEADS_S if 256 * a >= DT_COL else 0), 256), wide(s)
                elif kind == "conf":
                    src, dst = columns(conf_out[l], 512 * a, 512), half(s)
                elif kind == "attn":
                    src, dst = columns(attn_out[l], 512 * a, 512), half(s)
                elif kind == "ssm":
                    src, dst = columns(ssm_out[l], 256 * a, 256), wide(s)
                elif kind == "mix":
                    src, dst = columns(mix_out[l], 256 * a, 256), wide(s)
                elif kind == "g":
                    src, dst = columns(ffn_w_gate[0], 256 * a, 256), wide(s)
                elif kind == "u":
                    src, dst = columns(ffn_w_up[0], 256 * a, 256), wide(s)
                else:
                    src, dst = ffn_w_down[0][256 * a:256 * a + 256, :].rearrange("(j p) n -> p j n", p=P), rows2(s)
                sp.dma_start(dst, src).then_inc(full[s], 16)

            for s in range(6):
                sp.wait_ge(*released(LAST[s]))

            def expert_loads(e, g, b):
                sp.wait_ge(gu_s, e * (2 * GE) + g * 2 + 2 * GD - 2)
                col = g * 256
                sp.dma_start(wide(b), moe_w_gate[ds(e, 1)].rearrange("e (k p) n -> p (e k) n", p=P)[:, :, ds(col, 256)]
                             ).then_inc(full[b], 16)
                sp.dma_start(wide(2 + b), moe_w_up[ds(e, 1)].rearrange("e (k p) n -> p (e k) n", p=P)[:, :, ds(col, 256)]
                             ).then_inc(full[2 + b], 16)

            def expert_down(e, g, b):
                sp.wait_ge(dn_s, e * GE + g + DN0 + GD - 1)
                q = e * GE + g
                sp.dma_start(rows2(4 + b), moe_w_down.rearrange("e r n -> (e r) n")[ds(q * 256, 256), :]
                             .rearrange("(j p) n -> p j n", p=P)).then_inc(full[4 + b], 16)

            with sp.Fori(0, EXPERTS) as e:
                expert_loads(e, 0, 0)
                expert_loads(e, 1, 1)
                expert_down(e, 0, 0)
                with sp.Fori(1, GE // 2) as i:
                    for b in range(2):
                        expert_loads(e, i * 2 + b, b)
                        expert_down(e, i * 2 + b - 1, 1 - b)
                expert_down(e, GE - 1, 1)

            for q in range(2 * TT):
                sp.wait_ge(o_s, q + 1)
                t, cols = q % 2, slice((q // 2) * 512, (q // 2 + 1) * 512)
                sp.dma_start(out[0, t * P:(t + 1) * P, cols], o_tm[:, t, cols]).then_inc(od_s, 16)
            sp.wait_ge(od_s, 16 * 2 * TT)

        @block.gpsimd
        def _(pool):
            g = nc.gpsimd
            g.memset(ident[:, :], 0.0).then_inc(pcst, 1)
            pool.wait_ge(pcst, 1)
            g.affine_select(out=ident[:, :], in_=ident[:, :], compare_op=ALU.not_equal, fill=1.0, base=0,
                            pattern=[[-1, P]], channel_multiplier=1).then_inc(cst_s, 1)
            g.memset(ones[:, :], 1.0).then_inc(pcst, 1)
            g.memset(amask[:, :], 0.0).then_inc(pcst, 1)
            g.iota(slot_i[:, :], pattern=[[1, SEQ]], base=0, channel_multiplier=0).then_inc(pcst, 1)
            pool.wait_ge(pcst, 4)
            g.affine_select(out=triu[:, :], in_=ones[:, :], compare_op=ALU.is_ge, fill=0.0, base=0,
                            pattern=[[1, P]], channel_multiplier=-1).then_inc(cst_s, 1)
            g.affine_select(out=striu[:, :], in_=ones[:, :], compare_op=ALU.is_gt, fill=0.0, base=0,
                            pattern=[[1, P]], channel_multiplier=-1).then_inc(cst_s, 1)
            for c0 in (0, 256):
                g.affine_select(out=amask[:, c0:c0 + P], in_=amask[:, c0:c0 + P], compare_op=ALU.is_ge, fill=NEG,
                                base=0, pattern=[[-1, P]], channel_multiplier=1).then_inc(cst_s, 1)
            g.tensor_copy(slot_f[:, :], slot_i[:, :]).then_inc(cst_s, 1)
            g.memset(cpad[:, :, :], 0.0).then_inc(cst_s, 1)

            def ada_load(n):
                i = n - ADA_FIRST
                l, a, slot = n // ADA_CHUNKS, n % ADA_CHUNKS, (n + 1) % ADA_SLOTS
                if i < ADA_SLOTS:
                    pool.wait_ge(aacc_s, (2, ADA_FIRST)[i])
                else:
                    pool.wait_ge(apool_s, i - ADA_SLOTS + 1)
                g.dma_start(aring[:, slot, :].rearrange("p (k n) -> p k n", k=KT),
                            ada_w[l][:, 256 * a:256 * a + 256].rearrange("(k p) n -> p k n", p=P)
                            ).then_inc(afull[slot], 16)

            steps = 0
            for n in range(ADA_FIRST, ADA_FIRST + ADA_SLOTS):
                ada_load(n)
            pool.wait_ge(ccol_s, 1)
            for n in range(ADA_FIRST, DEPTH * ADA_CHUNKS):
                a, slot = n % ADA_CHUNKS, (n + 1) % ADA_SLOTS
                if n == ADA_CHUNKS:
                    pool.wait_ge(mg_s, 12)
                pool.wait_ge(afull[slot], 16 * ((n - ADA_FIRST) // ADA_SLOTS + 1))
                w = aring[:, slot, :].rearrange("p (k n) -> p k n", k=KT)
                last = g.tensor_tensor(w, w, ccol[:, :].unsqueeze(2).broadcast_to([P, KT, 256]), ALU.mult)
                for half_k in (4, 2, 1):
                    last.then_inc(pstep, 1)
                    steps += 1
                    pool.wait_ge(pstep, steps)
                    dst = w[:, 0:half_k, :] if half_k > 1 else aacc[:, a, :].unsqueeze(1)
                    last = g.tensor_tensor(dst, w[:, 0:half_k, :], w[:, half_k:2 * half_k, :], ALU.add)
                last.then_inc(apool_s, 1)
                if n + ADA_SLOTS < DEPTH * ADA_CHUNKS:
                    ada_load(n + ADA_SLOTS)
        CONSTS = 7

        def param_loads(layer):
            def rows(v):
                return v.rearrange("(m p) -> m p", p=P)
            for l in (layer,):
                for src, r in ((norm1_w[l], R_N1), (norm2_w[l], R_N2), (ada_b[l], R_ADA), (conf_conv_b[l], R_CB),
                               (conf_ln_w[l], R_LW), (conf_ln_b[l], R_LB), (ssm_conv_b[l], R_SB),
                               (ssm_norm_w[l], R_SN), (final_norm_w, R_FN)):
                    v = rows(src)
                    yield prow[r:r + v.shape[0], l, :], v
                yield cwrow[0:CONF_TAPS * CT, l, :], conf_conv_w[l].rearrange("k (m p) -> (k m) p", p=P)
                yield swrow[0:SSM_TAPS * XT, l, :], ssm_conv_w[l].rearrange("k (m p) -> (k m) p", p=P)
            for l in (layer,):
                yield wdt[:, l, :, :], w_in[l][:, DT_COL:DT_COL + HEADS_S].rearrange("(k p) n -> p k n", p=P)
                yield dtb[:, l, :], ssm_dt_bias[l:l + 1, :].broadcast_to([P, HEADS_S])
                yield alog[:, l, :], ssm_A_log[l:l + 1, :].broadcast_to([P, HEADS_S])
                yield dall[:, l, :], ssm_D[l:l + 1, :].broadcast_to([P, HEADS_S])
            if layer == 0:
                return
            yield rw[:, :, :], moe_router_w[0].rearrange("(k p) n -> p k n", p=P)
            yield rb[:, :], moe_router_b[0:1, :].broadcast_to([P, EXPERTS])
        N_PARAMS = [15, 15 + 2]

        @block.tensor
        def _(pe):
            mm = nc.tensor.matmul
            pe.wait_ge(cst_s, 1)
            pe.wait_ge(c_in_s, 16)
            nc.tensor.transpose(ps[:, 7, 0:KT], crow, ident[0:KT, 0:KT]).then_inc(ctr_s, 1)
            pe.wait_ge(x_in_s, 32)
            for m in range(KT):
                for t in range(TT):
                    last = nc.tensor.transpose(ps[:, m // 2, (m % 2) * SEQ + t * P:(m % 2) * SEQ + (t + 1) * P],
                                               x_in[:, t, m * P:(m + 1) * P], ident[:, :])
            last.then_inc(xtr_s, 1)
            pe.wait_ge(cst_s, CONSTS)

            def param_columns(l):
                pe.wait_ge(par_s[l], 16 * N_PARAMS[l])
                nc.tensor.transpose(ps[:, 5 + l, 0:ROWS], prow[0:ROWS, l, :], ident[0:ROWS, 0:ROWS])
                nc.tensor.transpose(ps[:, 5 + l, 128:128 + CONF_TAPS * CT], cwrow[0:CONF_TAPS * CT, l, :],
                                    ident[0:CONF_TAPS * CT, 0:CONF_TAPS * CT])
                nc.tensor.transpose(ps[:, 5 + l, 256:256 + SSM_TAPS * XT], swrow[0:SSM_TAPS * XT, l, :],
                                    ident[0:SSM_TAPS * XT, 0:SSM_TAPS * XT]).then_inc(prow_s, 1)

            def norm_sums(ni):
                for k in range(KT):
                    if k % 2 == 0:
                        pe.wait_ge(sq_s, KT // 2 * ni + k // 2 + 1)
                    last = mm(ps[:, 2, 0:SEQ], ones[:, :], sq[:, k, :], start=(k == 0), stop=(k == KT - 1))
                last.then_inc(st_s, 1)

            def ada_transpose(l, q):
                n = ADA_CHUNKS // 2 * l + q
                if l == 0 and 2 * q < ADA_FIRST:
                    pe.wait_ge(aacc_s, 2 * q + 2)
                else:
                    pe.wait_ge(apool_s, ADA_CHUNKS * l + 2 * q + 2 - ADA_FIRST)
                if n >= 2:
                    pe.wait_ge(ared_s, n - 1)
                for j in range(4):
                    last = nc.tensor.transpose(ps[:, ADA_BANK[l] + q % 2, j * P:(j + 1) * P],
                                               aacc[:, 2 * q + j // 2, (j % 2) * P:(j % 2 + 1) * P], ident[:, :])
                last.then_inc(atr_s, 1)

            def w_chunk(l, n, s, fill):
                pe.wait_ge(full[s], fill)
                for j in range(2):
                    for k in range(KT):
                        last = mm(ps[:, n % 2, j * SEQ:(j + 1) * SEQ], wide(s)[:, k, j * P:(j + 1) * P], hT[:, k, :],
                                  start=(k == 0), stop=(k == KT - 1))
                last.then_inc(proj_s, 1)

            def scores(l, h):
                if h >= 2:
                    pe.wait_ge(msk_s, HEADS_A * l + h - 1)
                p0 = DH * (h % 2)
                q, k = proj[p0:p0 + DH, Q + h // 2, :], proj[p0:p0 + DH, K + h // 2, :]
                mm(ps[:, 3 + h % 2, 0:P], q[:, 0:P], k[:, 0:P], start=True, stop=True)
                mm(ps[:, 3 + h % 2, P:P + SEQ], q[:, P:SEQ], k[:, :], start=True, stop=True).then_inc(sc_s, 1)

            def probs_transpose(l, h):
                pe.wait_ge(pr_s, HEADS_A * l + h + 1)
                for i in range(3):
                    last = nc.tensor.transpose(ps[:, 5 + h % 2, i * P:(i + 1) * P], sc[:, h % 2, (0, 1, 2)[i] * P:
                                               ((0, 1, 2)[i] + 1) * P], ident[:, :])
                last.then_inc(ptr_s, 1)

            def pv(l, h):
                pe.wait_ge(pte_s, HEADS_A * l + h + 1)
                if h >= 2 and h % 2 == 0:
                    pe.wait_ge(ao_s, 4 * l + h // 2)
                c0, p0 = (h // 2) % 2 * SEQ, DH * (h % 2)
                mm(ps[p0:p0 + DH, 7, c0:c0 + SEQ], v_tm[:, 0, h * DH:(h + 1) * DH], pT[:, h % 2, 0:SEQ],
                   start=True, stop=False)
                mm(ps[p0:p0 + DH, 7, c0 + P:c0 + SEQ], v_tm[:, 1, h * DH:(h + 1) * DH], pT[:, h % 2, SEQ:384],
                   start=False, stop=True).then_inc(pv_s, 1)

            def acum_bcast(l, k):
                hb, cc = k // 2, k % 2
                if k >= 2:
                    pe.wait_ge(lm_s, 8 * l + k - 1)
                for r in range(4):
                    h = 4 * hb + r
                    last = mm(ps[:, 3 + k % 2, r * P:(r + 1) * P], dts[:, 4, cc, h:h + 1].broadcast_to([P, P]),
                              triu[:, :], start=True, stop=True)
                last.then_inc(bc_s, 1)

            def y_batch(l, k):
                hb, cc = k // 2, k % 2
                pe.wait_ge(lm_s, 8 * l + k + 1)
                if hb >= 2 and cc == 0:
                    pe.wait_ge(yz_s, 4 * l + hb - 1)
                for r in range(4):
                    h = 4 * hb + r
                    p0, c0 = DH * (h % 2), (r // 2) * SEQ + cc * P
                    dst = ps[p0:p0 + DH, 5 + hb % 2, c0:c0 + P]
                    last = mm(dst, xdt[:, cc, h * DH:(h + 1) * DH], seg[:, k % 2, r, :], start=True, stop=(cc == 0))
                    if cc == 1:
                        last = mm(dst, prev[:, hb // 2, (h % 8) * DH:(h % 8 + 1) * DH], cdec[:, r, :],
                                  start=False, stop=True)
                last.then_inc(y_s, 1)

            def out_pair(l, idx, s, view, kk, cols, rhs):
                pair = 16 * l + idx
                if pair >= 2:
                    pe.wait_ge(mg_s, pair - 1)
                for j in range(2):
                    for k in range(kk):
                        last = mm(ps[:, idx % 2, j * SEQ:(j + 1) * SEQ], view(s)[:, k, (cols + j) * P:(cols + j + 1) * P],
                                  rhs[:, k, :], start=(k == 0), stop=(k == kk - 1))
                last.then_inc(om_s, 1)

            def gate_up(g_slot, u_slot, j, x_src, n, first=False):
                for w, c0 in ((g_slot, 0), (u_slot, SEQ)):
                    for k in range(KT):
                        if first and w == g_slot:
                            pe.wait_ge(h_s, KT + k + 1)
                        last = mm(ps[:, j, c0:c0 + n], wide(w)[:, k, j * P:(j + 1) * P], x_src[:, k, 0:n],
                                  start=(k == 0), stop=(k == KT - 1))
                last.then_inc(gu_s, 1)

            def down(slot, b, n, first, stop):
                for j in range(2):
                    for t in range((n + P - 1) // P):
                        rows = min(P, n - t * P)
                        for hf in range(2):
                            dst = ps[0:rows, 2 + 2 * t + hf, :] if rows > HALF else ps[HALF * hf:HALF * hf + rows, 4, :]
                            last = mm(dst, hm[:, b, j, t * P:t * P + rows],
                                      rows2(slot)[:, j, hf * 512:(hf + 1) * 512],
                                      start=(first and j == 0), stop=(stop and j == 1))
                last.then_inc(dn_s, 1)

            for l in range(DEPTH):
                norm_sums(2 * l)
                if l == 0:
                    param_columns(0)
                    for q in range(ADA_FIRST // 2):
                        ada_transpose(0, q)
                for t in range(TT):
                    for k in range(KT):
                        if t == 0:
                            pe.wait_ge(h_s, 2 * KT * l + k + 1)
                        last = mm(ps[:, 2, 256 + t * HEADS_S:256 + (t + 1) * HEADS_S], hT[:, k, t * P:(t + 1) * P],
                                  wdt[:, l, k, :], start=(k == 0), stop=(k == KT - 1))
                last.then_inc(dtmm_s, 1)
                with pe.Fori(0, LOOPED // SLOTS) as i:
                    for b in range(SLOTS):
                        s, f, _ = PLAN[("w", l, b)]
                        pe.wait_ge(ev_s, i * SLOTS + W_CHUNKS * l + b + 1)
                        w_chunk(l, b, s, i * 16 + 16 * f)

                def w_next(n):
                    pe.wait_ge(ev_s, W_CHUNKS * l + n + 1)
                    w_chunk(l, n, *slot_of(("w", l, n)))

                if l == 0:
                    param_columns(1)
                for n in range(LOOPED, 16):
                    w_next(n)
                pe.wait_ge(cv_s, CV0 + (l + 1) * CT * CONF_TAPS)
                for k in range(CT):
                    last = mm(ps[:, 2, 0:SEQ], ones[:, :], cacc[:, k, :], start=(k == 0), stop=(k == CT - 1))
                last.then_inc(cm_s, 1)
                w_next(16)
                w_next(17)
                w_next(18)
                pe.wait_ge(xsil_s, 3 * (l + 1))
                for t in range(TT):
                    for q in range(2):
                        for m in range(4):
                            last = nc.tensor.transpose(ps[:, 3 + 2 * t + q, m * P:(m + 1) * P],
                                                       xc[:, 4 * q + m, t * P:(t + 1) * P], ident[:, :])
                        last.then_inc(xst_s, 1)
                for g in range(GROUPS):
                    last = nc.tensor.transpose(ps[:, 7, g * P:(g + 1) * P], xc[:, 8 + g, 0:P], ident[:, :])
                last.then_inc(xst_s, 1)
                pe.wait_ge(dt_s, l + 1)
                pe.wait_ge(cx_s, l + 1)
                for cc in range(TT):
                    mm(ps[:, 2, 336 + cc * HEADS_S:336 + (cc + 1) * HEADS_S], triu[:, :], dts[:, 4, cc, :],
                       start=True, stop=True)
                mm(ps[:, 2, 368:384], ones[:, :], dts[:, 4, 0, :], start=True, stop=True).then_inc(ac_s, 1)
                w_next(19)
                pe.wait_ge(csq_s, l + 1)
                pe.wait_ge(acs_s, l + 1)
                for k in range(CT):
                    last = mm(ps[:, 2, 0:SEQ], ones[:, :], csq[:, k, :], start=(k == 0), stop=(k == CT - 1))
                last.then_inc(cvar_s, 1)
                if l == 0:
                    pe.wait_ge(xse_s, 5)
                    for q in range(ADA_FIRST // 2, ADA_CHUNKS // 2):
                        ada_transpose(0, q)
                    pe.wait_ge(ared_s, ADA_CHUNKS // 2)
                for i in range(12):
                    w_next(20 + i)
                    if i == 0:
                        pe.wait_ge(xse_s, 5 * (l + 1))
                        for g in range(GROUPS):
                            for cc in range(TT):
                                last = mm(ps[:, 7, (2 * g + cc) * P:(2 * g + cc + 1) * P],
                                          xc[:, 8 + g, cc * P:(cc + 1) * P], xc[:, 10 + g, cc * P:(cc + 1) * P],
                                          start=True, stop=True)
                        last.then_inc(cb_s, 1)
                        pe.wait_ge(ev_s, 2 + W_CHUNKS * l + 20)
                        for t in range(TT):
                            for m in range(4):
                                last = nc.tensor.transpose(ps[:, 5 + t, m * P:(m + 1) * P],
                                                           proj[:, V + m, t * P:(t + 1) * P], ident[:, :])
                            last.then_inc(vt_s, 1)
                    if 1 <= i <= 4:
                        if i == 1:
                            pe.wait_ge(vtm_s, 2 * (l + 1))
                            pe.wait_ge(cbm_s, l + 1)
                        for h in (2 * i - 2, 2 * i - 1):
                            probs_transpose(l, h)
                    if i < 4:
                        for h in (2 * i, 2 * i + 1):
                            scores(l, h)
                    if 1 <= i <= 4:
                        for h in (2 * i - 2, 2 * i - 1):
                            pv(l, h)
                    if i == 4:
                        pe.wait_ge(xd_s, l + 1)
                        for g in range(GROUPS):
                            mm(ps[:, 5 + g, :], b_tm[:, g, :], xdtd[:, g * 512:(g + 1) * 512],
                               start=True, stop=True).then_inc(stt_s, 1)
                        acum_bcast(l, 0)
                    if i >= 5:
                        if i == 5:
                            pe.wait_ge(prev_s, 2 * (l + 1))
                        acum_bcast(l, i - 4)
                        y_batch(l, i - 5)
                pe.wait_ge(cu_s, l + 1)
                for idx in range(4):
                    if idx < 2:
                        pe.wait_ge(ev_s, 1 + W_CHUNKS * (l + 1) + idx)
                    s, n = slot_of(("conf", l, idx // 2))
                    pe.wait_ge(full[s], n)
                    out_pair(l, idx, s, half, CT, 2 * (idx % 2), cacc)
                    if idx == 0:
                        y_batch(l, 7)
                    if idx == 2:
                        pe.wait_ge(gsq_s, 2 * (l + 1))
                        for g in range(GROUPS):
                            for k in range(4):
                                last = mm(ps[:, 7, g * SEQ:(g + 1) * SEQ], ones[:, :], ysq[:, 4 * g + k, :],
                                          start=(k == 0), stop=(k == 3))
                        last.then_inc(gst_s, 1)
                for idx in range(4):
                    s, n = slot_of(("attn", l, idx // 2))
                    pe.wait_ge(full[s], n)
                    out_pair(l, 4 + idx, s, half, 4, 2 * (idx % 2), ao)
                pe.wait_ge(gn_s, l + 1)
                for idx in range(4):
                    s, n = slot_of(("ssm", l, idx))
                    pe.wait_ge(full[s], n)
                    out_pair(l, 8 + idx, s, wide, KT, 0, proj[:, Z:Z + 8, :])
                pe.wait_ge(mg_s, 16 * l + 12)
                for idx in range(4):
                    s, n = slot_of(("mix", l, idx))
                    pe.wait_ge(full[s], n)
                    out_pair(l, 12 + idx, s, wide, KT, 0, merged)
                norm_sums(2 * l + 1)
                if l == 0:
                    for g in range(GD):
                        gs, gn = slot_of(("g", 0, g))
                        us, un = slot_of(("u", 0, g))
                        pe.wait_ge(full[gs], gn)
                        pe.wait_ge(full[us], un)
                        for j in range(2):
                            pe.wait_ge(hm_s, 2 * g + j + 1)
                            gate_up(gs, us, j, hT, SEQ, g == 0 and j == 0)
                        if g:
                            dsl, dn = slot_of(("d", 0, g - 1))
                            pe.wait_ge(full[dsl], dn)
                            pe.wait_ge(hm_s, HM0 + 2 * g)
                            down(dsl, (g - 1) % 2, SEQ, g == 1, False)
                        ada_transpose(1, g)
                    dsl, dn = slot_of(("d", 0, GD - 1))
                    pe.wait_ge(full[dsl], dn)
                    pe.wait_ge(hm_s, HM0 + 2 * GD)
                    down(dsl, (GD - 1) % 2, SEQ, False, True)
                    ada_transpose(1, ADA_CHUNKS // 2 - 1)
                    pe.wait_ge(ye_s, 1)
                    pe.wait_ge(ared_s, ADA_CHUNKS)
                    for m in range(KT):
                        pe.wait_ge(cf_s, m + 1)
                        for t in range(TT):
                            last = nc.tensor.transpose(ps[:, 6 + m % 2, t * P:(t + 1) * P],
                                                       ysb[:, t, m * P:(m + 1) * P], ident[:, :])
                        last.then_inc(c_s, 1)

            for t in range(TT):
                for k in range(KT):
                    if t == 0:
                        pe.wait_ge(h_s, 3 * KT + k + 1)
                    last = mm(ps[:, 0, t * EXPERTS:(t + 1) * EXPERTS], hT[:, k, t * P:(t + 1) * P], rw[:, k, :],
                              start=(k == 0), stop=(k == KT - 1))
            last.then_inc(lg_s, 1)
            for t in range(TT):
                for m in range(KT):
                    last = nc.tensor.transpose(ps[:, 2 + 2 * t + m // 4, (m % 4) * P:(m % 4 + 1) * P],
                                               hT[:, m, t * P:(t + 1) * P], ident[:, :])
                last.then_inc(htr_s, 1)
            pe.wait_ge(mk_s, 1)
            mask = rt[:, 12, :, :]
            mm(ps[:, 1, 0:8], striu[:, :], mask[:, 0, :], start=True, stop=True)
            mm(ps[:, 1, 8:16], ones[:, :], mask[:, 0, :], start=True, stop=False)
            mm(ps[:, 1, 8:16], striu[:, :], mask[:, 1, :], start=False, stop=True)
            mm(ps[:, 1, 16:24], ones[:, :], mask[:, 0, :], start=True, stop=False)
            mm(ps[:, 1, 16:24], ones[:, :], mask[:, 1, :], start=False, stop=True).then_inc(cum_s, 1)

            C_BASE, PER = KT, 1 + 2 * KT

            def gather(free_at, n):
                for m in range(KT):
                    pe.wait_ge(cf_s, free_at + m)
                    for t in range(TT):
                        last = mm(ps[:, 6 + (m + 1) % 2, 0:n], h_tm[:, t, m * P:(m + 1) * P], p_m[:, t, 0:n],
                                  start=(t == 0), stop=(t == TT - 1))
                    last.then_inc(c_s, 1)

            pe.wait_ge(htm_s, TT)
            pe.wait_ge(p_s, 1)
            gather(CF0 + C_BASE - 1, SEQ)
            pe.wait_ge(rk_s, 2)
            C1 = C_BASE + KT

            def scatter(n, free_at):
                slot_tiles = (n + P - 1) // P
                for m in range(KT):
                    pe.wait_ge(cf_s, free_at + m)
                    for st in range(slot_tiles):
                        rows = min(P, n - st * P)
                        last = mm(ps[:, 6 + (m + 1) % 2, 0:SEQ], ysb[0:rows, st, m * P:(m + 1) * P],
                                  pgT[0:rows, st, :], start=(st == 0), stop=(st == slot_tiles - 1))
                    last.then_inc(c_s, 1)

            with pe.Fori(0, EXPERTS) as e:
                count = pe.value_load(cnt[0:1, ds(e + 1, 1)], min_val=0, max_val=SEQ)
                before = pe.value_load(cnt[0:1, ds(e, 1)], min_val=0, max_val=SEQ)
                after = pe.value_load(cnt[0:1, ds(e + 2, 1)], min_val=0, max_val=SEQ)
                pe.wait_ge(cf_s, e * PER + CF0 + C1)

                def small_expert():
                    def group(gi, b, tiles):
                        pe.wait_ge(full[b], gi * 16 + 16 * FILLS[b] + 16)
                        pe.wait_ge(full[2 + b], gi * 16 + 16 * FILLS[2 + b] + 16)
                        pe.wait_ge(hm_s, tiles)
                        for w, c0 in ((b, 0), (2 + b, P)):
                            for k in range(KT):
                                for j in range(2):
                                    last = mm(ps[HALF * j:HALF * (j + 1), b, c0:c0 + P], xg[:, k, 0:HALF],
                                              wide(w)[:, k, j * P:(j + 1) * P], start=(k == 0), stop=(k == KT - 1))
                            last.then_inc(gu_s, 1)

                    def group_down(gi, b, tiles, groups, first, stop):
                        pe.wait_ge(hm_s, tiles + HM0)
                        nc.tensor.transpose(ps[:, 4 + b, 0:P], hsm[:, b, :], ident[:, :]).then_inc(ht_s, 1)
                        pe.wait_ge(full[4 + b], gi * 16 + 16 * FILLS[4 + b] + 16)
                        pe.wait_ge(hte_s, groups)
                        for j in range(2):
                            for hf in range(2):
                                last = mm(ps[HALF * hf:HALF * (hf + 1), 2, :], hm[:, b, 0, HALF * j:HALF * (j + 1)],
                                          rows2(4 + b)[:, j, hf * 512:(hf + 1) * 512],
                                          start=(first and j == 0), stop=(stop and j == 1))
                        last.then_inc(dn_s, 1)

                    T0 = e * (2 * GE) + 2 * GD
                    G0 = e * GE
                    half_e = e * (GE // 2)
                    group(half_e, 0, T0)
                    group(half_e, 1, T0 + 2)
                    scatter_before()
                    group_down(half_e, 0, T0 + 2, G0 + 1, True, False)
                    with pe.Fori(1, GE // 2) as i:
                        for b in range(2):
                            group(half_e + i, b, T0 + i * 4 + 2 * b)
                            if b == 0:
                                group_down(half_e + i - 1, 1, T0 + i * 4, G0 + i * 2, False, False)
                            else:
                                group_down(half_e + i, 0, T0 + i * 4 + 2, G0 + i * 2 + 1, False, False)
                    prepare(HALF)
                    group_down(half_e + GE // 2 - 1, 1, T0 + 2 * GE, G0 + GE, False, True)

                def expert(n):
                    if n == HALF:
                        small_expert()
                    else:
                        large_expert(n)
                        pe.sem_inc(ht_s, GE)

                def large_expert(n):
                    def group(gi, b, wait_tiles):
                        pe.wait_ge(full[b], gi * 16 + 16 * FILLS[b] + 16)
                        pe.wait_ge(full[2 + b], gi * 16 + 16 * FILLS[2 + b] + 16)
                        for j in range(2):
                            pe.wait_ge(hm_s, wait_tiles + j + 1)
                            gate_up(b, 2 + b, j, xg, n)

                    def group_down(gi, b, tiles, first, stop):
                        pe.wait_ge(full[4 + b], gi * 16 + 16 * FILLS[4 + b] + 16)
                        pe.wait_ge(hm_s, tiles + HM0)
                        down(4 + b, b, n, first, stop)

                    T0 = e * (2 * GE) + 2 * GD
                    half_e = e * (GE // 2)
                    group(half_e, 0, T0)
                    group(half_e, 1, T0 + 2)
                    scatter_before()
                    group_down(half_e, 0, T0 + 2, True, False)
                    with pe.Fori(1, GE // 2) as i:
                        for b in range(2):
                            group(half_e + i, b, T0 + i * 4 + 2 * b)
                            if b == 0:
                                group_down(half_e + i - 1, 1, T0 + i * 4, False, False)
                            else:
                                group_down(half_e + i, 0, T0 + i * 4 + 2, False, False)
                    prepare(n)
                    group_down(half_e + GE // 2 - 1, 1, T0 + 2 * GE, False, True)

                def scatter_before():
                    pe.wait_ge(ye_s, e + 1)
                    by_size(pe, before, lambda slots: scatter(slots, e * PER + CF0 + C1 - 1))

                def prepare(n):
                    slot_tiles = (n + P - 1) // P
                    pe.wait_ge(pg_s, e + 1)
                    pe.wait_ge(cf_s, e * PER + CF0 + C1 + KT)
                    for st in range(slot_tiles):
                        for t in range(TT):
                            last = nc.tensor.transpose(ps[:, 6, st * SEQ + t * P:st * SEQ + (t + 1) * P],
                                                       pg_m[:, t, st * P:(st + 1) * P], ident[:, :])
                    last.then_inc(c_s, 1)
                    pe.wait_ge(p_s, e + 2)
                    with pe.If(after <= P):
                        gather(e * PER + CF0 + C1 + KT, P)
                    with pe.Else():
                        gather(e * PER + CF0 + C1 + KT, SEQ)

                by_size(pe, count, expert)
            last_count = pe.value_load(cnt[0:1, EXPERTS:EXPERTS + 1], min_val=0, max_val=SEQ)
            pe.wait_ge(ye_s, EXPERTS + 1)
            by_size(pe, last_count, lambda slots: scatter(slots, PER * EXPERTS + CF0 + C1 - 1))

            norm_sums(2 * DEPTH)
            for m in range(KT):
                pe.wait_ge(h_s, 2 * DEPTH * KT + m + 1)
                for t in range(TT):
                    last = nc.tensor.transpose(ps[:, 4 + 2 * (m // 4) + t, (m % 4) * P:(m % 4 + 1) * P],
                                               hT[:, m, t * P:(t + 1) * P], ident[:, :])
                    if m % 4 == 3:
                        last.then_inc(fin_s, 1)

        @block.scalar
        def _(act):
            a_ = nc.scalar.activation

            def norm_squares(ni):
                for i in range(KT // 2):
                    if ni == 0:
                        act.wait_ge(x_s, 1)
                    elif ni % 2:
                        act.wait_ge(mg_s, 8 * (ni - 1) + 12 + i + 1)
                    elif ni == 2:
                        act.wait_ge(cf_s, CF0 + 2 * i + 2)
                    else:
                        act.wait_ge(cf_s, CF0 + 2 * KT + (1 + 2 * KT) * EXPERTS + 2 * i + 2)
                    a_(sq[:, 2 * i:2 * i + 2, :], xT[:, 2 * i:2 * i + 2, :], ACT.Square).then_inc(sq_s, 1)

            act.wait_ge(ctr_s, 1)
            a_(ccol[:, :], ps[:, 7, 0:KT], ACT.Silu).then_inc(ccol_s, 1)
            for l in range(DEPTH):
                for dst, src in param_loads(l):
                    act.dma_start(dst, src).then_inc(par_s[l], 16)
                if l == 0:
                    act.wait_ge(xtr_s, 1)
                    for b in range(4):
                        last = a_(xT[:, 2 * b:2 * b + 2, :], ps[:, b, :].rearrange("p (a b) -> p a b", a=2), ACT.Copy)
                    last.then_inc(x_s, 1)
                    norm_squares(0)

            def norm(ni):
                if ni:
                    norm_squares(ni)
                act.wait_ge(var_s, ni + 1)
                a_(rs[:, 1, :], rs[:, 0, :], ACT.Sqrt).then_inc(sd_s, 1)

            def shift(ni, factor, shift_cols):
                for m in range(KT):
                    act.wait_ge(nx_s, KT * ni + m + 1)
                    a_(hT[:, m, :], sq[:, m, :], ACT.Identity, bias=shift_cols[:, m:m + 1],
                       scale=factor[:, m:m + 1]).then_inc(h_s, 1)

            def evac(l, n):
                act.wait_ge(proj_s, W_CHUNKS * l + n + 1)
                a_(proj[:, 2 * n:2 * n + 2, :], ps[:, n % 2, :].rearrange("p (a b) -> p a b", a=2),
                   ACT.Copy).then_inc(ev_s, 1)

            def evac_y(n):
                if n == HALF:
                    for hf in range(2):
                        last = a_(ysb[0:HALF, 0, hf * 512:(hf + 1) * 512], ps[HALF * hf:HALF * (hf + 1), 2, :], ACT.Copy)
                    last.then_inc(ye_s, 1)
                    return
                for t in range((n + P - 1) // P):
                    rows = min(P, n - t * P)
                    for hf in range(2):
                        src = ps[0:rows, 2 + 2 * t + hf, :] if rows > HALF else ps[HALF * hf:HALF * hf + rows, 4, :]
                        last = a_(ysb[0:rows, t, hf * 512:(hf + 1) * 512], src, ACT.Copy)
                last.then_inc(ye_s, 1)

            for l in range(DEPTH):
                norm(2 * l)
                shift(2 * l, acolw[:, 0, :], modc[:, 0:KT])
                act.wait_ge(dtin_s, l + 1)
                a_(dts[:, 1, :, :], dts[:, 1, :, :], ACT.Exp, scale=-1.0).then_inc(dtexp_s, 1)
                a_(alog[:, l, :], alog[:, l, :], ACT.Exp).then_inc(dtexp_s, 1)
                act.wait_ge(dtexp_s, 2 * l + 2)
                a_(dts[:, 2, :, :], dts[:, 1, :, :], ACT.Ln, bias=1.0).then_inc(dtln_s, 1)
                for n in range(4):
                    evac(l, n)
                act.wait_ge(ev_s, 2 + W_CHUNKS * l + 4)
                a_(proj[:, GLU:GLU + CT, :], proj[:, GLU:GLU + CT, :], ACT.Sigmoid).then_inc(sig_s, 1)
                for n in range(4, 17):
                    evac(l, n)
                for q in range(3):
                    act.wait_ge(xv_s, 3 * l + q + 1)
                    a_(xc[:, 4 * q:4 * q + 4, :], xc[:, 4 * q:4 * q + 4, :], ACT.Silu).then_inc(xsil_s, 1)
                evac(l, 17)
                a_(proj[:, Z:Z + 8, :], proj[:, Z:Z + 8, :], ACT.Silu).then_inc(zs_s, 1)
                act.wait_ge(cx_s, l + 1)
                a_(csq[:, :, :], cacc[:, :, :], ACT.Square).then_inc(csq_s, 1)
                evac(l, 18)
                for q in range(4):
                    act.wait_ge(xst_s, 5 * l + q + 1)
                    a_(xs_tm[:, q // 2, (q % 2) * 512:(q % 2 + 1) * 512], ps[:, 3 + q, :],
                       ACT.Copy).then_inc(xse_s, 1)
                act.wait_ge(xst_s, 5 * l + 5)
                a_(b_tm[:, :, :], ps[:, 7, 0:SEQ].rearrange("p (a b) -> p a b", a=2), ACT.Copy).then_inc(xse_s, 1)
                act.wait_ge(acs_s, l + 1)
                a_(dec[:, 1, :], dec[:, 0, :], ACT.Exp).then_inc(dcy_s, 1)
                evac(l, 19)
                act.wait_ge(cvr_s, l + 1)
                a_(rs[:, 1, :], rs[:, 0, :], ACT.Sqrt).then_inc(csd_s, 1)
                act.wait_ge(cn_s, l + 1)
                for m in range(CT):
                    last = a_(cacc[:, m, :], cacc[:, m, :], ACT.Silu, bias=pcol[:, l, R_LB + m:R_LB + m + 1],
                              scale=pcol[:, l, R_LW + m:R_LW + m + 1])
                last.then_inc(cu_s, 1)

                def lmat_exp(k):
                    act.wait_ge(seg_s, 8 * l + k + 1)
                    if k % 2:
                        a_(cdec[:, :, :], ps[:, 3 + k % 2, :].rearrange("p (a b) -> p a b", a=4), ACT.Exp)
                    a_(seg[:, k % 2, :, :], seg[:, k % 2, :, :], ACT.Exp).then_inc(ls_s, 1)

                for i in range(12):
                    if 1 <= i <= 4:
                        for h in (2 * i - 2, 2 * i - 1):
                            b = h % 2
                            act.wait_ge(mx_s, HEADS_A * l + h + 1)
                            a_(sc[:, b, 0:P], sc[:, b, 0:P], ACT.Exp, bias=smx[:, b, 1, 0:1], accum_out=smx[:, b, 2, 0:1])
                            a_(sc[:, b, P:384], sc[:, b, P:384], ACT.Exp, bias=smx[:, b, 1, 1:2],
                               accum_out=smx[:, b, 2, 1:2]).then_inc(ex_s, 1)
                    if i >= 5:
                        lmat_exp(i - 5)
                    evac(l, 20 + i)
                    if i == 0:
                        for t in range(TT):
                            act.wait_ge(vt_s, 2 * l + t + 1)
                            a_(v_tm[:, t, :], ps[:, 5 + t, :], ACT.Copy).then_inc(vtm_s, 1)
                    if 1 <= i <= 4:
                        for h in (2 * i - 2, 2 * i - 1):
                            act.wait_ge(ptr_s, HEADS_A * l + h + 1)
                            a_(pT[:, h % 2, :], ps[:, 5 + h % 2, 0:384], ACT.Copy).then_inc(pte_s, 1)
                    if i == 4:
                        for g in range(GROUPS):
                            act.wait_ge(stt_s, 2 * l + g + 1)
                            a_(prev[:, g, :], ps[:, 5 + g, :], ACT.Copy).then_inc(prev_s, 1)
                lmat_exp(7)
                act.wait_ge(ev_s, 2 + W_CHUNKS * (l + 1))
                for g in range(3):
                    a_(proj[:, GATE + 8 * g:GATE + 8 * g + 8, :], proj[:, GATE + 8 * g:GATE + 8 * g + 8, :],
                       ACT.Sigmoid).then_inc(gate_s, 1)
                for g in range(GROUPS):
                    act.wait_ge(yz_s, 4 * l + 2 * g + 2)
                    a_(ysq[:, 4 * g:4 * g + 4, :], proj[:, Z + 4 * g:Z + 4 * g + 4, :], ACT.Square).then_inc(gsq_s, 1)
                act.wait_ge(gv_s, l + 1)
                a_(gr[:, 1, :, :], gr[:, 0, :, :], ACT.Sqrt).then_inc(gsd_s, 1)
                norm(2 * l + 1)
                shift(2 * l + 1, acolw[:, 1, :], modc[:, 24:32])
                if l == 0:
                    for T in range(2 * GD):
                        act.wait_ge(gu_s, T + 1)
                        a_(sil[:, T % 2, :], ps[:, T % 2, 0:SEQ], ACT.Silu).then_inc(sil_s, 1)
                    act.wait_ge(dn_s, DN0 + GD)
                    evac_y(SEQ)

            for t in range(TT):
                act.wait_ge(htr_s, t + 1)
                for hf in range(2):
                    last = a_(h_tm[:, t, hf * 512:(hf + 1) * 512], ps[:, 2 + 2 * t + hf, :], ACT.Copy)
                last.then_inc(htm_s, 1)
            act.wait_ge(re_s, 1)
            a_(rt[:, 8, :, 1:2], rt[:, 8, :, 0:1], ACT.Exp).then_inc(rx_s, 1)
            act.wait_ge(rk_s, 2)
            with act.Fori(0, EXPERTS) as e:
                count = act.value_load(cnt[0:1, ds(e + 1, 1)], min_val=0, max_val=SEQ)

                def expert(n):
                    if n == HALF:
                        with act.Fori(0, GE // 2) as i:
                            for b in range(2):
                                act.wait_ge(gu_s, e * (2 * GE) + i * 4 + 2 * GD + 2 * b + 2)
                                for j in range(2):
                                    a_(sil[:, b, HALF * j:HALF * (j + 1)], ps[:, b, HALF * j:HALF * (j + 1)],
                                       ACT.Silu).then_inc(sil_s, 1)
                        act.wait_ge(dn_s, e * GE + DN0 + GD + GE)
                        evac_y(n)
                        return
                    with act.Fori(0, GE) as i:
                        for j in range(2):
                            act.wait_ge(gu_s, e * (2 * GE) + i * 2 + 2 * GD + j + 1)
                            a_(sil[:, j, 0:n], ps[:, j, 0:n], ACT.Silu).then_inc(sil_s, 1)
                    act.wait_ge(dn_s, e * GE + DN0 + GD + GE)
                    evac_y(n)

                by_size(act, count, expert)
            norm(2 * DEPTH)
            for m in range(KT):
                act.wait_ge(nx_s, KT * 2 * DEPTH + m + 1)
                a_(hT[:, m, :], sq[:, m, :], ACT.Copy, scale=pcol[:, 0, R_FN + m:R_FN + m + 1]).then_inc(h_s, 1)
            for q in range(2 * TT):
                act.wait_ge(fin_s, q + 1)
                a_(o_tm[:, q % 2, (q // 2) * 512:(q // 2 + 1) * 512], ps[:, 4 + q, :], ACT.Copy).then_inc(o_s, 1)

        @block.vector
        def _(dve):
            v = nc.vector
            steps = [0]

            def then_wait(ins):
                steps[0] += 1
                ins.then_inc(vst, 1)
                dve.wait_ge(vst, steps[0])

            for s, n in ((ev_s, 2), (cv_s, CV0), (hm_s, HM0), (dn_s, DN0), (cf_s, CF0)):
                dve.sem_inc(s, n)
            v.memset(key9[:, :, EXPERTS:EXPERTS + 1], -1.0)
            v.memset(gate9[:, :, EXPERTS:EXPERTS + 1], 0.0)
            then_wait(v.memset(cntf[:, :], 0.0))

            dve.wait_ge(ccol_s, 1)

            def bc(ap, n):
                return ap.unsqueeze(1).broadcast_to([P, n, ap.shape[-1]])

            def ada_pair(a):
                for k in range(KT):
                    for i in (a, a + 1):
                        w = ada_first[i].rearrange("p (k n) -> p k n", k=KT)[:, k, :]
                        if k == 0:
                            dve.wait_ge(afirst[i], 16)
                            ins = v.tensor_scalar(aacc[:, i, :], w, ccol[:, 0:1], None, ALU.mult)
                        else:
                            dve.wait_ge(vst, steps[0] - (0 if i > a and k == KT - 1 else 1))
                            ins = v.scalar_tensor_tensor(aacc[:, i, :], w, ccol[:, k:k + 1], aacc[:, i, :],
                                                         ALU.mult, ALU.add)
                        if k < KT - 1:
                            steps[0] += 1
                            ins.then_inc(vst, 1)
                        else:
                            ins.then_inc(aacc_s, 1)

            def modulation(l, q0, q1):
                for q in range(q0, q1):
                    ada_reduce(l, q, modc)
                modulation_bias(l, q0, q1, modc)

            def ada_reduce(l, q, dst):
                dve.wait_ge(atr_s, ADA_CHUNKS // 2 * l + q + 1)
                v.tensor_reduce(dst[:, 4 * q:4 * q + 4],
                                ps[:, ADA_BANK[l] + q % 2, :].rearrange("p (a b) -> p a b", a=4),
                                AX.X, ALU.add).then_inc(ared_s, 1)

            def modulation_bias(l, q0, q1, src):
                dve.wait_ge(ared_s, ADA_CHUNKS // 2 * l + q1)
                c0, c1 = 4 * q0, 4 * q1
                then_wait(v.tensor_tensor(modc[:, c0:c1], src[:, c0:c1], pcol[:, l, R_ADA + c0:R_ADA + c1], ALU.add))

            def factor(l, part):
                s0, w0 = (8, R_N1) if part == 0 else (32, R_N2)
                then_wait(v.scalar_tensor_tensor(acolw[:, part, :], modc[:, s0:s0 + KT], 1.0,
                                                 pcol[:, l, w0:w0 + KT], ALU.add, ALU.mult))

            def rms(ni):
                rms_inverse(ni)
                rms_scale(ni)

            def rms_inverse(ni):
                dve.wait_ge(st_s, ni + 1)
                v.tensor_scalar(rs[:, 0, :], ps[:, 2, 0:SEQ], 1.0 / D_MODEL, EPS, ALU.mult, ALU.add).then_inc(var_s, 1)
                dve.wait_ge(sd_s, ni + 1)
                then_wait(v.reciprocal(rs[:, 2, :], rs[:, 1, :]))

            def rms_scale(ni):
                for m in range(KT):
                    v.tensor_tensor(sq[:, m, :], xT[:, m, :], rs[:, 2, :], ALU.mult).then_inc(nx_s, 1)

            def head_scores(l, h):
                b, n = h % 2, HEADS_A * l + h
                dve.wait_ge(sc_s, n + 1)
                if n >= 2:
                    dve.wait_ge(ptr_s, n - 1)
                v.scalar_tensor_tensor(sc[:, b, :], ps[:, 3 + b, 0:384], DH ** -0.5, amask[:, :],
                                       ALU.mult, ALU.add).then_inc(msk_s, 1)
                dve.wait_ge(msk_s, n + 1)
                v.reduce_max(smx[:, b, 0, 0:1], sc[:, b, 0:P], AX.X)
                then_wait(v.reduce_max(smx[:, b, 0, 1:2], sc[:, b, P:384], AX.X))
                v.tensor_scalar(smx[:, b, 1, :], smx[:, b, 0, :], -1.0, None, ALU.mult).then_inc(mx_s, 1)

            def head_probs(l, h):
                b, n = h % 2, HEADS_A * l + h
                dve.wait_ge(ex_s, n + 1)
                then_wait(v.reciprocal(smx[:, b, 3, :], smx[:, b, 2, :]))
                v.tensor_scalar(sc[:, b, 0:P], sc[:, b, 0:P], smx[:, b, 3, 0:1], None, ALU.mult)
                v.tensor_scalar(sc[:, b, P:384], sc[:, b, P:384], smx[:, b, 3, 1:2], None, ALU.mult).then_inc(pr_s, 1)

            def seg_of(l, k):
                hb, cc = k // 2, k % 2
                dve.wait_ge(bc_s, 8 * l + k + 1)
                if 8 * l + k >= 2:
                    dve.wait_ge(y_s, 8 * l + k - 1)
                for r in range(4):
                    last = v.tensor_scalar(seg[:, k % 2, r, :], ps[:, 3 + k % 2, r * P:(r + 1) * P],
                                           acum[:, cc, 4 * hb + r:4 * hb + r + 1], 0.0, ALU.subtract, ALU.min)
                last.then_inc(seg_s, 1)

            def lmat(l, k):
                hb, cc = k // 2, k % 2
                dve.wait_ge(ls_s, 8 * l + k + 1)
                if cc:
                    v.tensor_tensor(cdec[:, :, :], cdec[:, :, :], bc(xc[:, 10 + hb // 2, P:SEQ], 4), ALU.mult)
                v.tensor_tensor(seg[:, k % 2, :, :], seg[:, k % 2, :, :], bc(cbm[:, hb // 2, cc, :], 4),
                                ALU.mult).then_inc(lm_s, 1)

            def y_out(l, hb):
                dve.wait_ge(y_s, 8 * l + 2 * hb + 2)
                for j in range(2):
                    m = 2 * hb + j
                    last = v.scalar_tensor_tensor(xc[:, m, :], xc[:, m, :], dcol[:, l, m:m + 1],
                                                  ps[:, 5 + hb % 2, j * SEQ:(j + 1) * SEQ], ALU.mult, ALU.add)
                then_wait(last)
                z = proj[:, Z + 2 * hb:Z + 2 * hb + 2, :]
                v.tensor_tensor(z, xc[:, 2 * hb:2 * hb + 2, :], z, ALU.mult).then_inc(yz_s, 1)

            def residual(l, idx, first_col):
                for j in range(2):
                    m = 2 * idx + j
                    last = v.scalar_tensor_tensor(xT[:, m, :], ps[:, idx % 2, j * SEQ:(j + 1) * SEQ],
                                                  modc[:, first_col + m:first_col + m + 1], xT[:, m, :],
                                                  ALU.mult, ALU.add)
                return last

            ada_pair(0)
            ada_pair(2)
            ada_pair(4)

            def params(l):
                dve.wait_ge(prow_s, l + 1)
                v.tensor_copy(pcol[:, l, :], ps[:, 5 + l, 0:ROWS])
                v.tensor_copy(cwcol[:, l, :], ps[:, 5 + l, 128:128 + CONF_TAPS * CT])
                v.tensor_copy(swcol[:, l, :], ps[:, 5 + l, 256:256 + SSM_TAPS * XT]).then_inc(pcol_s, 1)
                dve.wait_ge(pcol_s, l + 1)
                dve.wait_ge(par_s[l], 16 * N_PARAMS[l])
                for hh in range(2):
                    p0 = DH * hh
                    v.tensor_copy(dcol[p0:p0 + DH, l, :], dall[p0:p0 + DH, l, hh:HEADS_S:2])

            for l in range(DEPTH):
                if l == 0:
                    rms_inverse(0)
                    params(0)
                    ada_pair(6)
                    modulation(0, 0, ADA_FIRST // 2)
                    factor(0, 0)
                    rms_scale(0)
                else:
                    factor(l, 0)
                    rms(2 * l)
                dve.wait_ge(dtmm_s, l + 1)
                then_wait(v.tensor_tensor(dts[:, 0, :, :], ps[:, 2, 256:288].rearrange("p (a b) -> p a b", a=2),
                                          bc(dtb[:, l, :], TT), ALU.add))
                then_wait(v.tensor_scalar(dts[:, 3, :, :], dts[:, 0, :, :], -1.0, None, ALU.mult))
                v.tensor_tensor(dts[:, 1, :, :], dts[:, 0, :, :], dts[:, 3, :, :], ALU.max).then_inc(dtin_s, 1)
                dve.wait_ge(dtln_s, l + 1)
                then_wait(v.scalar_tensor_tensor(dts[:, 3, :, :], dts[:, 0, :, :], 0.0, dts[:, 2, :, :], ALU.max, ALU.add))
                v.scalar_tensor_tensor(dts[:, 4, :, :], dts[:, 3, :, :], -1.0, bc(alog[:, l, :], TT),
                                       ALU.mult, ALU.mult).then_inc(dt_s, 1)
                dve.wait_ge(sig_s, l + 1)
                if l:
                    dve.wait_ge(cvar_s, l)
                    v.memset(cpad[:, :, 0:PADC], 0.0)
                then_wait(v.tensor_tensor(cpad[:, :, PADC:], proj[:, VAL:VAL + CT, :], proj[:, GLU:GLU + CT, :], ALU.mult))
                for m in range(CT):
                    v.tensor_scalar(cacc[:, m, :], cpad[:, m, 0:SEQ], cwcol[:, l, m:m + 1],
                                    pcol[:, l, R_CB + m:R_CB + m + 1], ALU.mult, ALU.add).then_inc(cv_s, 1)
                C0 = CV0 + l * CT * CONF_TAPS
                with dve.Fori(1, CONF_TAPS) as k:
                    for m in range(CT):
                        dve.wait_ge(cv_s, k * CT + C0 + m + 1 - CT)
                        v.scalar_tensor_tensor(cacc[:, m, :], cpad[:, m, ds(k, SEQ)], cwcol[:, l, ds(k * CT + m, 1)],
                                               cacc[:, m, :], ALU.mult, ALU.add).then_inc(cv_s, 1)
                if l == 0:
                    params(1)
                for q in range(3):
                    dve.wait_ge(ev_s, 2 + W_CHUNKS * l + XBC // 2 + 2 * q + 2)
                    for tap in range(SSM_TAPS - 1, -1, -1):
                        sh = SSM_TAPS - 1 - tap
                        for m in range(4 * q, 4 * q + 4):
                            w = swcol[:, l, tap * XT + m:tap * XT + m + 1]
                            if sh == 0:
                                last = v.tensor_scalar(xc[:, m, :], proj[:, XBC + m, :], w,
                                                       pcol[:, l, R_SB + m:R_SB + m + 1], ALU.mult, ALU.add)
                            else:
                                last = v.scalar_tensor_tensor(xc[:, m, sh:], proj[:, XBC + m, 0:SEQ - sh], w,
                                                              xc[:, m, sh:], ALU.mult, ALU.add)
                        if sh < SSM_TAPS - 1:
                            then_wait(last)
                    last.then_inc(xv_s, 1)
                dve.wait_ge(cm_s, l + 1)
                then_wait(v.tensor_scalar(rs[:, 2, :], ps[:, 2, 0:SEQ], 1.0 / CONF_WIDTH, None, ALU.mult))
                v.tensor_tensor(cacc[:, :, :], cacc[:, :, :], bc(rs[:, 2, :], CT), ALU.subtract).then_inc(cx_s, 1)
                dve.wait_ge(ac_s, l + 1)
                then_wait(v.tensor_copy(acum[:, :, :], ps[:, 2, 336:368].rearrange("p (a b) -> p a b", a=2)))
                v.tensor_tensor(dec[:, 0, :], ps[:, 2, 368:384], acum[:, 0, :], ALU.subtract).then_inc(acs_s, 1)
                dve.wait_ge(cvar_s, l + 1)
                v.tensor_scalar(rs[:, 0, :], ps[:, 2, 0:SEQ], 1.0 / CONF_WIDTH, EPS, ALU.mult, ALU.add).then_inc(cvr_s, 1)
                dve.wait_ge(csd_s, l + 1)
                then_wait(v.reciprocal(rs[:, 2, :], rs[:, 1, :]))
                v.tensor_tensor(cacc[:, :, :], cacc[:, :, :], bc(rs[:, 2, :], CT), ALU.mult).then_inc(cn_s, 1)
                if l == 0:
                    modulation(0, ADA_FIRST // 2, ADA_CHUNKS // 2)
                factor(l, 1)
                dve.wait_ge(cb_s, l + 1)
                v.tensor_tensor(cbm[:, :, :, :].rearrange("p a b c -> p (a b) c"),
                                ps[:, 7, :].rearrange("p (a b) -> p a b", a=4), bc(triu[:, :], 4),
                                ALU.mult).then_inc(cbm_s, 1)
                for i in range(1, 5):
                    for h in (2 * i - 2, 2 * i - 1):
                        head_scores(l, h)
                    for h in (2 * i - 2, 2 * i - 1):
                        head_probs(l, h)
                    if i == 1:
                        for t in range(TT):
                            last = v.tensor_tensor(xdt[:, t, :].rearrange("p (h d) -> p h d", d=DH),
                                                   xs_tm[:, t, :].rearrange("p (h d) -> p h d", d=DH),
                                                   dts[:, 3, t, :].unsqueeze(2).broadcast_to([P, HEADS_S, DH]), ALU.mult)
                        then_wait(last)
                        dve.wait_ge(dcy_s, l + 1)
                        v.tensor_tensor(xdtd.rearrange("p (h d) -> p h d", d=DH),
                                        xdt[:, 0, :].rearrange("p (h d) -> p h d", d=DH),
                                        dec[:, 1, :].unsqueeze(2).broadcast_to([P, HEADS_S, DH]), ALU.mult).then_inc(xd_s, 1)
                    dve.wait_ge(pv_s, HEADS_A * l + 2 * i)
                    v.tensor_copy(ao[:, i - 1, :], ps[:, 7, (i - 1) % 2 * SEQ:(i - 1) % 2 * SEQ + SEQ]).then_inc(ao_s, 1)
                for k in range(8):
                    seg_of(l, k)
                    lmat(l, k)
                    if k >= 2 and k % 2 == 0:
                        y_out(l, k // 2 - 1)
                dve.wait_ge(zs_s, l + 1)
                y_out(l, 3)
                dve.wait_ge(gate_s, 3 * (l + 1))

                def merge_conf(idx):
                    dve.wait_ge(om_s, 16 * l + idx + 1)
                    v.tensor_tensor(merged[:, 2 * idx:2 * idx + 2, :], ps[:, idx % 2, :].rearrange("p (a b) -> p a b", a=2),
                                    proj[:, GATE + 2 * idx:GATE + 2 * idx + 2, :], ALU.mult).then_inc(mg_s, 1)

                def merge_add(n, idx, g0):
                    dve.wait_ge(om_s, 16 * l + n + idx + 1)
                    g = proj[:, g0 + 2 * idx:g0 + 2 * idx + 2, :]
                    then_wait(v.tensor_tensor(g, ps[:, idx % 2, :].rearrange("p (a b) -> p a b", a=2), g, ALU.mult))
                    v.tensor_tensor(merged[:, 2 * idx:2 * idx + 2, :], merged[:, 2 * idx:2 * idx + 2, :], g,
                                    ALU.add).then_inc(mg_s, 1)

                for idx in range(3):
                    merge_conf(idx)
                dve.wait_ge(gst_s, l + 1)
                v.tensor_scalar(gr[:, 0, :, :], ps[:, 7, :].rearrange("p (a b) -> p a b", a=2), 1.0 / 512, EPS,
                                ALU.mult, ALU.add).then_inc(gv_s, 1)
                merge_conf(3)
                dve.wait_ge(gsd_s, l + 1)
                then_wait(v.reciprocal(gr[:, 2, :, :], gr[:, 1, :, :]))
                merge_add(4, 0, GATE + 16)
                for m in range(KT):
                    last = v.scalar_tensor_tensor(proj[:, Z + m, :], proj[:, Z + m, :], pcol[:, l, R_SN + m:R_SN + m + 1],
                                                  gr[:, 2, m // 4, :], ALU.mult, ALU.mult)
                last.then_inc(gn_s, 1)
                for idx in range(1, 4):
                    merge_add(4, idx, GATE + 16)
                for idx in range(4):
                    merge_add(8, idx, GATE + 8)
                for idx in range(4):
                    dve.wait_ge(om_s, 16 * l + 12 + idx + 1)
                    last = residual(l, idx, 16)
                    last.then_inc(mg_s, 1)
                dve.wait_ge(mg_s, 16 * (l + 1))
                rms(2 * l + 1)
                if l == 0:
                    for T in range(2 * GD):
                        g = T // 2
                        dve.wait_ge(sil_s, T + 1)
                        dve.wait_ge(dn_s, g + 1)
                        v.tensor_tensor(hm[:, g % 2, T % 2, :], sil[:, T % 2, :], ps[:, T % 2, SEQ:2 * SEQ],
                                        ALU.mult).then_inc(hm_s, 1)
                        if T % 2 == 0 and T:
                            ada_reduce(1, T // 2 - 1, modn)
                    for q in range(GD - 1, ADA_CHUNKS // 2):
                        ada_reduce(1, q, modn)
                    for m in range(KT):
                        dve.wait_ge(c_s, m + 1)
                        v.scalar_tensor_tensor(xT[:, m, :], ps[:, 6 + m % 2, 0:SEQ], modc[:, 40 + m:41 + m], xT[:, m, :],
                                               ALU.mult, ALU.add).then_inc(cf_s, 1)
                    dve.wait_ge(cf_s, CF0 + KT)
                    modulation_bias(1, 0, ADA_CHUNKS // 2, modn)

            R = [rt[:, i, :, :] for i in range(20)]
            dve.wait_ge(lg_s, 1)
            then_wait(v.tensor_tensor(R[0], ps[:, 0, 0:16].rearrange("p (a b) -> p a b", a=2), bc(rb[:, :], TT), ALU.add))
            then_wait(v.tensor_scalar(R[1], bc(slot_f[:, 0:EXPERTS], TT), -1.0, float(EXPERTS), ALU.mult, ALU.add))
            logits = R[0]
            for pick, (m_, mask_) in enumerate(((2, 10), (3, 11))):
                then_wait(v.tensor_reduce(rt[:, m_, :, 0:1], logits, AX.X, ALU.max))
                then_wait(v.tensor_tensor(R[4], logits, rt[:, m_, :, 0:1].broadcast_to([P, TT, EXPERTS]), ALU.is_equal))
                then_wait(v.tensor_tensor(R[5], R[4], R[1], ALU.mult))
                then_wait(v.tensor_reduce(rt[:, 6, :, 0:1], R[5], AX.X, ALU.max))
                then_wait(v.tensor_tensor(R[mask_], R[1], rt[:, 6, :, 0:1].broadcast_to([P, TT, EXPERTS]), ALU.is_equal))
                if pick == 0:
                    then_wait(v.scalar_tensor_tensor(R[7], R[10], NEG, logits, ALU.mult, ALU.add))
                    logits = R[7]
            v.tensor_tensor(R[12], R[10], R[11], ALU.add).then_inc(mk_s, 1)
            v.tensor_tensor(rt[:, 8, :, 0:1], rt[:, 3, :, 0:1], rt[:, 2, :, 0:1], ALU.subtract).then_inc(re_s, 1)
            dve.wait_ge(cum_s, 1)
            v.tensor_copy(cntf[0:1, 1:EXPERTS + 1], ps[0:1, 1, 16:24])
            then_wait(v.scalar_tensor_tensor(R[15], ps[:, 1, 0:16].rearrange("p (a b) -> p a b", a=2), 1.0, R[12],
                                             ALU.add, ALU.mult))
            v.tensor_copy(cnt[:, :], cntf[:, :]).then_inc(rk_s, 1)
            v.tensor_scalar(key9[:, :, 0:EXPERTS], R[15], -1.0, None, ALU.add).then_inc(rk_s, 1)
            dve.wait_ge(rk_s, 2)
            for t in range(TT):
                last = v.tensor_scalar(p_m[:, t, :], slot_f[:, :], key9[:, t, 0:1], None, ALU.is_equal)
            last.then_inc(p_s, 1)
            v.memset(pgT[:, :, :], 0.0)
            for m in range(KT):
                dve.wait_ge(c_s, KT + m + 1)
                v.tensor_copy(xg[:, m, :], ps[:, 6 + (m + 1) % 2, 0:SEQ]).then_inc(cf_s, 1)
            dve.wait_ge(rx_s, 1)
            then_wait(v.tensor_scalar(rt[:, 8, :, 2:3], rt[:, 8, :, 1:2], 1.0, None, ALU.add))
            then_wait(v.reciprocal(rt[:, 8, :, 3:4], rt[:, 8, :, 2:3]))
            then_wait(v.tensor_tensor(rt[:, 8, :, 4:5], rt[:, 8, :, 1:2], rt[:, 8, :, 3:4], ALU.mult))
            then_wait(v.tensor_tensor(R[13], R[10], rt[:, 8, :, 3:4].broadcast_to([P, TT, EXPERTS]), ALU.mult))
            then_wait(v.tensor_tensor(R[14], R[11], rt[:, 8, :, 4:5].broadcast_to([P, TT, EXPERTS]), ALU.mult))
            then_wait(v.tensor_tensor(gate9[:, :, 0:EXPERTS], R[13], R[14], ALU.add))
            C1, PER = 2 * KT, 1 + 2 * KT

            def merge(products):
                for m in range(KT):
                    dve.wait_ge(c_s, products(m))
                    v.scalar_tensor_tensor(xT[:, m, :], ps[:, 6 + (m + 1) % 2, 0:SEQ], modc[:, 40 + m:41 + m],
                                           xT[:, m, :], ALU.mult, ALU.add).then_inc(cf_s, 1)

            with dve.Fori(0, EXPERTS) as e:
                count = dve.value_load(cnt[0:1, ds(e + 1, 1)], min_val=0, max_val=SEQ)
                after = dve.value_load(cnt[0:1, ds(e + 2, 1)], min_val=0, max_val=SEQ)
                for t in range(TT):
                    v.tensor_scalar(p_m[:, t, :], slot_f[:, :], key9[:, t, ds(e + 1, 1)], None, ALU.is_equal)
                    last = v.tensor_scalar(pg_m[:, t, :], slot_f[:, :], key9[:, t, ds(e, 1)], gate9[:, t, ds(e, 1)],
                                           ALU.is_equal, ALU.mult)
                last.then_inc(pg_s, 1)
                dve.wait_ge(pg_s, e + 1)
                dve.sem_inc(p_s, 1)

                def small_hidden():
                    def multiply(b, tiles, groups):
                        dve.wait_ge(dn_s, groups + 1)
                        dve.wait_ge(sil_s, tiles + 2)
                        for j in range(2):
                            v.tensor_tensor(hsm[:, b, HALF * j:HALF * (j + 1)], sil[:, b, HALF * j:HALF * (j + 1)],
                                            ps[:, b, P + HALF * j:P + HALF * (j + 1)], ALU.mult).then_inc(hm_s, 1)

                    def evacuate(b, groups):
                        dve.wait_ge(ht_s, groups)
                        v.tensor_copy(hm[:, b, 0, 0:P], ps[:, 4 + b, 0:P]).then_inc(hte_s, 1)

                    T0 = e * (2 * GE) + 2 * GD
                    G0 = e * GE
                    multiply(0, T0, G0 + GD)
                    multiply(1, T0 + 2, G0 + GD + 1)
                    merge_before()
                    evacuate(0, G0 + 1)
                    with dve.Fori(1, GE // 2) as i:
                        multiply(0, T0 + i * 4, G0 + i * 2 + GD)
                        evacuate(1, G0 + i * 2)
                        multiply(1, T0 + i * 4 + 2, G0 + i * 2 + GD + 1)
                        evacuate(0, G0 + i * 2 + 1)
                    prepared(HALF)
                    evacuate(1, G0 + GE)

                def expert(n):
                    if n == HALF:
                        small_hidden()
                    else:
                        hidden(n)
                        prepared(n)
                        dve.sem_inc(hte_s, GE)

                def merge_before():
                    merge(lambda m: e * PER + C1 + 1 + m)

                def prepared(n):
                    dve.wait_ge(c_s, e * PER + C1 + KT + 1)
                    st = (n + P - 1) // P
                    v.tensor_copy(pgT[:, 0:st, :], ps[:, 6, 0:st * SEQ].rearrange("p (a b) -> p a b", a=st)).then_inc(cf_s, 1)
                    with dve.If(after <= P):
                        tokens(P)
                    with dve.Else():
                        tokens(SEQ)

                def tokens(width):
                    for m in range(KT):
                        dve.wait_ge(c_s, e * PER + C1 + KT + 2 + m)
                        v.tensor_copy(xg[:, m, 0:width], ps[:, 6 + (m + 1) % 2, 0:width]).then_inc(cf_s, 1)

                def hidden(n):
                    def multiply(b, downs, tiles):
                        dve.wait_ge(dn_s, downs)
                        for j in range(2):
                            dve.wait_ge(sil_s, tiles + j + 1)
                            v.tensor_tensor(hm[:, b, j, 0:n], sil[:, j, 0:n], ps[:, j, SEQ:SEQ + n],
                                            ALU.mult).then_inc(hm_s, 1)

                    T0 = e * (2 * GE) + 2 * GD
                    for b in range(2):
                        multiply(b, e * GE + GD + b + 1, T0 + 2 * b)
                    merge_before()
                    with dve.Fori(1, GE // 2) as i:
                        for b in range(2):
                            multiply(b, e * GE + i * 2 + GD + b + 1, T0 + i * 4 + 2 * b)

                by_size(dve, count, expert)
            merge(lambda m: PER * EXPERTS + C1 + 1 + m)
            dve.wait_ge(cf_s, CF0 + C1 + PER * EXPERTS + KT)
            rms(2 * DEPTH)


_INS = ['x', 'c', 'norm1_w', 'norm2_w', 'ada_w', 'ada_b', 'w_in', 'conf_conv_w', 'conf_conv_b', 'conf_ln_w',
        'conf_ln_b', 'conf_out', 'ssm_conv_w', 'ssm_conv_b', 'ssm_dt_bias', 'ssm_A_log', 'ssm_D', 'ssm_norm_w',
        'ssm_out', 'attn_out', 'mix_out', 'ffn_w_gate', 'ffn_w_up', 'ffn_w_down', 'moe_router_w', 'moe_router_b',
        'moe_w_gate', 'moe_w_up', 'moe_w_down', 'final_norm_w']


def kernel(**inputs):
    import numpy as np
    import concourse.bacc as bacc
    from concourse.bass_utils import run_bass_kernel_spmd

    nc = bacc.Bacc("TRN2", target_bir_lowering=False, num_devices=1)
    arrays, args = {}, []
    for name in _INS:
        a = np.ascontiguousarray(inputs[name])
        arrays[f"in_{name}"] = a
        args.append(nc.dram_tensor(f"in_{name}", a.shape, mybir.dt.from_np(a.dtype), kind="ExternalInput").ap())
    out = nc.dram_tensor("out_0", (1, SEQ, D_MODEL), mybir.dt.float32, kind="ExternalOutput").ap()
    trunk(nc, *args, out)
    r = run_bass_kernel_spmd(nc, [arrays], core_ids=[0])
    return r.results[0]["out_0"]
```
